# Optimizing a Trainium2 kernel written in Bass

```python
import math
import jax
import jax.numpy as jnp
from jax import lax
import numpy as np
import jax, jax.numpy as jnp

D_MODEL = 1024
BATCH = 1
SEQ = 512
DEPTH = 1

GRID_W = 64
CTX_LEN = 256
NORM_EPS = 1e-6
N_MOD = 6

NA_HEADS = 16
NA_HEAD_DIM = 64
NA_WIDTH = NA_HEADS * NA_HEAD_DIM
NA_KH = 8
NA_KW = 16
ROPE_BASE = 10000.0

SSD_WIDTH = 2 * D_MODEL
SSD_HEAD_DIM = 64
SSD_HEADS = SSD_WIDTH // SSD_HEAD_DIM
SSD_GROUPS = 4
SSD_STATE = 128
SSD_CONV = 5
SSD_CHUNK = 128
SSD_XBC = SSD_WIDTH + 2 * SSD_GROUPS * SSD_STATE

N_EXPERTS = 16
EXPERT_FF = 2048
EC_CAPACITY_FACTOR = 2

IN_COLS = 3 * NA_WIDTH + SSD_WIDTH + SSD_XBC + 2 * SSD_HEADS + 2 * D_MODEL


def _rmsnorm(x, g):
    xf = x.astype(jnp.float32)
    xf = xf * lax.rsqrt(jnp.mean(xf * xf, axis=-1, keepdims=True) + NORM_EPS)
    return (xf * g.astype(jnp.float32)).astype(x.dtype)

def _modulate(x, g, shift, scale):
    return _rmsnorm(x, g) * (1 + scale) + shift

def _ada(cvec, w_ada, b_ada):
    mod = jax.nn.silu(cvec) @ w_ada + b_ada
    return jnp.split(mod, N_MOD, axis=-1)

def _split_in(p):
    offs = np.cumsum([NA_WIDTH, NA_WIDTH, NA_WIDTH, SSD_WIDTH, SSD_XBC, 2 * SSD_HEADS])
    return jnp.split(p, [int(o) for o in offs], axis=-1)

def _heads(t):
    return t.reshape(t.shape[0], t.shape[1], NA_HEADS, NA_HEAD_DIM)

def _rotate(t, pos):
    half = t.shape[-1] // 2
    inv_freq = ROPE_BASE ** (-jnp.arange(half, dtype=jnp.float32) / half)
    ang = pos.astype(jnp.float32)[:, None] * inv_freq[None, :]
    cos = jnp.cos(ang)[:, None, :].astype(t.dtype)
    sin = jnp.sin(ang)[:, None, :].astype(t.dtype)
    t1, t2 = t[..., :half], t[..., half:]
    return jnp.concatenate([t1 * cos - t2 * sin, t1 * sin + t2 * cos], axis=-1)

def _rope_2d(t, rows, cols):
    da = t.shape[-1] // 2
    return jnp.concatenate([_rotate(t[..., :da], rows), _rotate(t[..., da:], cols)], axis=-1)

def _neighbourhood_attention(q, k, v, k_ctx, v_ctx, rpb):
    Bsz, L, H, Dh = q.shape
    rows = L // GRID_W
    kh = min(NA_KH, rows)
    n_loc = kh * GRID_W
    scale = Dh ** -0.5
    qg = q.reshape(Bsz, rows, GRID_W, H, Dh)
    kg = k.reshape(Bsz, rows, GRID_W, H, Dh)
    vg = v.reshape(Bsz, rows, GRID_W, H, Dh)
    col = jnp.arange(GRID_W)
    col_start = jnp.clip(col - NA_KW // 2, 0, GRID_W - NA_KW)
    col_ok = (col[None, :] >= col_start[:, None]) & (col[None, :] < col_start[:, None] + NA_KW)
    col_idx = jnp.clip(col[None, :] - col[:, None] + NA_KW - 1, 0, 2 * NA_KW - 2)
    rpb_col = rpb[:, :, col_idx]
    mask = jnp.tile(col_ok, (1, kh))

    def row_block(r):
        r0 = jnp.clip(r - kh // 2, 0, rows - kh)
        q_r = lax.dynamic_index_in_dim(qg, r, axis=1, keepdims=False)
        k_r = lax.dynamic_slice_in_dim(kg, r0, kh, axis=1).reshape(Bsz, n_loc, H, Dh)
        v_r = lax.dynamic_slice_in_dim(vg, r0, kh, axis=1).reshape(Bsz, n_loc, H, Dh)
        bias = jnp.take(rpb_col, r0 + jnp.arange(kh) - r + NA_KH - 1, axis=1)
        bias = jnp.transpose(bias, (0, 2, 1, 3)).reshape(H, GRID_W, n_loc).astype(jnp.float32)
        s_loc = jnp.einsum('bqhd,bkhd->bhqk', q_r, k_r).astype(jnp.float32) * scale + bias
        s_loc = jnp.where(mask, s_loc, -jnp.inf)
        s_ctx = jnp.einsum('bqhd,bkhd->bhqk', q_r, k_ctx).astype(jnp.float32) * scale
        p = jax.nn.softmax(jnp.concatenate([s_loc, s_ctx], axis=-1), axis=-1).astype(v.dtype)
        return (jnp.einsum('bhqk,bkhd->bqhd', p[..., :n_loc], v_r)
                + jnp.einsum('bhqk,bkhd->bqhd', p[..., n_loc:], v_ctx))

    out = lax.map(row_block, jnp.arange(rows))
    return jnp.moveaxis(out, 0, 1).reshape(Bsz, L, H * Dh)

def _context_attention(q, k, v):
    Bsz, T, H, Dh = q.shape
    s = jnp.einsum('bqhd,bkhd->bhqk', q, k).astype(jnp.float32) * Dh ** -0.5
    p = jax.nn.softmax(s, axis=-1).astype(v.dtype)
    return jnp.einsum('bhqk,bkhd->bqhd', p, v).reshape(Bsz, T, H * Dh)

def _dwconv(x, w, b):
    nch = x.shape[-1]
    out = lax.conv_general_dilated(x, w.astype(x.dtype)[:, None, :], window_strides=(1,),
                                   padding=[(SSD_CONV // 2, SSD_CONV // 2)],
                                   dimension_numbers=('NWC', 'WIO', 'NWC'),
                                   feature_group_count=nch)
    return out + b

def _ssd_prep(xbc, dt_raw, conv_w, conv_b, dtb_f, dtb_b):
    Bsz, L, _ = xbc.shape
    xbc = jax.nn.silu(_dwconv(xbc, conv_w, conv_b))
    xs, Bm, Cm = jnp.split(xbc, [SSD_WIDTH, SSD_WIDTH + SSD_GROUPS * SSD_STATE], axis=-1)
    xs = xs.reshape(Bsz, L, SSD_HEADS, SSD_HEAD_DIM)
    Bm = Bm.reshape(Bsz, L, SSD_GROUPS, SSD_STATE)
    Cm = Cm.reshape(Bsz, L, SSD_GROUPS, SSD_STATE)
    dt_f = jax.nn.softplus(dt_raw[..., :SSD_HEADS] + dtb_f)
    dt_b = jax.nn.softplus(dt_raw[..., SSD_HEADS:] + dtb_b)
    return xs, Bm, Cm, dt_f, dt_b

def _ssd_scan(xs, dt, A, Bm, Cm, h0, return_y):
    Bsz, L, H, P = xs.shape
    nc = L // SSD_CHUNK
    R = H // SSD_GROUPS
    x = (xs * dt[..., None]).reshape(Bsz, nc, SSD_CHUNK, SSD_GROUPS, R, P)
    a = (dt * A).astype(jnp.float32).reshape(Bsz, nc, SSD_CHUNK, SSD_GROUPS, R)
    a_cs = jnp.cumsum(jnp.moveaxis(a, 2, -1), axis=-1)
    Bc = Bm.reshape(Bsz, nc, SSD_CHUNK, SSD_GROUPS, SSD_STATE)
    decay_to_end = jnp.exp(a_cs[..., -1:] - a_cs).astype(xs.dtype)
    states = jnp.einsum('bclgn,bcgrl,bclgrp->bcgrpn', Bc, decay_to_end, x)
    chunk_decay = jnp.exp(a_cs[..., -1]).astype(xs.dtype)

    def step(h, inp):
        dec, st = inp
        return dec[..., None, None] * h + st, h

    h_last, h_prev = lax.scan(step, h0.reshape(Bsz, SSD_GROUPS, R, P, SSD_STATE),
                              (jnp.moveaxis(chunk_decay, 1, 0), jnp.moveaxis(states, 1, 0)))
    h_last = h_last.reshape(Bsz, H, P, SSD_STATE)
    if not return_y:
        return None, h_last
    Cc = Cm.reshape(Bsz, nc, SSD_CHUNK, SSD_GROUPS, SSD_STATE)
    lower = jnp.tril(jnp.ones((SSD_CHUNK, SSD_CHUNK), dtype=bool))
    seg = a_cs[..., :, None] - a_cs[..., None, :]
    Lm = jnp.exp(jnp.where(lower, seg, -jnp.inf)).astype(xs.dtype)
    cb = jnp.einsum('bclgn,bcsgn->bcgls', Cc, Bc)
    y_diag = jnp.einsum('bcgls,bcgrls,bcsgrp->bclgrp', cb, Lm, x)
    y_off = jnp.einsum('bclgn,bcgrpn,bcgrl->bclgrp', Cc, jnp.moveaxis(h_prev, 0, 1),
                       jnp.exp(a_cs).astype(xs.dtype))
    return (y_diag + y_off).reshape(Bsz, L, H, P), h_last

def _bidir_ssd(xs, Bm, Cm, dt_f, dt_b, A_f, A_b, d_skip, h0_f, h0_b, return_y):
    flip = lambda t: jnp.flip(t, axis=1)
    y_f, h_f = _ssd_scan(xs, dt_f, A_f, Bm, Cm, h0_f, return_y)
    y_b, h_b = _ssd_scan(flip(xs), flip(dt_b), A_b, flip(Bm), flip(Cm), h0_b, return_y)
    if not return_y:
        return None, h_f, h_b
    return y_f + flip(y_b) + d_skip[:, None] * xs, h_f, h_b

def _ssd_gated_norm(y, z, g):
    Bsz, L = y.shape[:2]
    u = (y.reshape(Bsz, L, SSD_WIDTH) * jax.nn.silu(z)).astype(jnp.float32)
    u = u.reshape(Bsz, L, SSD_GROUPS, SSD_WIDTH // SSD_GROUPS)
    u = u * lax.rsqrt(jnp.mean(u * u, axis=-1, keepdims=True) + NORM_EPS)
    return (u.reshape(Bsz, L, SSD_WIDTH) * g.astype(jnp.float32)).astype(y.dtype)

def _merge(o_na, y_ssd, gates, w_br_na, w_br_ssd, w_out):
    g_na, g_ssd = jnp.split(gates, 2, axis=-1)
    u = jax.nn.sigmoid(g_na) * (o_na @ w_br_na) + jax.nn.sigmoid(g_ssd) * (y_ssd @ w_br_ssd)
    return u @ w_out

def _token_mixer(h, hc, w_in, na_rpb, conv_w, conv_b, a_log_f, a_log_b, dtb_f, dtb_b, d_skip,
                 ssd_norm, w_br_na, w_br_ssd, w_out, update_ctx):
    Bsz, L, _ = h.shape
    q, k, v, z, xbc, dt_raw, gates = _split_in(h @ w_in)
    qc, kc, vc, zc, xbcc, dtc, gates_c = _split_in(hc @ w_in)
    pos = jnp.arange(L)
    rows, cols = pos // GRID_W, pos % GRID_W
    o_na = _neighbourhood_attention(_rope_2d(_heads(q), rows, cols), _rope_2d(_heads(k), rows, cols),
                                    _heads(v), _heads(kc), _heads(vc), na_rpb)
    A_f, A_b = -jnp.exp(a_log_f), -jnp.exp(a_log_b)
    h0 = jnp.zeros((Bsz, SSD_HEADS, SSD_HEAD_DIM, SSD_STATE), h.dtype)
    y_c, hf_c, hb_c = _bidir_ssd(*_ssd_prep(xbcc, dtc, conv_w, conv_b, dtb_f, dtb_b),
                                 A_f, A_b, d_skip, h0, h0, update_ctx)
    y, _, _ = _bidir_ssd(*_ssd_prep(xbc, dt_raw, conv_w, conv_b, dtb_f, dtb_b),
                         A_f, A_b, d_skip, hf_c, hb_c, True)
    mix = _merge(o_na, _ssd_gated_norm(y, z, ssd_norm), gates, w_br_na, w_br_ssd, w_out)
    if not update_ctx:
        return mix, None
    o_na_c = _context_attention(_heads(qc), _heads(kc), _heads(vc))
    mix_c = _merge(o_na_c, _ssd_gated_norm(y_c, zc, ssd_norm), gates_c, w_br_na, w_br_ssd, w_out)
    return mix, mix_c

def _ec_moe(h, w_router, w_eg, w_eu, w_ed):
    Bsz, T, _ = h.shape
    cap = EC_CAPACITY_FACTOR * T // N_EXPERTS
    aff = jax.nn.softmax((h @ w_router).astype(jnp.float32), axis=-1)
    gate, idx = lax.top_k(jnp.transpose(aff, (0, 2, 1)), cap)
    b_idx = jnp.arange(Bsz)[:, None, None]
    xg = h[b_idx, idx]
    hid = jax.nn.silu(jnp.einsum('becd,edf->becf', xg, w_eg)) * jnp.einsum('becd,edf->becf', xg, w_eu)
    yo = jnp.einsum('becf,efd->becd', hid, w_ed) * gate[..., None].astype(h.dtype)
    return jnp.zeros_like(h).at[b_idx, idx].add(yo)

def _layer(x, ctx, c, c_ctx, w_ada, b_ada, n_pre_mix, n_post_mix, n_pre_ffn, n_post_ffn, w_in, na_rpb,
           conv_w, conv_b, a_log_f, a_log_b, dtb_f, dtb_b, d_skip, ssd_norm, w_br_na, w_br_ssd, w_out,
           w_router, w_eg, w_eu, w_ed, update_ctx):
    sh1, sc1, ga1, sh2, sc2, ga2 = _ada(c[:, None, :], w_ada, b_ada)
    csh1, csc1, cga1, csh2, csc2, cga2 = _ada(c_ctx, w_ada, b_ada)
    mix, mix_c = _token_mixer(_modulate(x, n_pre_mix, sh1, sc1), _modulate(ctx, n_pre_mix, csh1, csc1),
                              w_in, na_rpb, conv_w, conv_b, a_log_f, a_log_b, dtb_f, dtb_b, d_skip,
                              ssd_norm, w_br_na, w_br_ssd, w_out, update_ctx)
    x = x + ga1 * _rmsnorm(mix, n_post_mix)
    x = x + ga2 * _rmsnorm(_ec_moe(_modulate(x, n_pre_ffn, sh2, sc2), w_router, w_eg, w_eu, w_ed), n_post_ffn)
    if update_ctx:
        ctx = ctx + cga1 * _rmsnorm(mix_c, n_post_mix)
        ctx = ctx + cga2 * _rmsnorm(_ec_moe(_modulate(ctx, n_pre_ffn, csh2, csc2), w_router, w_eg, w_eu, w_ed),
                                    n_post_ffn)
    return x, ctx

def first_inputs(seed: int = 0) -> dict:
    key = jax.random.key(seed)
    ks = jax.random.split(key, 26)
    f32 = jnp.float32

    def nrm(k, shape, s):
        return jax.random.normal(k, shape, f32) * s

    dt0 = jnp.exp(jax.random.uniform(ks[14], (DEPTH, 2, SSD_HEADS), f32, math.log(1e-3), math.log(1e-1)))
    dt_bias = dt0 + jnp.log(-jnp.expm1(-dt0))
    a_log = jnp.log(jax.random.uniform(ks[15], (DEPTH, 2, SSD_HEADS), f32, 1.0, 16.0))
    return {
        'x': nrm(ks[0], (BATCH, SEQ, D_MODEL), 1.0),
        'c': nrm(ks[1], (BATCH, D_MODEL), 1.0),
        'ctx': nrm(ks[2], (BATCH, CTX_LEN, D_MODEL), 1.0),
        'c_ctx': nrm(ks[3], (D_MODEL,), 1.0),
        'w_ada': nrm(ks[4], (DEPTH, D_MODEL, N_MOD * D_MODEL), 0.5 * D_MODEL ** -0.5),
        'b_ada': nrm(ks[5], (DEPTH, N_MOD * D_MODEL), 0.02),
        'norm_pre_mix': 1.0 + nrm(ks[6], (DEPTH, D_MODEL), 0.02),
        'norm_post_mix': 1.0 + nrm(ks[7], (DEPTH, D_MODEL), 0.02),
        'norm_pre_ffn': 1.0 + nrm(ks[8], (DEPTH, D_MODEL), 0.02),
        'norm_post_ffn': 1.0 + nrm(ks[9], (DEPTH, D_MODEL), 0.02),
        'w_in': nrm(ks[10], (DEPTH, D_MODEL, IN_COLS), D_MODEL ** -0.5),
        'na_rpb': nrm(ks[11], (DEPTH, NA_HEADS, 2 * NA_KH - 1, 2 * NA_KW - 1), 0.1),
        'ssd_conv_w': nrm(ks[12], (DEPTH, SSD_CONV, SSD_XBC), SSD_CONV ** -0.5),
        'ssd_conv_b': nrm(ks[13], (DEPTH, SSD_XBC), 0.02),
        'ssd_a_log_fwd': a_log[:, 0],
        'ssd_a_log_bwd': a_log[:, 1],
        'ssd_dt_bias_fwd': dt_bias[:, 0],
        'ssd_dt_bias_bwd': dt_bias[:, 1],
        'ssd_d_skip': 1.0 + nrm(ks[16], (DEPTH, SSD_HEADS), 0.02),
        'ssd_norm': 1.0 + nrm(ks[17], (DEPTH, SSD_WIDTH), 0.02),
        'w_branch_na': nrm(ks[18], (DEPTH, NA_WIDTH, D_MODEL), NA_WIDTH ** -0.5),
        'w_branch_ssd': nrm(ks[19], (DEPTH, SSD_WIDTH, D_MODEL), SSD_WIDTH ** -0.5),
        'w_out': nrm(ks[20], (DEPTH, D_MODEL, D_MODEL), D_MODEL ** -0.5),
        'w_router': nrm(ks[21], (DEPTH, D_MODEL, N_EXPERTS), D_MODEL ** -0.5),
        'w_exp_gate': nrm(ks[22], (DEPTH, N_EXPERTS, D_MODEL, EXPERT_FF), D_MODEL ** -0.5),
        'w_exp_up': nrm(ks[23], (DEPTH, N_EXPERTS, D_MODEL, EXPERT_FF), D_MODEL ** -0.5),
        'w_exp_down': nrm(ks[24], (DEPTH, N_EXPERTS, EXPERT_FF, D_MODEL), EXPERT_FF ** -0.5),
    }

def first_block(x, c, ctx, c_ctx, w_ada, b_ada, norm_pre_mix, norm_post_mix, norm_pre_ffn, norm_post_ffn,
              w_in, na_rpb, ssd_conv_w, ssd_conv_b, ssd_a_log_fwd, ssd_a_log_bwd, ssd_dt_bias_fwd,
              ssd_dt_bias_bwd, ssd_d_skip, ssd_norm, w_branch_na, w_branch_ssd, w_out, w_router,
              w_exp_gate, w_exp_up, w_exp_down):
    for i in range(DEPTH):
        x, ctx = _layer(x, ctx, c, c_ctx, w_ada[i], b_ada[i], norm_pre_mix[i], norm_post_mix[i],
                        norm_pre_ffn[i], norm_post_ffn[i], w_in[i], na_rpb[i], ssd_conv_w[i], ssd_conv_b[i],
                        ssd_a_log_fwd[i], ssd_a_log_bwd[i], ssd_dt_bias_fwd[i], ssd_dt_bias_bwd[i],
                        ssd_d_skip[i], ssd_norm[i], w_branch_na[i], w_branch_ssd[i], w_out[i], w_router[i],
                        w_exp_gate[i], w_exp_up[i], w_exp_down[i], i < DEPTH - 1)
    return x


DEPTH_2 = 2

HEAD_DIM = 64
N_HEADS = D_MODEL // HEAD_DIM
N_HEADS_A = N_HEADS // 4
N_HEADS_B = N_HEADS // 4
N_HEADS_C = N_HEADS - N_HEADS_A - N_HEADS_B
WIDTH_A = N_HEADS_A * HEAD_DIM
WIDTH_B = N_HEADS_B * HEAD_DIM
WIDTH_C = N_HEADS_C * HEAD_DIM
DIFF_DIM = HEAD_DIM // 2
ROPE_THETA = 500000.0
ROPE_FRACTION = 4
Q_BLOCK = 128
MOBA_BLOCK = 256
MOBA_TOPK = 3
MOBA_Q_CHUNK = 32
DILATED_PATTERNS = ((128, 1), (512, 4), (2048, 16))
SW_BLOCK = 128
D_FF = ((8 * D_MODEL // 3 + 255) // 256) * 256
CONV_WIDTH = 3
EPS = 1e-6
NEG_INF = -1e30


def rms_norm(x, g):
    xf = x.astype(jnp.float32)
    y = xf * lax.rsqrt(jnp.mean(xf * xf, axis=-1, keepdims=True) + EPS)
    return (y * g.astype(jnp.float32)).astype(x.dtype)

def partial_rope(x, positions):
    d = x.shape[-1]
    rot = d // ROPE_FRACTION
    half = rot // 2
    inv = jnp.power(jnp.float32(ROPE_THETA), -jnp.arange(half, dtype=jnp.float32) * 2.0 / rot)
    ang = positions.astype(jnp.float32)[..., None] * inv
    ang = ang.reshape((x.shape[0],) + (1,) * (x.ndim - 3) + ang.shape[1:])
    cos = jnp.cos(ang).astype(x.dtype)
    sin = jnp.sin(ang).astype(x.dtype)
    x1 = x[..., :half]
    x2 = x[..., half:rot]
    return jnp.concatenate([x1 * cos - x2 * sin, x2 * cos + x1 * sin, x[..., rot:]], axis=-1)

def to_heads(t, h):
    b, s, _ = t.shape
    return t.reshape(b, s, h, -1).transpose(0, 2, 1, 3)

def from_heads(t):
    b, h, s, d = t.shape
    return t.transpose(0, 2, 1, 3).reshape(b, s, h * d)

def differential_attention(q, k, v, positions, lam, g_head, lam_init):
    b, s, _ = q.shape
    h = N_HEADS_A
    q = partial_rope(q.reshape(b, s, h, 2, DIFF_DIM).transpose(0, 2, 3, 1, 4), positions)
    k = partial_rope(k.reshape(b, s, h, 2, DIFF_DIM).transpose(0, 2, 3, 1, 4), positions)
    vf = to_heads(v, h).astype(jnp.float32)
    nq = s // Q_BLOCK
    qb = q.reshape(b, h, 2, nq, Q_BLOCK, DIFF_DIM).transpose(3, 0, 1, 2, 4, 5)
    key_pos = jnp.arange(s)
    scale = DIFF_DIM ** -0.5

    def block(args):
        qi, i = args
        sc = jnp.einsum('bhcqd,bhckd->bhcqk', qi, k).astype(jnp.float32) * scale
        q_pos = i * Q_BLOCK + jnp.arange(Q_BLOCK)
        sc = jnp.where(key_pos[None, :] <= q_pos[:, None], sc, NEG_INF)
        p = jax.nn.softmax(sc, axis=-1)
        a = p[:, :, 0] - lam * p[:, :, 1]
        return jnp.einsum('bhqk,bhkd->bhqd', a, vf)

    o = lax.map(block, (qb, jnp.arange(nq)))
    o = o.transpose(1, 2, 0, 3, 4).reshape(b, h, s, HEAD_DIM)
    o = rms_norm(o, g_head) * (1.0 - lam_init)
    return from_heads(o)

def moba_attention(q, k, v, positions):
    b, s, _ = q.shape
    h = N_HEADS_B
    q = partial_rope(to_heads(q, h), positions)
    k = partial_rope(to_heads(k, h), positions)
    v = to_heads(v, h)
    nb = -(-s // MOBA_BLOCK)
    sp = nb * MOBA_BLOCK
    pad = ((0, 0), (0, 0), (0, sp - s), (0, 0))
    q, k, v = jnp.pad(q, pad), jnp.pad(k, pad), jnp.pad(v, pad)
    n_sel = max(1, min(MOBA_TOPK, nb - 1))
    kb = k.reshape(b, h, nb, MOBA_BLOCK, HEAD_DIM)
    vb = v.reshape(b, h, nb, MOBA_BLOCK, HEAD_DIM)
    k_mean = jnp.mean(kb.astype(jnp.float32), axis=3)
    gate = jnp.einsum('bhsd,bhnd->bhsn', q.astype(jnp.float32), k_mean)
    q_blk = jnp.arange(sp) // MOBA_BLOCK
    gate = jnp.where(jnp.arange(nb)[None, :] < q_blk[:, None], gate, NEG_INF)
    _, sel = lax.top_k(gate, n_sel)
    valid = jnp.arange(n_sel)[None, :] < q_blk[:, None]
    c = MOBA_Q_CHUNK
    nc = sp // c
    qc = q.reshape(b, h, nc, c, HEAD_DIM).transpose(2, 0, 1, 3, 4)
    selc = sel.reshape(b, h, nc, c, n_sel).transpose(2, 0, 1, 3, 4)
    validc = valid.reshape(nc, c, n_sel)
    b_idx = jnp.arange(b)[:, None, None, None]
    h_idx = jnp.arange(h)[None, :, None, None]
    scale = HEAD_DIM ** -0.5

    def chunk(args):
        qi, si, vi, ci = args
        kg = kb[b_idx, h_idx, si]
        vg = vb[b_idx, h_idx, si].astype(jnp.float32)
        q_pos = ci * c + jnp.arange(c)
        start = (ci * c) // MOBA_BLOCK * MOBA_BLOCK
        k_own = lax.dynamic_slice_in_dim(k, start, MOBA_BLOCK, axis=2)
        v_own = lax.dynamic_slice_in_dim(v, start, MOBA_BLOCK, axis=2).astype(jnp.float32)
        s_sel = jnp.einsum('bhqd,bhqnkd->bhqnk', qi, kg).astype(jnp.float32) * scale
        s_sel = jnp.where(vi[None, None, :, :, None], s_sel, NEG_INF).reshape(b, h, c, n_sel * MOBA_BLOCK)
        s_own = jnp.einsum('bhqd,bhkd->bhqk', qi, k_own).astype(jnp.float32) * scale
        k_pos = start + jnp.arange(MOBA_BLOCK)
        s_own = jnp.where(k_pos[None, :] <= q_pos[:, None], s_own, NEG_INF)
        p = jax.nn.softmax(jnp.concatenate([s_sel, s_own], axis=-1), axis=-1)
        p_sel = p[..., :n_sel * MOBA_BLOCK].reshape(b, h, c, n_sel, MOBA_BLOCK)
        p_own = p[..., n_sel * MOBA_BLOCK:]
        return (jnp.einsum('bhqnk,bhqnkd->bhqd', p_sel, vg)
                + jnp.einsum('bhqk,bhkd->bhqd', p_own, v_own))

    o = lax.map(chunk, (qc, selc, validc, jnp.arange(nc)))
    o = o.transpose(1, 2, 0, 3, 4).reshape(b, h, sp, HEAD_DIM)[:, :, :s]
    return from_heads(o)

def dilated_branch(q, k, v, window, dil):
    b, h, s, d = q.shape
    span = dil * SW_BLOCK
    sp = -(-s // span) * span
    m_len = sp // dil
    nb = m_len // SW_BLOCK
    w_sub = window // dil

    def sub(t):
        t = jnp.pad(t, ((0, 0), (0, 0), (0, sp - s), (0, 0)))
        return t.reshape(b, h, m_len, dil, d).transpose(0, 1, 3, 2, 4).reshape(b, h, dil, nb, SW_BLOCK, d)

    def band(t):
        prev = jnp.pad(t, ((0, 0), (0, 0), (0, 0), (1, 0), (0, 0), (0, 0)))[:, :, :, :-1]
        return jnp.concatenate([prev, t], axis=4)

    qs = sub(q)
    kw = band(sub(k))
    vw = band(sub(v)).astype(jnp.float32)
    sc = jnp.einsum('bhrnqd,bhrnkd->bhrnqk', qs, kw).astype(jnp.float32) * (d ** -0.5)
    qi = jnp.arange(SW_BLOCK)[:, None]
    kj = jnp.arange(2 * SW_BLOCK)[None, :] - SW_BLOCK
    dist = qi - kj
    blk = jnp.arange(nb)[:, None, None]
    mask = (dist >= 0) & (dist <= w_sub) & (blk * SW_BLOCK + kj >= 0)
    sc = jnp.where(mask, sc, NEG_INF)
    mx = jnp.max(sc, axis=-1, keepdims=True)
    e = jnp.exp(sc - mx)
    den = jnp.sum(e, axis=-1)
    o = jnp.einsum('bhrnqk,bhrnkd->bhrnqd', e, vw) / den[..., None]
    lse = mx[..., 0] + jnp.log(den)
    o = o.reshape(b, h, dil, m_len, d).transpose(0, 1, 3, 2, 4).reshape(b, h, sp, d)[:, :, :s]
    lse = lse.reshape(b, h, dil, m_len).transpose(0, 1, 3, 2).reshape(b, h, sp)[:, :, :s]
    return o, lse

def dilated_attention(q, k, v, positions):
    h = N_HEADS_C
    q = partial_rope(to_heads(q, h), positions)
    k = partial_rope(to_heads(k, h), positions)
    v = to_heads(v, h)
    outs, lses = [], []
    for window, dil in DILATED_PATTERNS:
        o, lse = dilated_branch(q, k, v, window, dil)
        outs.append(o)
        lses.append(lse)
    wts = jax.nn.softmax(jnp.stack(lses, axis=0), axis=0)
    o = jnp.sum(wts[..., None] * jnp.stack(outs, axis=0), axis=0)
    return from_heads(o)

def conv_gated_mlp(h, w_up, conv_w, conv_b, w_down):
    u = h @ w_up
    u = lax.conv_general_dilated(u, conv_w[:, None, :].astype(u.dtype), window_strides=(1,),
                                 padding=[(CONV_WIDTH - 1, 0)],
                                 dimension_numbers=('NWC', 'WIO', 'NWC'),
                                 feature_group_count=u.shape[-1]) + conv_b
    gate, val = jnp.split(u, 2, axis=-1)
    return (jax.nn.silu(gate) * val) @ w_down

def second_inputs(seed: int = 0) -> dict:
    key = jax.random.key(seed)
    ks = jax.random.split(key, 16)
    nrm = jax.random.normal
    return {
        'x': nrm(ks[0], (BATCH, SEQ, D_MODEL), jnp.float32),
        'positions': jnp.broadcast_to(jnp.arange(SEQ, dtype=jnp.int32)[None, :], (BATCH, SEQ)),
        'g_mix': 1.0 + 0.02 * nrm(ks[1], (DEPTH_2, D_MODEL), jnp.float32),
        'w_in': nrm(ks[2], (DEPTH_2, D_MODEL, 3 * D_MODEL), jnp.float32) * D_MODEL ** -0.5,
        'w_out': nrm(ks[3], (DEPTH_2, D_MODEL, D_MODEL), jnp.float32) * D_MODEL ** -0.5,
        'lambda_q1': 0.1 * nrm(ks[4], (DEPTH_2, DIFF_DIM), jnp.float32),
        'lambda_k1': 0.1 * nrm(ks[5], (DEPTH_2, DIFF_DIM), jnp.float32),
        'lambda_q2': 0.1 * nrm(ks[6], (DEPTH_2, DIFF_DIM), jnp.float32),
        'lambda_k2': 0.1 * nrm(ks[7], (DEPTH_2, DIFF_DIM), jnp.float32),
        'g_diff': 1.0 + 0.02 * nrm(ks[8], (DEPTH_2, HEAD_DIM), jnp.float32),
        'g_ffn': 1.0 + 0.02 * nrm(ks[9], (DEPTH_2, D_MODEL), jnp.float32),
        'w_up': nrm(ks[10], (DEPTH_2, D_MODEL, 2 * D_FF), jnp.float32) * D_MODEL ** -0.5,
        'conv_w': nrm(ks[11], (DEPTH_2, CONV_WIDTH, 2 * D_FF), jnp.float32) * CONV_WIDTH ** -0.5,
        'conv_b': 0.01 * nrm(ks[12], (DEPTH_2, 2 * D_FF), jnp.float32),
        'w_down': nrm(ks[13], (DEPTH_2, D_FF, D_MODEL), jnp.float32) * D_FF ** -0.5,
        'g_final': 1.0 + 0.02 * nrm(ks[14], (D_MODEL,), jnp.float32),
    }

def second_block(x, positions, g_mix, w_in, w_out, lambda_q1, lambda_k1, lambda_q2, lambda_k2,
              g_diff, g_ffn, w_up, conv_w, conv_b, w_down, g_final):
    widths = [WIDTH_A] * 3 + [WIDTH_B] * 3 + [WIDTH_C] * 3
    cuts = []
    acc = 0
    for wd in widths[:-1]:
        acc += wd
        cuts.append(acc)
    for layer in range(DEPTH_2):
        h = rms_norm(x, g_mix[layer])
        qkv = h @ w_in[layer]
        qa, ka, va, qb, kb, vb, qc, kc, vc = jnp.split(qkv, cuts, axis=-1)
        lam_init = 0.8 - 0.6 * math.exp(-0.3 * layer)
        lam = (jnp.exp(jnp.sum(lambda_q1[layer].astype(jnp.float32) * lambda_k1[layer].astype(jnp.float32)))
               - jnp.exp(jnp.sum(lambda_q2[layer].astype(jnp.float32) * lambda_k2[layer].astype(jnp.float32)))
               + lam_init)
        o_a = differential_attention(qa, ka, va, positions, lam, g_diff[layer], lam_init).astype(x.dtype)
        o_b = moba_attention(qb, kb, vb, positions).astype(x.dtype)
        o_c = dilated_attention(qc, kc, vc, positions).astype(x.dtype)
        mix = jnp.concatenate([o_a, o_b, o_c], axis=-1)
        x = x + mix @ w_out[layer]
        h2 = rms_norm(x, g_ffn[layer])
        x = x + conv_gated_mlp(h2, w_up[layer], conv_w[layer], conv_b[layer], w_down[layer]).astype(x.dtype)
    return rms_norm(x, g_final)


def setup_inputs(seed=0):
    out = dict(first_inputs(seed))
    for name, value in second_inputs(seed + 1).items():
        if name != "x":
            out[name + "_2"] = value
    return out


def reference(
    x, c, ctx, c_ctx, w_ada, b_ada, norm_pre_mix, norm_post_mix, norm_pre_ffn, norm_post_ffn,
    w_in, na_rpb, ssd_conv_w, ssd_conv_b, ssd_a_log_fwd, ssd_a_log_bwd, ssd_dt_bias_fwd,
    ssd_dt_bias_bwd, ssd_d_skip, ssd_norm, w_branch_na, w_branch_ssd, w_out, w_router,
    w_exp_gate, w_exp_up, w_exp_down, positions_2, g_mix_2, w_in_2, w_out_2, lambda_q1_2,
    lambda_k1_2, lambda_q2_2, lambda_k2_2, g_diff_2, g_ffn_2, w_up_2, conv_w_2, conv_b_2,
    w_down_2, g_final_2,
):
    x = first_block(
        x, c, ctx, c_ctx, w_ada, b_ada, norm_pre_mix, norm_post_mix, norm_pre_ffn,
        norm_post_ffn, w_in, na_rpb, ssd_conv_w, ssd_conv_b, ssd_a_log_fwd, ssd_a_log_bwd,
        ssd_dt_bias_fwd, ssd_dt_bias_bwd, ssd_d_skip, ssd_norm, w_branch_na, w_branch_ssd,
        w_out, w_router, w_exp_gate, w_exp_up, w_exp_down,
    )
    return second_block(
        x, positions_2, g_mix_2, w_in_2, w_out_2, lambda_q1_2, lambda_k1_2, lambda_q2_2,
        lambda_k2_2, g_diff_2, g_ffn_2, w_up_2, conv_w_2, conv_b_2, w_down_2, g_final_2,
    )


_drawn_inputs = setup_inputs


def setup_inputs(seed=0):
    import zlib

    import numpy as np

    out = dict(_drawn_inputs(seed))
    spreads = {}
    factors = {'norm_post_ffn': 7.358,
     'na_rpb': 8.0,
     'ssd_d_skip': 3.347,
     'g_mix_2': 3.477,
     'lambda_k1_2': 4.677,
     'lambda_q2_2': 3.232,
     'lambda_k2_2': 3.15,
     'g_diff_2': 5.768,
     'g_ffn_2': 3.087,
     'conv_b_2': 5.911,
     'g_final_2': 2.839}
    for name, (base, spread) in spreads.items():
        noise = np.random.default_rng([zlib.crc32(name.encode()), seed]).standard_normal(out[name].shape)
        drawn = base * np.exp(spread * noise) if base else spread * noise
        out[name] = jnp.asarray(drawn.astype(out[name].dtype))
    for name, factor in factors.items():
        out[name] = (out[name] * factor).astype(out[name].dtype)
    return out
```

```python
import math

import numpy as np
import concourse.bass as bass
from concourse import mybir
from contextlib import ExitStack

F32 = mybir.dt.float32
I32 = mybir.dt.int32
ALU = mybir.AluOpType
ACT = mybir.ActivationFunctionType
AX = mybir.AxisListType

EPS = 1e-6
NEG = -1e30
MAGIC = 12582912.0
WSLOT = 2048

CQ, CK, CV, CZ, CX, CB, CC, CDT, CGN, CGS = 0, 1024, 2048, 3072, 5120, 7168, 7680, 8192, 8256, 9280


def shape_constants():
    parts, at, n = [], {}, 0

    def put(name, a):
        nonlocal n
        a = np.asarray(a, np.float32)
        at[name] = (n, n + a.shape[1])
        parts.append(a)
        n += a.shape[1]

    p = np.arange(128)
    put("ident", np.eye(128))
    put("ule", p[:, None] <= p[None, :])
    put("uge", p[:, None] >= p[None, :])
    put("ones", np.ones((128, 128)))
    put("negf", np.where(p[None, :] >= p[:, None], 0.0, NEG))
    put("negb", np.where(p[None, :] <= p[:, None], 0.0, NEG))
    dist = 384 + p[:, None] - np.arange(512)[None, :]
    put("causal", np.where(dist >= 0, 0.0, NEG))
    count = (dist >= 0) * ((dist <= 128) * 1.0 + (dist % 4 == 0) + (dist % 16 == 0))
    put("dilated", np.where(count > 0, np.log(np.maximum(count, 1.0)), NEG))
    rna = np.zeros((128, 128))
    rb = np.zeros((128, 128))
    rd = np.zeros((128, 128))
    for f in range(128):
        if f % 32 < 16:
            rna[f, f + 16] = -1
        else:
            rna[f, f - 16] = 1
        if f % 64 < 8:
            rb[f, f + 8] = -1
        elif f % 64 < 16:
            rb[f, f - 8] = 1
        if f % 32 < 4:
            rd[f, f + 4] = -1
        elif f % 32 < 8:
            rd[f, f - 4] = 1
    put("rna", rna.T)
    put("rb", rb.T)
    put("rd", rd.T)
    t = np.arange(512)
    inv = (np.float32(10000.0) ** (-np.arange(16, dtype=np.float32) / np.float32(16))).astype(np.float32)
    pos = np.where(((p % 64) < 32)[:, None], (t // 64)[None, :], (t % 64)[None, :]).astype(np.float32)
    ang = (pos * inv[p % 16][:, None]).astype(np.float32).astype(np.float64)
    put("nacos", np.cos(ang))
    put("nasin", np.sin(ang))
    ib = np.power(np.float32(500000.0), -np.arange(8, dtype=np.float32) * np.float32(2.0) / np.float32(16))
    idf = np.power(np.float32(500000.0), -np.arange(4, dtype=np.float32) * np.float32(2.0) / np.float32(8))
    put("invb", np.where(p % 64 < 16, ib[p % 8], 0.0)[:, None])
    put("invd", np.where(p % 32 < 8, idf[p % 4], 0.0)[:, None])
    col = np.arange(64)
    cs = np.clip(col - 8, 0, 48)
    ok = (col[None, :] >= cs[:, None]) & (col[None, :] < cs[:, None] + 16)
    put("colmask", np.where(ok[p % 64], 0.0, NEG))
    put("iota", np.tile(col[None, :], (128, 1)))
    return np.concatenate(parts, axis=1), at


class Engine:

    def __init__(self, sem):
        self.sem, self.count, self.todo, self.seen = sem, 0, [], {}

    def need(self, waits):
        for t in waits:
            if t is None:
                continue
            if isinstance(t, list):
                self.need(t)
                continue
            sem, v = t
            if self.seen.get(id(sem), 0) < v:
                self.seen[id(sem)] = v
                self.todo.append(lambda e, s=sem, v=v: e.wait_ge(s, v))

    def op(self, make, *waits, signal=True):
        self.need(waits)
        if not signal:
            self.todo.append(make)
            return None
        self.count += 1
        self.todo.append(lambda e: make(e).then_inc(self.sem, 1))
        return (self.sem, self.count)

    def run(self, e):
        for f in self.todo:
            f(e)


class Ring:

    def __init__(self, bufs):
        self.bufs, self.free, self.i = bufs, [[] for _ in bufs], -1

    def take(self):
        self.i += 1
        k = self.i % len(self.bufs)
        waits, self.free[k] = self.free[k], []
        return k, self.bufs[k], waits

    def release(self, k, *toks):
        self.free[k] = self.free[k] + list(toks)


def build(nc, A, out, dumps=None, stop=None):
    dumps = dumps or {}
    ctx = ExitStack()
    with ctx:
        arena = ctx.enter_context(nc.sbuf_tensor("arena", [128, 53200], F32))
        psum = ctx.enter_context(nc.psum_tensor("psum", [128, 4096], F32))
        nsem = [0]

        def sem(name=None):
            nsem[0] += 1
            return ctx.enter_context(nc.semaphore(name or f"s{nsem[0]}"))

        PE, DVE, AC, PL, SP = (Engine(sem("s_" + n)) for n in ("pe", "dve", "act", "pool", "sp"))
        ENG = [PE, DVE, AC, PL]

        def sb(a, n):
            return arena[:, a:a + n]

        def r3(ap, n):
            return ap.rearrange("p (a b) -> p a b", b=n)

        top = [0]

        def place(n):
            a = top[0]
            top[0] += n
            assert top[0] <= 53200, top[0]
            return sb(a, n)

        CN = A["consts"].shape[1]
        consts = place(CN)
        at = A["at"]

        def con(name):
            a, b = at[name]
            return consts[:, a:b]

        ident, ones = con("ident"), con("ones")
        WR = place(6 * WSLOT)
        cvT = place(16)
        cvb = place(1024)
        vecs = place(128 + 120 + 112 + 3 * 88)
        vmain, vcw, vcb = vecs[:, 0:128], vecs[:, 128:248], vecs[:, 248:360]
        vcw2 = vecs[:, 360:624]
        modc = place(64)
        gam1 = place(1024)
        gam2 = place(1024)
        small = place(256)
        BASE = top[0]

        banks = [psum[:, 512 * i:512 * i + 512] for i in range(8)]
        PS = Ring(banks)

        wslots = [WR[:, i * WSLOT:(i + 1) * WSLOT] for i in range(6)]
        wsems = [sem(f"s_w{i}") for i in range(8)]
        wcount = [0] * 8
        W = Ring(wslots)

        def mm(o, l, r, start, stop_, *waits, signal=False):
            return PE.op(lambda e: e.matmul(o, l, r, start=start, stop=stop_), *waits, signal=signal)

        def tr(o, i, *waits, signal=False):
            k = i.shape[0]
            return PE.op(lambda e: e.transpose(o, i, ident[0:k, 0:k]), *waits, signal=signal)

        def dma(eng, o, i, *waits, s=None):
            if s is None:
                s = [sem(), 0]
            s[1] += 16
            eng.need(waits)
            eng.todo.append(lambda e: e.dma_start(o, i).then_inc(s[0], 16))
            return (s[0], s[1])

        def tt(E, o, a, b, op, *waits):
            return E.op(lambda e: e.tensor_tensor(o, a, b, op), *waits)

        def ts(E, o, a, s1, op0, *waits, s2=None, op1=None):
            if op1 is None:
                return E.op(lambda e: e.tensor_scalar(o, a, s1, None, op0), *waits)
            return E.op(lambda e: e.tensor_scalar(o, a, s1, s2, op0, op1), *waits)

        def stt(o, a, s, b, op0, op1, *waits):
            return DVE.op(lambda e: e.scalar_tensor_tensor(out=o, in0=a, scalar=s, in1=b, op0=op0, op1=op1), *waits)

        def act(o, i, f, *waits, bias=0.0, scale=1.0, acc=None):
            if acc is not None:
                return AC.op(lambda e: e.activation(o, i, f, bias=bias, scale=scale, accum_out=acc), *waits)
            return AC.op(lambda e: e.activation(o, i, f, bias=bias, scale=scale), *waits)

        def copy(E, o, i, *waits):
            if E is AC:
                return act(o, i, ACT.Copy, *waits)
            return E.op(lambda e: e.tensor_copy(o, i), *waits)

        def zero(E, o, *waits):
            return E.op(lambda e: e.memset(o, 0.0), *waits)

        def recip(o, i, *waits):
            return DVE.op(lambda e: e.reciprocal(o, i), *waits)

        def reduce_(o, i, op, *waits, negate=None):
            return DVE.op(lambda e: e.tensor_reduce(o, i, AX.X, op, negate=negate), *waits)

        def latest():
            return [(E.sem, E.count) for E in ENG]

        def bc(ap, n):
            return ap.unsqueeze(2).to_broadcast([ap.shape[0], ap.shape[1], n])

        def rep(ap, n):
            return ap.unsqueeze(1).to_broadcast([ap.shape[0], n, ap.shape[1]])

        def wload(parts, *waits):
            k, buf, w = W.take()
            SP.need([w, list(waits)])
            for dst, src in parts(buf):
                wcount[k] += 16
                SP.todo.append(lambda e, d=dst, s=src, k=k: e.dma_start(d, s).then_inc(wsems[k], 16))
            return k, buf, (wsems[k], wcount[k])

        def wblock(src, r0, nk, c0, n):
            def parts(buf):
                d = r3(buf[:, 0:nk * n], n)
                return [(d, src[r0:r0 + 128 * nk, c0:c0 + n].rearrange("(k p) n -> p k n", p=128))]
            k, buf, tok = wload(parts)
            return k, r3(buf[:, 0:nk * n], n), tok, nk

        def wcols(src, rows, c0, n):
            nk = rows // 128
            return [wblock(src, r0 * 128, min(4, nk - r0), c0, n) for r0 in range(0, nk, 4)]

        def gemm(blocks, outs, stat, mov, evac, *waits):
            for n, i in enumerate(outs):
                b, bank, free = PS.take()
                kt = 0
                nkt = sum(x[3] for x in blocks)
                for k, w, tok, nk in blocks:
                    for j in range(nk):
                        o, l, r = shape_mm(bank, stat(i, kt, w[:, j, :]), mov(i, kt, w[:, j, :]))
                        last = mm(o, l, r, kt == 0, kt == nkt - 1, free, tok, list(waits),
                                  signal=(kt == nkt - 1 or (n == len(outs) - 1 and j == nk - 1)))
                        kt += 1
                    if n == len(outs) - 1:
                        W.release(k, last)
                PS.release(b, evac(i, o, last))

        def shape_mm(bank, l, r):
            m = l.shape[1]
            n = 1
            for d in r.shape[1:]:
                n *= d
            return bank[0:m, 0:n], l, r

        def chunked(blocks, outs, stat, mov, evac, per, *waits):
            opened = {}
            nkt = sum(x[3] for x in blocks)
            kt0 = 0
            for g in range(0, len(blocks), per):
                part = blocks[g:g + per]
                nk_part = sum(x[3] for x in part)
                for n, i in enumerate(outs):
                    if i not in opened:
                        opened[i] = PS.take()
                    b, bank, free = opened[i]
                    kt = kt0
                    for k, w, tok, nk in part:
                        for j in range(nk):
                            o, l, r = shape_mm(bank, stat(i, kt, w[:, j, :]), mov(i, kt, w[:, j, :]))
                            fin = kt == nkt - 1
                            last = mm(o, l, r, kt == 0, fin, free, tok, list(waits),
                                      signal=fin or (n == len(outs) - 1 and j == nk - 1))
                            kt += 1
                        if n == len(outs) - 1:
                            W.release(k, last)
                    if kt == nkt:
                        PS.release(b, evac(i, o, last))
                kt0 += nk_part

        def evac2(n):
            return AC if n % 2 else DVE

        setup = [dma(SP, consts, A["consts"])]
        dsem = [sem("s_vec"), 0]
        stage = sb(BASE, 6 * 128)
        z0 = zero(DVE, stage)
        rows = 0

        def vec(col, r, ap, n):
            return dma(AC, stage[r:r + n, col * 128:(col + 1) * 128], ap, z0, s=dsem)

        one = lambda ap: ap.rearrange("a (n p) -> (a n) p", p=128)
        vl = [
            (0, 0, one(A["b_ada"]), 48), (0, 48, one(A["norm_pre_mix"]), 8), (0, 56, one(A["norm_pre_ffn"]), 8),
            (0, 64, one(A["ssd_norm"]), 16), (0, 80, one(A["g_mix_2"]), 16), (0, 96, one(A["g_ffn_2"]), 16),
            (0, 112, one(A["c"]), 8), (0, 120, A["c_ctx"].rearrange("(n p) -> n p", p=128), 8),
            (1, 0, A["ssd_conv_w"].rearrange("a j (n p) -> (a j n) p", p=128), 120),
            (2, 0, one(A["ssd_conv_b"]), 24), (2, 24, one(A["conv_b_2"]), 88),
        ]
        cw2 = A["conv_w_2"].rearrange("a j (n p) -> (a j n) p", p=128)
        for i in range(3):
            vl.append((3 + i, 0, cw2[88 * i:88 * i + 88, :], 88))
        for col, r, ap, n in vl:
            tv = vec(col, r, ap, n)
        dst = [(vmain, 128), (vcw, 120), (vcb, 112)] + [(vcw2[:, 88 * i:88 * i + 88], 88) for i in range(3)]
        tvec = []
        for i, (d, n) in enumerate(dst):
            b, bank, free = PS.take()
            t = tr(bank[:, 0:128], stage[:, i * 128:(i + 1) * 128], free, tv, setup, signal=True)
            t = copy(DVE, d, bank[:, 0:n], t)
            PS.release(b, t)
            tvec.append(t)
        bada = vmain[:, 0:48]
        gpm, gpf, gssd = vmain[:, 48:56], vmain[:, 56:64], vmain[:, 64:80]
        gmix2, gffn2 = vmain[:, 80:96], vmain[:, 96:112]
        cv3 = r3(cvT, 2)
        t1 = act(cv3[:, :, 0], vmain[:, 112:120], ACT.Silu, tvec[0])
        t2 = act(cv3[:, :, 1], vmain[:, 120:128], ACT.Silu)
        tcb = copy(DVE, r3(cvb, 128), bc(cv3[:, :, 0], 128), t1)

        for ci, chunk in enumerate((0, 1, 3, 4)):
            for half in range(2):
                blocks = wcols(A["w_ada"], 1024, chunk * 1024 + half * 512, 512)

                def ev(i, o, tok, ci=ci, half=half, chunk=chunk):
                    j = half * 4 + i
                    d = modc[:, ci * 16 + j * 2:ci * 16 + j * 2 + 2]
                    return ts(DVE, d, o, bada[:, chunk * 8 + j:chunk * 8 + j + 1], ALU.add, tok)
                gemm(blocks, range(4), lambda i, kt, w: w[:, i * 128:(i + 1) * 128], lambda i, kt, w: cv3[:, kt, :], ev, t2)
        grow = sb(BASE + 1024, 4096)
        tg = []
        dsem2 = [sem("s_grow"), 0]
        bc1 = lambda ap: ap.rearrange("a n -> (a n)").partition_broadcast(128)
        for i, ap in enumerate((A["b_ada"][:, 2048:3072], A["b_ada"][:, 5120:6144], A["norm_post_mix"], A["norm_post_ffn"])):
            tgr = dma(AC, grow[:, i * 1024:(i + 1) * 1024], bc1(ap), s=dsem2)
        cvb3 = r3(cvb, 128)
        for gi, (chunk, dstg) in enumerate(((2, gam1), (5, gam2))):
            for half in range(2):
                blocks = wcols(A["w_ada"], 1024, chunk * 1024 + half * 512, 512)

                def ev(i, o, tok, gi=gi, half=half, dstg=dstg):
                    a = half * 512
                    d = dstg[:, a:a + 512]
                    t = tt(DVE, d, o, grow[:, gi * 1024 + a:gi * 1024 + a + 512], ALU.add, tok, tgr)
                    tg.append(tt(PL, d, d, grow[:, (2 + gi) * 1024 + a:(2 + gi) * 1024 + a + 512], ALU.mult, t))
                    return t
                gemm(blocks, [0], lambda i, kt, w: cvb3[:, kt, :], lambda i, kt, w: w, ev, tcb)
        mc = modc.rearrange("p (c j w) -> p c j w", c=4, w=2)
        t0 = latest()
        ta = []
        for ci, g in ((1, gpm), (3, gpf)):
            for w_ in range(2):
                d = mc[:, ci, :, w_]
                ta.append(stt(d, d, 1.0, g, ALU.add, ALU.mult, t0))
        tmod = ta + tg

        def rstd(v, n, *waits, mean=1024.0):
            s = small[:, 0:n]
            s2 = small[:, 64:64 + n]
            t = ts(DVE, v, v, 1.0 / mean, ALU.mult, list(waits), s2=EPS, op1=ALU.add)
            t = act(s, v, ACT.Ln, t)
            t = act(s, s, ACT.Exp, t, scale=-0.5)
            t = tt(DVE, s2, s, v, ALU.mult, t)
            t = tt(DVE, s2, s2, s, ALU.mult, t)
            t = ts(DVE, s2, s2, -0.5, ALU.mult, t, s2=1.5, op1=ALU.add)
            return tt(DVE, v, s, s2, ALU.mult, t)

        def normed_T(src, nt, HTd, junk, xn, ssq, scale_of, shift_of, *waits):
            tq = list(waits)
            for i in range(nt):
                tq = [act(junk[:, 0:1024], src[:, i, :], ACT.Square, tq, acc=ssq[:, i:i + 1])]
            t = rstd(ssq[:, 0:nt], nt, tq)
            tx = [ts(DVE if i % 2 else PL, xn[:, i, :], src[:, i, :], ssq[:, i:i + 1], ALU.mult, t) for i in range(nt)]
            done = []
            for j in range(8):
                b, bank, free = PS.take()
                for i in range(nt):
                    last = tr(bank[:, i * 128:(i + 1) * 128], xn[:, i, j * 128:(j + 1) * 128], free, tx[i],
                              signal=(i == nt - 1))
                s1, s2 = scale_of(j), shift_of(j)
                if s2 is None:
                    t = act(HTd[:, j, :], bank[:, 0:nt * 128], ACT.Copy, last, scale=s1)
                elif j % 2:
                    t = act(HTd[:, j, :], bank[:, 0:nt * 128], ACT.Identity, last, scale=s1, bias=s2)
                else:
                    t = ts(DVE, HTd[:, j, :], bank[:, 0:nt * 128], s1, ALU.mult, last, s2=s2, op1=ALU.add)
                PS.release(b, t)
                done.append(t)
            return done

        o = BASE
        HT = r3(sb(o, 6144), 768)
        o += 6144
        PB = o
        xin = r3(sb(o + 5120, 4096), 1024)
        cin = r3(sb(o + 9216, 2048), 1024)
        tb = latest()
        xT = A["x"].rearrange("a (t p) d -> p (a t) d", p=128)
        tx = dma(AC, xin, xT, tb)
        tc_ = dma(AC, cin, A["ctx"].rearrange("a (t p) d -> p (a t) d", p=128), tb)
        xn = r3(sb(o + 11264, 6144), 1024)
        junk = sb(o + 17408, 1024)
        ssq = small[:, 128:144]
        th = normed_T(xin, 4, HT[:, :, 0:512], junk, xn, ssq[:, 0:4], lambda j: mc[:, 1, j, 0:1], lambda j: mc[:, 0, j, 0:1], tx, tmod)
        tcx = normed_T(cin, 2, HT[:, :, 512:768], junk, xn[:, 4:6, :], ssq[:, 4:6], lambda j: mc[:, 1, j, 1:2], lambda j: mc[:, 0, j, 1:2], tc_)
        tH = th + tcx
        tdump = []
        tyD = []

        def dump(name, ap, *waits):
            if name in dumps:
                tdump.append(dma(SP, dumps[name], ap, latest(), list(waits)))
                for E in ENG:
                    E.need([tdump[-1]])

        dump("HT", HT)

        def dram(name, shape):
            return nc.dram_tensor(name, shape, F32, kind="Internal").ap()

        if stop != "B":
            yD = dram("yT_scratch", [128, 16, 512])
            acsD = dram("acs_scratch", [64, 512])
            tb = latest()
            o = PB
            BF = r3(sb(o, 3072), 768); o += 3072
            CF = r3(sb(o, 2048), 512); o += 2048
            BT = r3(sb(o, 768), 128); o += 768
            pads = Ring([sb(o + 776 * i, 776) for i in range(2)]); o += 1552
            accs = Ring([sb(o + 776 * i, 772) for i in range(2)]); o += 1552
            xsF = Ring([sb(o, 768)]); o += 768
            xsT = r3(sb(o, 3072), 512); o += 3072
            hf = r3(sb(o, 2048), 512); o += 2048
            hb = r3(sb(o, 2048), 512); o += 2048
            zs = r3(sb(o, 2048), 512); o += 2048
            yTr = Ring([sb(o, 512)]); o += 512
            RBr = Ring([sb(o + 512 * i, 512) for i in range(2)]); o += 1024
            Er = Ring([sb(o + 512 * i, 512) for i in range(3)]); o += 1536
            XD = Ring([sb(o + 512 * i, 512) for i in range(4)]); o += 2048
            TY = Ring([sb(o + 512 * i, 512) for i in range(3)]); o += 1536
            cbr = Ring([sb(o + 128 * i, 128) for i in range(2)]); o += 256
            dt, acs = cvb[:, 0:384], cvb[:, 384:768]
            d1, atot = XD.bufs[0][:, 0:384], XD.bufs[1][:, 0:384]
            eac = sb(o, 384); o += 384
            wst = sb(o, 384); o += 384
            cdec = sb(o, 384); o += 384
            rows64 = sb(o, 64 * 2 + 32); o += 160
            assert o <= 53200, o
            tz = []
            for p_ in pads.bufs:
                for a, b in ((0, 2), (514, 518), (774, 776)):
                    tz.append(zero(DVE, p_[:, a:b], tb))
            dtb, nA, dsk = rows64[:, 0:64], rows64[:, 64:128], rows64[:, 128:160]
            rs = [sem("s_rows"), 0]
            for d, ap in ((dtb[:, 0:32], A["ssd_dt_bias_fwd"]), (dtb[:, 32:64], A["ssd_dt_bias_bwd"]),
                          (nA[:, 0:32], A["ssd_a_log_fwd"]), (nA[:, 32:64], A["ssd_a_log_bwd"]), (dsk, A["ssd_d_skip"])):
                tr_ = dma(AC, d, bc1(ap), tb, s=rs)
            t = act(nA, nA, ACT.Exp, tr_)
            tnA = ts(DVE, nA, nA, -1.0, ALU.mult, t)
            blk = wblock(A["w_in"], 0, 8, CDT, 64)
            b, bank, free = PS.take()
            for i in range(6):
                for kt in range(8):
                    last = mm(bank[:, i * 64:(i + 1) * 64], HT[:, kt, i * 128:(i + 1) * 128], blk[1][:, kt, :],
                              kt == 0, kt == 7, free, blk[2], tH, signal=(i == 5 and kt == 7))
            W.release(blk[0], last)
            raw = dt
            t = tt(DVE, r3(raw, 64), r3(bank[:, 0:384], 64), rep(dtb, 6), ALU.add, last, tr_, tb)
            PS.release(b, t)
            t = stt(d1, raw, -1.0, raw, ALU.mult, ALU.max, t)
            t = act(acs, d1, ACT.Exp, t, scale=-1.0)
            t = ts(DVE, d1, acs, 1.0, ALU.add, t)
            tl = act(eac, d1, ACT.Ln, t)
            t = ts(DVE, atot, d1, -1.0, ALU.add, t)
            t = tt(DVE, acs, acs, atot, ALU.subtract, t)
            t = recip(d1, d1, t, tl)
            t = tt(DVE, acs, acs, d1, ALU.mult, t)
            t = tt(DVE, acs, acs, eac, ALU.add, t, tl)
            tdt = stt(dt, raw, 0.0, acs, ALU.max, ALU.add, t)
            a_ = d1
            ta_ = tt(DVE, r3(a_, 64), r3(dt, 64), rep(nA, 6), ALU.mult, tdt, tnA)
            a3 = r3(a_, 64)
            b, bank, free = PS.take()
            o3 = r3(bank[:, 0:384], 64)
            mm(bank[:, 0:192], con("ule"), a3[:, :, 0:32], True, True, free, ta_)
            last = mm(bank[:, 192:384], con("uge"), a3[:, :, 32:64], True, True, signal=True)
            ac3 = r3(acs, 64)
            t = copy(DVE, ac3[:, :, 0:32], r3(bank[:, 0:192], 32), last)
            tac = copy(DVE, ac3[:, :, 32:64], r3(bank[:, 192:384], 32), last)
            PS.release(b, tac)
            b, bank, free = PS.take()
            last = mm(bank[:, 0:384], ones, a_, True, True, free, signal=True)
            tat = copy(DVE, atot, bank[:, 0:384], last)
            PS.release(b, tat)
            tcd = act(cdec, atot, ACT.Exp, tat)
            XD.release(1, tcd)
            tea = act(eac, acs, ACT.Exp, tac)
            t = tt(DVE, wst, atot, acs, ALU.subtract, tat, tac)
            t = act(wst, wst, ACT.Exp, t)
            tws = tt(DVE, wst, wst, dt, ALU.mult, t)
            acT = TY.bufs[0][0:64, :]
            b, bank, free = PS.take()
            for i in range(4):
                last = tr(bank[0:64, i * 128:(i + 1) * 128], ac3[:, i, :], free, tac, signal=(i == 3))
            t = copy(DVE, acT, bank[0:64, 0:512], last)
            PS.release(b, t)
            tacD = dma(AC, acsD, acT, t)
            TY.release(0, tacD)

            def conv_tile(blocks, i, ti, dx, dc, *dwaits):
                b1, k1, f1 = PS.take()
                for kt in range(8):
                    blk = blocks[kt // 4]
                    last1 = mm(k1[:, 0:512], blk[1][:, kt % 4, i * 128:(i + 1) * 128], HT[:, kt, 0:512],
                               kt == 0, kt == 7, f1, blk[2], tH, signal=(kt == 7))
                b2, k2, f2 = PS.take()
                for kt in range(8):
                    blk = blocks[kt // 4]
                    last2 = mm(k2[:, 0:256], blk[1][:, kt % 4, i * 128:(i + 1) * 128], HT[:, kt, 512:768],
                               kt == 0, kt == 7, f2, signal=(kt == 7))
                pk, pad, pf = pads.take()
                c1 = copy(AC, pad[:, 2:514], k1[:, 0:512], last1, pf, tz)
                c2 = copy(AC, pad[:, 518:774], k2[:, 0:256], last2)
                PS.release(b1, c1)
                PS.release(b2, c2)
                ak, ac_, af = accs.take()
                w5 = lambda j: vcw[:, j * 24 + ti:j * 24 + ti + 1]
                t = ts(DVE, ac_, pad[:, 0:772], w5(0), ALU.mult, c1, c2, af)
                for j in range(1, 5):
                    t = stt(ac_, pad[:, j:j + 772], w5(j), ac_, ALU.mult, ALU.add, t)
                pads.release(pk, t)
                bias = vcb[:, ti:ti + 1]
                s1 = act(dx, ac_[:, 0:512], ACT.Silu, t, list(dwaits), bias=bias)
                s2 = s1
                if dc is not None:
                    s2 = act(dc, ac_[:, 516:772], ACT.Silu, bias=bias)
                accs.release(ak, s2)
                return s2, last2

            tBF, tCF = [], []
            blocks = wcols(A["w_in"], 1024, CB, 512)
            for g in range(4):
                t, last = conv_tile(blocks, g, 16 + g, BF[:, g, 0:512], BF[:, g, 512:768], tb)
                tBF.append(t)
            for x_ in blocks:
                W.release(x_[0], last)
            blocks = wcols(A["w_in"], 1024, CC, 512)
            for g in range(4):
                t, last = conv_tile(blocks, g, 20 + g, CF[:, g, :], None, tb)
                tCF.append(t)
            for x_ in blocks:
                W.release(x_[0], last)
            dump("BF", BF)
            dump("CF", CF)
            dump("dt", dt)
            dump("acs", acs)

            ysem = [[sem(f"s_yD{i}"), 0] for i in range(2)]
            rbs = [[sem(f"s_rb{i}"), 0] for i in range(3)]
            prev_y = []
            prev_xs = []
            tyD = [None, None]
            for g in range(4):
                hd = slice(8 * g, 8 * g + 8)
                blocks = wcols(A["w_in"], 1024, CX + 512 * g, 512)
                txs = []
                for i in range(4):
                    k, xf, f = xsF.take()
                    t, last = conv_tile(blocks, i, 4 * g + i, xf[:, 0:512], xf[:, 512:768], f)
                    for part, n in ((0, 4), (4, 2)):
                        b, bank, free = PS.take()
                        for c in range(n):
                            lt = tr(bank[:, c * 128:(c + 1) * 128], xf[:, (part + c) * 128:(part + c + 1) * 128], free, t,
                                    signal=(c == n - 1))
                        e = copy(AC if part else DVE, xsT[:, part:part + n, i * 128:(i + 1) * 128], r3(bank[:, 0:n * 128], 128), lt, prev_xs)
                        PS.release(b, e)
                        txs.append(e)
                    xsF.release(k, lt)
                for x_ in blocks:
                    W.release(x_[0], last)
                tbt = []
                for part, n in ((0, 4), (4, 2)):
                    b, bank, free = PS.take()
                    for c in range(n):
                        lt = tr(bank[:, c * 128:(c + 1) * 128], BF[:, g, (part + c) * 128:(part + c + 1) * 128], free,
                                tBF[g], signal=(c == n - 1))
                    e = copy(DVE, BT[:, part:part + n, :], r3(bank[:, 0:n * 128], 128), lt, prev_xs)
                    PS.release(b, e)
                    tbt.append(e)
                blocks = wcols(A["w_in"], 1024, CZ + 512 * g, 512)
                tzs = []

                def ev(i, o_, tok):
                    t = act(zs[:, i, :], o_, ACT.Silu, tok, prev_y)
                    tzs.append(t)
                    return t
                gemm(blocks, range(4), lambda i, kt, w: HT[:, kt, i * 128:(i + 1) * 128], lambda i, kt, w: w, ev, tH)

                def state(c, d):
                    k, xd, f = XD.take()
                    wv = r3(wst, 64)[:, c, 32 * d + 8 * g:32 * d + 8 * g + 8]
                    t = tt(PL, r3(xd, 64), r3(xsT[:, c, :], 64), bc(wv, 64), ALU.mult, f, txs, tws)
                    b, bank, free = PS.take()
                    lt = mm(bank, BT[:, c, :], xd, True, True, free, tbt, t, signal=True)
                    XD.release(k, lt)
                    return b, bank, lt

                th_ = []
                hfin = prev_y
                for d, H_, order in ((0, hf, (4, 5, 0, 1, 2)), (1, hb, (5, 4, 3, 2, 1))):
                    slots = (0, 0, 1, 2, 3) if d == 0 else (3, 3, 2, 1, 0)
                    t = None
                    for n, c in enumerate(order):
                        b, bank, lt = state(c, d)
                        dstn = H_[:, slots[n], :]
                        if n == 0:
                            t = copy(DVE, dstn, bank, lt, hfin)
                        else:
                            srcn = H_[:, slots[n - 1], :]
                            cd = bc(r3(cdec, 64)[:, c, 32 * d + 8 * g:32 * d + 8 * g + 8], 64)
                            t = tt(DVE, r3(dstn, 64), r3(srcn, 64), cd, ALU.mult, t, tcd)
                            t = tt(DVE, dstn, dstn, bank, ALU.add, t, lt)
                        PS.release(b, t)
                    th_.append(t)
                tus = []
                ylast = []
                ssy = small[:, 160:164]
                for c in range(4):
                    cs_ = slice(c * 128, (c + 1) * 128)
                    b, bank, free = PS.take()
                    lt = mm(bank[:, 0:128], BF[:, g, cs_], CF[:, g, cs_], True, True, free, tBF[g], tCF[g], signal=True)
                    ck, cb, cf = cbr.take()
                    tcb_ = copy(AC, cb, bank[:, 0:128], lt, cf)
                    PS.release(b, tcb_)
                    xd2 = []
                    for d in range(2):
                        k, xd, f = XD.take()
                        dv = r3(dt, 64)[:, c, 32 * d + 8 * g:32 * d + 8 * g + 8]
                        t = tt(PL, r3(xd, 64), r3(xsT[:, c, :], 64), bc(dv, 64), ALU.mult, f, txs, tdt)
                        xd2.append((k, xd, t))
                    M = {}
                    yb, ybank, yfree = PS.take()
                    mt = []
                    for hq in range(2):
                        for d in range(2):
                            h0 = 8 * g + 4 * hq
                            rk, rb, rf = RBr.take()
                            srcr = acsD[32 * d + h0:32 * d + h0 + 4, cs_]
                            td = dma(AC, r3(rb, 128), srcr.partition_broadcast(128), rf, tacD, s=rbs[rk])
                            colv = ac3[:, c, 32 * d + h0:32 * d + h0 + 4]
                            t = tt(DVE, r3(rb, 128), r3(rb, 128), bc(colv, 128), ALU.subtract, td, tac)
                            t = tt(PL, r3(rb, 128), r3(rb, 128), rep(con("negb" if d else "negf"), 4), ALU.add, t)
                            ek, eb, ef = Er.take()
                            t = act(eb, rb, ACT.Exp, t, ef)
                            RBr.release(rk, t)
                            tm = tt(PL, r3(eb, 128), r3(eb, 128), rep(cb, 4), ALU.mult, t, tcb_)
                            M[d] = (ek, r3(eb, 128), tm)
                        for h in range(4):
                            hh = 4 * hq + h
                            for d in range(2):
                                ek, eb, tm = M[d]
                                lt = mm(ybank[:, hh * 64:hh * 64 + 64], eb[:, h, :], xd2[d][1][:, hh * 64:hh * 64 + 64],
                                        d == 0, d == 1, yfree, tm, xd2[d][2], signal=(h == 3 and d == 1))
                        for d in range(2):
                            Er.release(M[d][0], lt)
                    cbr.release(ck, tm)
                    for k, _, _ in xd2:
                        XD.release(k, lt)
                    tydiag = lt
                    ts_ = []
                    ty = []
                    for d, H_ in ((0, hf), (1, hb)):
                        b, bank, free = PS.take()
                        lt = mm(bank, CF[:, g, cs_], H_[:, c, :], True, True, free, tCF[g], th_[d], signal=True)
                        k, tb1, f = TY.take()
                        ev_ = bc(r3(eac, 64)[:, c, 32 * d + 8 * g:32 * d + 8 * g + 8], 64)
                        t = tt(DVE, r3(tb1, 64), r3(bank, 64), ev_, ALU.mult, lt, tea, f)
                        PS.release(b, t)
                        ty.append((k, tb1, t))
                    t = tt(PL, ty[0][1], ty[0][1], ty[1][1], ALU.add, ty[0][2], ty[1][2])
                    k, tb2, f = TY.take()
                    t2_ = tt(PL, r3(tb2, 64), r3(xsT[:, c, :], 64), bc(dsk[:, 8 * g:8 * g + 8], 64), ALU.mult, f, txs, tr_)
                    t3 = tt(PL, ty[0][1], ty[0][1], tb2, ALU.add, t, t2_)
                    t4 = tt(DVE, ty[0][1], ybank, ty[0][1], ALU.add, t3, tydiag)
                    PS.release(yb, t4)
                    if g == 0:
                        dump(f"y{c}", ty[0][1], t4)
                    t5 = tt(DVE, zs[:, c, :], zs[:, c, :], ty[0][1], ALU.mult, t4, tzs)
                    TY.release(ty[0][0], t5)
                    TY.release(ty[1][0], t)
                    TY.release(k, t3)
                    k, tb3, f = TY.take()
                    t6 = act(tb3, zs[:, c, :], ACT.Square, t5, f, acc=ssy[:, c:c + 1])
                    TY.release(k, t6)
                    tus.append(t6)
                prev_xs = [tydiag, t3, tm, (PL.sem, PL.count), (PE.sem, PE.count)]
                t = rstd(ssy, 4, tus, mean=512.0)
                tn = [ts(PL if c % 2 else DVE, zs[:, c, :], zs[:, c, :], ssy[:, c:c + 1], ALU.mult, t) for c in range(4)]
                for i in range(4):
                    b, bank, free = PS.take()
                    for c in range(4):
                        lt = tr(bank[:, c * 128:(c + 1) * 128], zs[:, c, i * 128:(i + 1) * 128], free, tn, signal=(c == 3))
                    k, yt, f = yTr.take()
                    t = act(yt, bank, ACT.Copy, lt, f, scale=gssd[:, 4 * g + i:4 * g + i + 1])
                    PS.release(b, t)
                    td = dma(AC, yD[:, 4 * g + i, :], yt, t, s=ysem[k])
                    yTr.release(k, td)
                    tyD[k] = td
                prev_y = [lt, (PE.sem, PE.count), (DVE.sem, DVE.count), (PL.sem, PL.count)]

        def attention(units, Sr, PTr, waits):
            small_ring = Ring([small[:, 176 + 4 * i:180 + 4 * i] for i in range(8)])

            def scores(u):
                u["P"] = []
                for m in u["maps"]:
                    sk, S, sf = Sr.take()
                    vk, sv, vf = small_ring.take()
                    n = 0
                    td = []
                    for kp, kn, bias in m["keys"]:
                        b, bank, free = PS.take()
                        lt = mm(bank[:, 0:kn], m["q"], kp, True, True, free, waits, signal=True)
                        if bias is None:
                            t = act(S[:, n:n + kn], bank[:, 0:kn], ACT.Copy, lt, sf, scale=u["scale"])
                        else:
                            bap, btok = bias()
                            t = stt(S[:, n:n + kn], bank[:, 0:kn], u["scale"], bap, ALU.mult, ALU.add, lt, sf, btok)
                            tbias = t
                        PS.release(b, t)
                        td.append(t)
                        n += kn
                    t = reduce_(sv[:, 0:1], S[:, 0:n], ALU.max, td, vf, negate=True)
                    t = act(S[:, 0:n], S[:, 0:n], ACT.Exp, t, bias=sv[:, 0:1], acc=sv[:, 1:2])
                    t = recip(sv[:, 1:2], sv[:, 1:2], t)
                    u["P"].append((sk, S, vk, sv, t, n))
                if "post" in u:
                    u["post"](tbias)
                if len(u["P"]) == 2:
                    (sk0, S0, vk0, sv0, t0, n), (sk1, S1, vk1, sv1, t1, _) = u["P"]
                    t = tt(DVE, sv1[:, 2:3], sv1[:, 1:2], u["nlam"], ALU.mult, t1)
                    t = ts(PL, S1[:, 0:n], S1[:, 0:n], sv1[:, 2:3], ALU.mult, t)
                    t = stt(S0[:, 0:n], S0[:, 0:n], sv0[:, 1:2], S1[:, 0:n], ALU.mult, ALU.add, t, t0)
                    Sr.release(sk1, t)
                    small_ring.release(vk1, t)
                    u["P"] = [(sk0, S0, vk0, sv0, t, n)]

            def turn(u, par):
                sk, S, vk, sv, t, n = u["P"][0]
                pk, PT, pf = PTr.take()
                te = []
                for a in range(0, n, 512):
                    m_ = min(512, n - a)
                    b, bank, free = PS.take()
                    for j in range(m_ // 128):
                        lt = tr(bank[:, j * 128:(j + 1) * 128], S[:, a + j * 128:a + (j + 1) * 128], free, t,
                                signal=(j == m_ // 128 - 1))
                    e = copy(AC if (a or par) else DVE, PT[:, a:a + m_], bank[:, 0:m_], lt, pf)
                    PS.release(b, e)
                    te.append(e)
                Sr.release(sk, lt)
                u["PT"] = (pk, PT, te)

            def values(u):
                sk, S, vk, sv, t, n = u["P"][0]
                pk, PT, te = u["PT"]
                b, bank, free = PS.take()
                nk = n // 128
                for j in range(nk):
                    lt = mm(bank[:, 0:64], PT[:, j * 128:(j + 1) * 128], u["v"](j), j == 0, j == nk - 1, free, te, waits,
                            signal=(j == nk - 1))
                PTr.release(pk, lt)
                t2 = u["out"](bank[:, 0:64], lt, sv)
                PS.release(b, t2)
                small_ring.release(vk, t2)

            N = len(units)
            for i in range(N + 3):
                if i < N:
                    if "pre" in units[i]:
                        units[i]["pre"]()
                    scores(units[i])
                if 0 <= i - 2 < N:
                    turn(units[i - 2], i % 2)
                if 0 <= i - 3 < N:
                    values(units[i - 3])

        def rope(blocks, i, par, cos, sin, rot, dests, tmp, waits, ttab):
            b1, k1, f1 = PS.take()
            for kt in range(8):
                blk = blocks[kt // 4]
                l1 = mm(k1[:, 0:512], blk[1][:, kt % 4, i * 128:(i + 1) * 128], HT[:, kt, 0:512], kt == 0, kt == 7,
                        f1, blk[2], waits, signal=(kt == 7))
            rk, (raw, tc1, tc2), rf = tmp.take()
            t = copy(AC, raw, k1[:, 0:512], l1, rf)
            PS.release(b1, t)
            b2, k2, f2 = PS.take()
            l2 = mm(k2[:, 0:512], rot, raw, True, True, f2, t, signal=True)
            ta1 = tt(PL, tc1, raw, cos, ALU.mult, t, ttab)
            tb1 = tt(DVE, tc2, k2[:, 0:512], sin, ALU.mult, l2, ttab)
            PS.release(b2, tb1)
            tds = []
            for n, (a, z, d) in enumerate(dests):
                E_ = PL if z - a == 128 else DVE
                tds.append(tt(E_, d[a:z, :], tc1[a:z, :], tc2[a:z, :], ALU.add, ta1, tb1, waits))
            tmp.release(rk, tds, l2)
            return tds, l1

        if stop not in ("B", "C"):
            o = PB
            kF = r3(sb(o, 3072), 768); o += 3072
            qP = r3(sb(o, 4096), 512); o += 4096
            V = r3(sb(o, 3072), 512); o += 3072
            O = r3(sb(o, 4096), 1024); o += 4096
            oT = r3(sb(o, 4096), 512); o += 4096
            biasr = Ring([sb(o + 896 * i, 896) for i in range(2)]); o += 1792
            Sr = Ring([sb(o + 768 * i, 768) for i in range(3)]); o += 2304
            PTr = Ring([sb(o + 768 * i, 768) for i in range(2)]); o += 1536
            tmp = Ring([tuple(sb(o + 1536 * i + 512 * j, 512) for j in range(3)) for i in range(2)]); o += 3072
            assert o <= 53200, o
            tb = latest() + tyD
            rp = dram("rpb_copies", [16, 64, 465])
            rpb = A["na_rpb"]
            trp = dma(AC, rp, bass.AP(rpb.tensor, 0, [[465, 16], [0, 64], [1, 465]]), tb)
            tzq = [zero(DVE, qP.rearrange("p a b -> p (a b)"), tb, trp)]
            bsem = [[sem(f"s_bias{i}"), 0] for i in range(2)]
            prev = [tb, trp]
            tOall = []
            for half in range(2):
                tq, tk, tv_ = [], [], []
                blocks = wcols(A["w_in"], 1024, CQ + 512 * half, 512)
                for i in range(4):
                    tds, last = rope(blocks, i, 0, con("nacos"), con("nasin"), con("rna"),
                                     [(0, 64, qP[:, 2 * i, :]), (64, 128, qP[:, 2 * i + 1, :])], tmp, [tH, prev, tzq], [])
                    tq.append(tds)
                for x_ in blocks:
                    W.release(x_[0], last)
                blocks = wcols(A["w_in"], 1024, CK + 512 * half, 512)
                for i in range(4):
                    tds, last = rope(blocks, i, 0, con("nacos"), con("nasin"), con("rna"), [(0, 128, kF[:, i, 0:512])], tmp, [tH, prev], [])
                    b2, k2, f2 = PS.take()
                    for kt in range(8):
                        blk = blocks[kt // 4]
                        last = mm(k2[:, 0:256], blk[1][:, kt % 4, i * 128:(i + 1) * 128], HT[:, kt, 512:768], kt == 0, kt == 7,
                                  f2, signal=(kt == 7))
                    t = copy(AC, kF[:, i, 512:768], k2[:, 0:256], last, prev)
                    PS.release(b2, t)
                    tk.append([tds, t])
                for x_ in blocks:
                    W.release(x_[0], last)
                blocks = wcols(A["w_in"], 1024, CV + 512 * half, 512)

                def ev(i, o_, tok):
                    t = copy(evac2(i), V[:, i, :], o_, tok, prev)
                    tv_.append(t)
                    return t
                gemm(blocks, range(6), lambda i, kt, w: HT[:, kt, i * 128:(i + 1) * 128], lambda i, kt, w: w, ev, tH)
                units = []
                for hl in range(8):
                    h = 8 * half + hl
                    st = {}

                    def pre(h=h, st=st):
                        k, bb, f = biasr.take()
                        for a in range(2):
                            base = h * 29760 + (1 - a) * 31 + 15
                            src = bass.AP(rp.tensor, base, [[464, 64], [31, 14], [1, 64]])
                            td = dma(AC, r3(bb[64 * a:64 * a + 64, :], 64), src, f, trp, s=bsem[k])
                        st["k"], st["b"] = k, bb
                        st["t"] = tt(PL, r3(bb, 64), r3(bb, 64), rep(con("colmask"), 14), ALU.add, td)

                    for qt in range(4):
                        def outf(ps, lt, sv, qt=qt, h=h):
                            t = ts(DVE, O[:, qt, h * 64:(h + 1) * 64], ps, sv[:, 1:2], ALU.mult, lt)
                            tOall.append(t)
                            return t
                        q = qP[:, 2 * (hl // 2) + hl % 2, qt * 128:(qt + 1) * 128]
                        kk = kF[:, hl // 2, :]

                        def bias(st=st, qt=qt):
                            return st["b"][:, (6 - 2 * qt) * 64:(6 - 2 * qt) * 64 + 512], st["t"]
                        u = dict(maps=[dict(q=q, keys=[(kk[:, 0:512], 512, bias), (kk[:, 512:768], 256, None)])],
                                 scale=0.125, out=outf, v=lambda j, hl=hl: V[:, j, hl * 64:(hl + 1) * 64])
                        if qt == 0:
                            u["pre"] = pre
                        if qt == 3:
                            u["post"] = lambda t, st=st: biasr.release(st["k"], t)
                        units.append(u)
                attention(units, Sr, PTr, [tq, tk, tv_])
                prev = [(PE.sem, PE.count)]
                tzq = []
            dump("O", O)
            toT = []
            for j in range(8):
                b, bank, free = PS.take()
                for i in range(4):
                    lt = tr(bank[:, i * 128:(i + 1) * 128], O[:, i, j * 128:(j + 1) * 128], free, tOall[-1], signal=(i == 3))
                t = copy(evac2(j), oT[:, j, :], bank, lt)
                PS.release(b, t)
                toT.append(t)

        if stop not in ("B", "C", "D"):
            tb = latest()
            yT = r3(sb(PB, 8192), 512)
            G = r3(sb(PB + 8192, 2048), 512)
            o = PB + 3072 + 4096 + 3072 + 4096 + 4096
            uT = r3(sb(o, 4096), 512); o += 4096
            mix = r3(sb(o, 4096), 1024); o += 4096
            tmpE = Ring([sb(PB + 10240, 512), sb(PB + 10752, 512)])
            assert o <= 53200, o
            ty_ = dma(AC, yT, yD, tb, tyD)
            tu = {}
            tG = {}
            for br, (cg, wsrc, rows_, src_) in enumerate(((CGN, A["w_branch_na"], 1024, oT), (CGS, A["w_branch_ssd"], 2048, yT))):
                for half in range(2):
                    blocks = wcols(A["w_in"], 1024, cg + 512 * half, 512)

                    def ev(i, o_, tok):
                        t = act(G[:, i, :], o_, ACT.Sigmoid, tok, tb, tG.get(("r", i)))
                        tG[i] = t
                        return t
                    gemm(blocks, range(4), lambda i, kt, w: w[:, i * 128:(i + 1) * 128], lambda i, kt, w: HT[:, kt, 0:512], ev, tH)
                    blocks = wcols(wsrc, rows_, 512 * half, 512)

                    def ev(i, o_, tok, half=half, br=br):
                        j = half * 4 + i
                        if br == 0:
                            t = tt(DVE, uT[:, j, :], o_, G[:, i, :], ALU.mult, tok, tG[i], tb)
                            tG[("r", i)] = t
                            tu[j] = t
                            return t
                        k, tm_, f = tmpE.take()
                        t = tt(DVE, tm_, o_, G[:, i, :], ALU.mult, tok, tG[i], f)
                        tG[("r", i)] = t
                        tu[j] = tt(PL, uT[:, j, :], uT[:, j, :], tm_, ALU.add, t, tu[j])
                        tmpE.release(k, tu[j])
                        return t
                    chunked(blocks, range(4), lambda i, kt, w: w[:, i * 128:(i + 1) * 128],
                            lambda i, kt, w, src_=src_: src_[:, kt, :], ev, 2, ty_ if br else None, toT)
            tu_ = [tu[j] for j in range(8)]
            tmx = []
            for half in range(2):
                blocks = wcols(A["w_out"], 1024, 512 * half, 512)

                def ev(i, o_, tok, half=half):
                    t = copy(evac2(i), mix[:, i, half * 512:half * 512 + 512], o_, tok, tb)
                    tmx.append(t)
                    return t
                gemm(blocks, range(4), lambda i, kt, w: uT[:, kt, i * 128:(i + 1) * 128], lambda i, kt, w: w, ev, tu_)
            dump("mix", mix)

        X = r3(sb(BASE, 4096), 1024)
        HT2 = r3(sb(BASE + 4096, 4096), 512)
        PF = BASE + 8192

        def residual(m, gam, ssq_, junk_, tm_, txload):
            tq = tm_
            for i in range(4):
                tq = [act(junk_, m[:, i, :], ACT.Square, tq, acc=ssq_[:, i:i + 1])]
            t = rstd(ssq_, 4, tq)
            done = []
            for i in range(4):
                t1 = stt(m[:, i, :], m[:, i, :], ssq_[:, i:i + 1], gam, ALU.mult, ALU.mult, t)
                done.append(tt(PL if i % 2 else DVE, X[:, i, :], X[:, i, :], m[:, i, :], ALU.add, t1, txload))
            return done

        if stop not in ("B", "C", "D", "E0"):
            tb = latest()
            txr = dma(AC, X, xT, tb)
            junk = sb(PB + 8192, 1024)
            tX = residual(mix, gam1, small[:, 128:132], junk, tmx, txr)
            dump("X1", X)
            tb = latest() + tX
            o = PF
            P = r3(sb(o, 4096), 1024)
            h2 = r3(sb(o + 4096, 4096), 1024)
            yo = r3(sb(o, 8192), 1024); o += 8192
            xg = r3(sb(o, 8192), 1024); o += 8192
            PgT = r3(sb(o, 4096), 512); o += 4096
            hidr = Ring([sb(o + 512 * i, 512) for i in range(2)]); o += 1024
            hidT = r3(sb(o, 2048), 128); o += 2048
            wr_ = sb(o, 128); o += 128
            aff = sb(o, 64); o += 64
            hflat = hidT.rearrange("p a b -> p (a b)")
            wrk, slotT = hflat[:, 0:512], hflat[:, 512:1024]
            slot = sb(o, 64); o += 64
            m8 = sb(o, 8); o += 8
            Pg = r3(xg.rearrange("p a b -> p (a b)")[:, 0:4096], 1024)
            assert o <= 53200, (o)
            th2 = normed_T(X, 4, HT2, PgT.rearrange("p a b -> p (a b)")[:, 0:1024], h2, small[:, 128:132],
                           lambda j: mc[:, 3, j, 0:1], lambda j: mc[:, 2, j, 0:1], tb)
            th3 = []
            tall = latest()
            for i in range(4):
                for hf_ in range(2):
                    b, bank, free = PS.take()
                    for j in range(4):
                        lt = tr(bank[:, j * 128:(j + 1) * 128], HT2[:, hf_ * 4 + j, i * 128:(i + 1) * 128], free, th2, signal=(j == 3))
                    t = copy(evac2(hf_), h2[:, i, hf_ * 512:hf_ * 512 + 512], bank, lt, tall)
                    PS.release(b, t)
                    th3.append(t)
            twr = dma(AC, r3(wr_, 16), A["w_router"].rearrange("(k p) e -> p k e", p=128), tb)
            b, bank, free = PS.take()
            for i in range(4):
                for kt in range(8):
                    lt = mm(bank[:, i * 16:(i + 1) * 16], HT2[:, kt, i * 128:(i + 1) * 128], r3(wr_, 16)[:, kt, :], kt == 0, kt == 7,
                            free, twr, th2, signal=(i == 3 and kt == 7))
            sv = small[:, 144:160]
            t = reduce_(sv[:, 0:4], r3(bank[:, 0:64], 16), ALU.max, lt)
            t = tt(DVE, r3(aff, 16), r3(bank[:, 0:64], 16), bc(sv[:, 0:4], 16), ALU.subtract, t, tb)
            PS.release(b, t)
            t = act(aff, aff, ACT.Exp, t)
            t = reduce_(sv[:, 4:8], r3(aff, 16), ALU.add, t)
            t = recip(sv[:, 4:8], sv[:, 4:8], t)
            taff = tt(DVE, r3(aff, 16), r3(aff, 16), bc(sv[:, 4:8], 16), ALU.mult, t)
            b, bank, free = PS.take()
            for i in range(4):
                lt = tr(bank[0:16, i * 128:(i + 1) * 128], aff[:, i * 16:(i + 1) * 16], free, taff, signal=(i == 3))
            t = copy(DVE, wrk[0:16, :], bank[0:16, :], lt, tb)
            PS.release(b, t)
            for n in range(8):
                t = DVE.op(lambda e: e.max(m8[0:16, :], wrk[0:16, :]), t)
                t = DVE.op(lambda e: e.match_replace(wrk[0:16, :], m8[0:16, :], wrk[0:16, :], -1.0), t)
            t = ts(DVE, wrk[0:16, :], wrk[0:16, :], 0.0, ALU.is_lt, t)
            t = DVE.op(lambda e: e.tensor_tensor_scan(slotT[0:16, :], wrk[0:16, :], wrk[0:16, :], 0.0, ALU.add, ALU.max), t)
            t = tt(DVE, slotT[0:16, :], slotT[0:16, :], wrk[0:16, :], ALU.mult, t)
            t = ts(DVE, slotT[0:16, :], slotT[0:16, :], -1.0, ALU.add, t)
            b, bank, free = PS.take()
            for i in range(4):
                lt = tr(bank[:, i * 16:(i + 1) * 16], slotT[0:16, i * 128:(i + 1) * 128], free, t, signal=(i == 3))
            tsl = copy(DVE, slot, bank[:, 0:64], lt)
            PS.release(b, tsl)
            dump("slot", slot)
            dump("aff", aff)
            tP, tPg = [], []
            for i in range(4):
                p3 = r3(P[:, i, :], 64)
                t = tt(DVE, p3, bc(slot[:, i * 16:(i + 1) * 16], 64), rep(con("iota"), 16), ALU.is_equal, tsl, tall)
                tP.append(t)
                tPg.append(tt(PL, r3(Pg[:, i, :], 64), p3, bc(aff[:, i * 16:(i + 1) * 16], 64), ALU.mult, t))
            tPT = []
            for m in range(8):
                b, bank, free = PS.take()
                for i in range(4):
                    lt = tr(bank[:, i * 128:(i + 1) * 128], Pg[:, i, m * 128:(m + 1) * 128], free, tPg[i], signal=(i == 3))
                t = copy(evac2(m), PgT[:, m, :], bank, lt)
                PS.release(b, t)
                tPT.append(lt)
                tlastPT = t
            tPTall = latest()
            txg = []
            for kt in range(8):
                for hf_ in range(2):
                    b, bank, free = PS.take()
                    for i in range(4):
                        lt = mm(bank, h2[:, i, kt * 128:(kt + 1) * 128], P[:, i, hf_ * 512:hf_ * 512 + 512], i == 0, i == 3, free,
                                tP, th3, signal=(i == 3))
                    t = copy(evac2(hf_), xg[:, kt, hf_ * 512:hf_ * 512 + 512], bank, lt, tPTall)
                    PS.release(b, t)
                    txg.append(t)
            dump("xg", xg)
            tgath = [(PE.sem, PE.count)]
            yot = {}
            prevT = []
            for m in range(8):
                eg = [A["w_exp_gate"][2 * m + j] for j in range(2)]
                eu = [A["w_exp_up"][2 * m + j] for j in range(2)]
                ed = [A["w_exp_down"][2 * m + j] for j in range(2)]
                thT = []
                for s in range(4):
                    res = []
                    for w2 in (eg, eu):
                        b, bank, free = PS.take()
                        for kg in range(2):
                            bl = [wblock(w2[j], kg * 512, 4, s * 512, 512) for j in range(2)]
                            for kk in range(4):
                                kt = kg * 4 + kk
                                for j in range(2):
                                    lt = mm(bank[64 * j:64 * j + 64, :], xg[:, kt, (2 * m + j) * 64:(2 * m + j + 1) * 64],
                                            bl[j][1][:, kk, :], kt == 0, kt == 7, free, bl[j][2], txg,
                                            signal=(kk == 3))
                                    if kk == 3:
                                        W.release(bl[j][0], lt)
                        res.append((b, bank, lt))
                    k, hid, f = hidr.take()
                    t = act(hid, res[0][1], ACT.Silu, res[0][2], f)
                    PS.release(res[0][0], t)
                    t = tt(DVE, hid, hid, res[1][1], ALU.mult, t, res[1][2])
                    PS.release(res[1][0], t)
                    b, bank, free = PS.take()
                    for j in range(4):
                        lt = tr(bank[:, j * 128:(j + 1) * 128], hid[:, j * 128:(j + 1) * 128], free, t, signal=(j == 3))
                    hidr.release(k, lt)
                    e = copy(DVE, hidT[:, s * 4:s * 4 + 4, :], r3(bank, 128), lt, prevT)
                    PS.release(b, e)
                    thT.append(e)
                for n in range(2):
                    b, bank, free = PS.take()
                    for kg in range(4):
                        bl = [wblock(ed[j], kg * 512, 4, n * 512, 512) for j in range(2)]
                        for kk in range(4):
                            kt = kg * 4 + kk
                            for j in range(2):
                                lt = mm(bank[64 * j:64 * j + 64, :], hidT[:, kt, 64 * j:64 * j + 64], bl[j][1][:, kk, :],
                                        kt == 0, kt == 15, free, bl[j][2], thT, signal=(kk == 3))
                                if kk == 3:
                                    W.release(bl[j][0], lt)
                    e = copy(AC, yo[:, m, n * 512:n * 512 + 512], bank, lt, tgath)
                    PS.release(b, e)
                    yot[m] = e
                prevT = [lt]
            dump("yo", yo)
            moe = r3(xg.rearrange("p a b -> p (a b)")[:, 0:4096], 1024)
            tms = []
            tall = [lt, tlastPT]
            for i in range(4):
                for n in range(2):
                    b, bank, free = PS.take()
                    for m in range(8):
                        lt = mm(bank, PgT[:, m, i * 128:(i + 1) * 128], yo[:, m, n * 512:n * 512 + 512], m == 0, m == 7, free,
                                [yot[m_] for m_ in yot], tlastPT, tPTall, signal=(m == 7))
                    t = copy(evac2(n), moe[:, i, n * 512:n * 512 + 512], bank, lt, tall)
                    PS.release(b, t)
                    tms.append(t)
            dump("moe", moe)
            tX = residual(moe, gam2, small[:, 128:132], xg.rearrange("p a b -> p (a b)")[:, 4096:5120], tms, [])
            dump("X2", X)

        if stop not in ("B", "C", "D", "E0", "E", "F"):
            tb = latest() + tX
            o = PF
            tabs = [sb(o + 512 * i, 512) for i in range(4)]; o += 2048
            lamv = sb(o, 16); o += 16
            gd = sb(o, 128); o += 128
            PG = o
            posf = sb(PG, 512)
            angb = [sb(PG + 512 * (i + 1), 512) for i in range(3)]
            posi = sb(PG + 2560, 512).bitcast(I32)
            t = dma(AC, posi, A["positions"].rearrange("a n -> (a n)").partition_broadcast(128), tb)
            t = copy(DVE, posf, posi, t)
            C1 = 6.28125
            rest = 2 * math.pi - C1
            C2 = float(np.float32(round(rest * 2 ** 21) / 2 ** 21))
            C3 = float(np.float32(rest - C2))
            ttab = []
            for n, (inv_, which) in enumerate((("invb", 0), ("invb", 1), ("invd", 0), ("invd", 1))):
                ang, kk_, r_ = angb
                t = ts(DVE, ang, posf, con(inv_), ALU.mult, t)
                t = ts(DVE, kk_, ang, 1.0 / (2 * math.pi), ALU.mult, t, s2=0.25 if which == 0 else 0.0, op1=ALU.add)
                t = ts(DVE, kk_, kk_, MAGIC, ALU.add, t)
                t = ts(DVE, kk_, kk_, MAGIC, ALU.subtract, t)
                t = stt(r_, kk_, -C1, ang, ALU.mult, ALU.add, t)
                t = stt(r_, kk_, -C2, r_, ALU.mult, ALU.add, t)
                t = stt(r_, kk_, -C3, r_, ALU.mult, ALU.add, t)
                if which == 0:
                    t = ts(DVE, r_, r_, math.pi / 2, ALU.add, t)
                t = ts(DVE, r_, r_, 3.1415925, ALU.min, t, s2=-3.1415925, op1=ALU.max)
                t = act(tabs[n], r_, ACT.Sin, t)
                ttab.append(t)
            cosb, sinb, cosd, sind = tabs
            lam4 = sb(PG + 2048, 4 * 64)
            ls = [sem("s_lam"), 0]
            for i, nme in enumerate(("lambda_q1", "lambda_k1", "lambda_q2", "lambda_k2")):
                tl_ = dma(AC, lam4[:, i * 64:(i + 1) * 64], A[nme].rearrange("a n -> (a n)").partition_broadcast(128), tb, s=ls)
            tgd = dma(AC, gd, A["g_diff"].rearrange("a n -> (a n)").partition_broadcast(128), tb)
            prod = lam4
            t = tt(DVE, prod[:, 0:64], lam4[:, 0:64], lam4[:, 64:128], ALU.mult, tl_)
            t = tt(DVE, prod[:, 64:128], lam4[:, 128:192], lam4[:, 192:256], ALU.mult, t)
            t = reduce_(lamv[:, 0:4], r3(prod[:, 0:128], 32), ALU.add, t)
            t = act(lamv[:, 4:8], lamv[:, 0:4], ACT.Exp, t)
            inits = [0.8 - 0.6 * math.exp(-0.3 * l) for l in range(2)]
            t = tt(DVE, lamv[:, 8:10], lamv[:, 6:8], lamv[:, 4:6], ALU.subtract, t)
            tlam = [ts(DVE, lamv[:, 8 + l:9 + l], lamv[:, 8 + l:9 + l], -inits[l], ALU.add, t) for l in range(2)]
            tgs = [ts(DVE, gd[:, 64 * l:64 * l + 64], gd[:, 64 * l:64 * l + 64], 1.0 - inits[l], ALU.mult, tgd) for l in range(2)]

            dump("tabs", sb(PF, 2048))
            for layer in range(2):
                tb = latest() + ttab + tlam + tgs + tX
                o = PG
                qP = r3(sb(o, 6144), 512); o += 6144
                kF = r3(sb(o, 2048), 512); o += 2048
                V = r3(sb(o, 2048), 512); o += 2048
                O = r3(sb(o, 4096), 1024); o += 4096
                Sr = Ring([sb(o + 512 * i, 512) for i in range(6)]); o += 3072
                PTr = Ring([sb(o + 512 * i, 512) for i in range(3)]); o += 1536
                tmp = Ring([tuple(sb(o + 1536 * i + 512 * j, 512) for j in range(3)) for i in range(2)]); o += 3072
                hn = sb(o, 64 * 4); o += 256
                assert o <= 53200, o
                xnb = r3(sb(PG, 4096), 1024)
                HT = HT2
                tH = normed_T(X, 4, HT2, sb(PG + 4096, 1024), xnb, small[:, 128:132],
                              lambda j: gmix2[:, layer * 8 + j:layer * 8 + j + 1], lambda j: None, tb)
                tb = latest()
                tz2 = [zero(DVE, qP.rearrange("p a b -> p (a b)"), tb)]
                tOall = []
                Wi = A["w_in_2"][layer]
                hnr = Ring([hn[:, 64 * i:64 * i + 64] for i in range(4)])

                def vcols(c0, n, d0, dst_wait, blocks, w0, tv_):
                    def ev(i, o_, tok):
                        t = copy(evac2(i), V[:, i, d0:d0 + n], o_, tok, dst_wait)
                        tv_.append(t)
                        return t
                    gemm(blocks, range(4), lambda i, kt, w: HT2[:, kt, i * 128:(i + 1) * 128], lambda i, kt, w: w[:, w0:w0 + n], ev, tH)

                def proj(c0, kind, dest, waits_, toks):
                    blocks = wcols(Wi, 1024, c0, 256)
                    cs2 = (cosd, sind, con("rd")) if kind == "d" else (cosb, sinb, con("rb"))
                    for i in range(2):
                        tds, last = rope(blocks, i, 0, *cs2, dest(i), tmp, [tH, waits_], ttab)
                        toks.append(tds)
                    for x_ in blocks:
                        W.release(x_[0], last)

                def outn(O_, qt, col):
                    def f(ps, lt, sv):
                        t = ts(DVE, O_[:, qt, col:col + 64], ps, sv[:, 1:2], ALU.mult, lt)
                        tOall.append(t)
                        return t
                    return f

                def outd(O_, qt, col):
                    def f(ps, lt, sv):
                        k, hb_, f_ = hnr.take()
                        t0 = copy(DVE, hb_, ps, lt, f_)
                        d = O_[:, qt, col:col + 64]
                        t = act(d, hb_, ACT.Square, t0, acc=sv[:, 0:1])
                        t = ts(DVE, sv[:, 0:1], sv[:, 0:1], 1.0 / 64, ALU.mult, t, s2=EPS, op1=ALU.add)
                        t = act(sv[:, 1:2], sv[:, 0:1], ACT.Ln, t)
                        t = act(sv[:, 1:2], sv[:, 1:2], ACT.Exp, t, scale=-0.5)
                        t = stt(sv[:, 2:3], sv[:, 1:2], sv[:, 0:1], sv[:, 1:2], ALU.mult, ALU.mult, t)
                        t = ts(DVE, sv[:, 2:3], sv[:, 2:3], -0.5, ALU.mult, t, s2=1.5, op1=ALU.add)
                        t = tt(DVE, sv[:, 1:2], sv[:, 1:2], sv[:, 2:3], ALU.mult, t)
                        t = stt(d, hb_, sv[:, 1:2], gd[:, 64 * layer:64 * layer + 64], ALU.mult, ALU.mult, t)
                        hnr.release(k, t)
                        tOall.append(t)
                        return t
                    return f

                tq, tk, tv_ = [], [], []
                proj(0, "d", lambda i: [(32 * c, 32 * c + 32, qP[:, 4 * i + c, :]) for c in range(4)], tz2, tq)
                proj(256, "d", lambda i: [(0, 128, kF[:, i, :])], tb, tk)
                blocks = wcols(Wi, 1024, 512, 256)
                vcols(512, 256, 0, tb, blocks, 0, tv_)
                proj(768, "b", lambda i: [(64 * c, 64 * c + 64, qP[:, 8 + 2 * i + c, :]) for c in range(2)], tz2, tq)
                proj(1024, "b", lambda i: [(0, 128, kF[:, 2 + i, :])], tb, tk)
                blocks = wcols(Wi, 1024, 1280, 256)
                vcols(1280, 256, 256, tb, blocks, 0, tv_)
                units = []
                for h in range(8):
                    for qt in range(4):
                        n = 128 * (qt + 1)
                        bias = lambda qt=qt: (con("causal")[:, 384 - 128 * qt:512], None)
                        qs = slice(qt * 128, qt * 128 + 128)
                        if h < 4:
                            maps = [dict(q=qP[:, 4 * (h // 2) + 2 * (h % 2) + c, qs], keys=[(kF[:, h // 2, 0:n], n, bias)]) for c in range(2)]
                            units.append(dict(maps=maps, scale=32 ** -0.5, out=outd(O, qt, 64 * h), nlam=lamv[:, 8 + layer:9 + layer],
                                              v=lambda j, h=h: V[:, j, 64 * h:64 * h + 64]))
                        else:
                            hb2 = h - 4
                            maps = [dict(q=qP[:, 8 + hb2, qs], keys=[(kF[:, 2 + hb2 // 2, 0:n], n, bias)])]
                            units.append(dict(maps=maps, scale=0.125, out=outn(O, qt, 64 * h),
                                              v=lambda j, h=h: V[:, j, 64 * h:64 * h + 64]))
                attention(units, Sr, PTr, [tq, tk, tv_])
                if layer == 0:
                    dump("kF", kF); dump("V", V); dump("qP", qP); dump("HT2", HT2)
                tb2 = latest()
                tz2 = [zero(DVE, qP[:, 0:8, :].rearrange("p a b -> p (a b)"), tb2)]
                tq, tk, tv_ = [], [], []
                for s in range(2):
                    proj(1536 + 256 * s, "b", lambda i: [(64 * c, 64 * c + 64, qP[:, 4 * s + 2 * i + c, :]) for c in range(2)], tz2, tq)
                for s in range(2):
                    proj(2048 + 256 * s, "b", lambda i: [(0, 128, kF[:, 2 * s + i, :])], tb2, tk)
                blocks = wcols(Wi, 1024, 2560, 512)
                vcols(2560, 512, 0, tb2, blocks, 0, tv_)
                units = []
                for h in range(8):
                    for qt in range(4):
                        n = 128 * (qt + 1)
                        qs = slice(qt * 128, qt * 128 + 128)
                        bias = lambda qt=qt: (con("dilated")[:, 384 - 128 * qt:512], None)
                        maps = [dict(q=qP[:, h, qs], keys=[(kF[:, h // 2, 0:n], n, bias)])]
                        units.append(dict(maps=maps, scale=0.125, out=outn(O, qt, 512 + 64 * h),
                                          v=lambda j, h=h: V[:, j, 64 * h:64 * h + 64]))
                attention(units, Sr, PTr, [tq, tk, tv_])
                tO = latest()
                if layer == 0:
                    dump("O2", O)
                oT = HT2
                toT = []
                for j in range(8):
                    b, bank, free = PS.take()
                    for i in range(4):
                        lt = tr(bank[:, i * 128:(i + 1) * 128], O[:, i, j * 128:(j + 1) * 128], free, tO, signal=(i == 3))
                    t = copy(evac2(j), oT[:, j, :], bank, lt)
                    PS.release(b, t)
                    toT.append(t)
                tX = []
                for half in range(2):
                    blocks = wcols(A["w_out_2"][layer], 1024, 512 * half, 512)

                    def ev(i, o_, tok, half=half):
                        d = X[:, i, half * 512:half * 512 + 512]
                        t = tt(DVE, d, o_, d, ALU.add, tok)
                        tX.append(t)
                        return t
                    gemm(blocks, range(4), lambda i, kt, w: oT[:, kt, i * 128:(i + 1) * 128], lambda i, kt, w: w, ev, toT)
                if layer == 0:
                    dump("X3", X)
                tb = latest() + tX
                o = PG
                actT = r3(sb(o, 11264), 512); o += 11264
                pads = Ring([sb(o + 516 * i, 514) for i in range(4)]); o += 2064
                accs = Ring([sb(o + 512 * i, 512) for i in range(4)]); o += 2048
                xnb = r3(sb(o, 4096), 1024)
                junk = sb(o + 4096, 1024)
                tH = normed_T(X, 4, HT2, junk, xnb, small[:, 128:132],
                              lambda j: gffn2[:, layer * 8 + j:layer * 8 + j + 1], lambda j: None, tb)
                tz = [zero(DVE, p_[:, 0:2], tb) for p_ in pads.bufs]
                Wu = A["w_up_2"][layer]
                tact = []
                for s in range(11):
                    bl = []
                    for kg in range(2):
                        def parts(buf, kg=kg, s=s):
                            d = r3(buf, 512)
                            rr = Wu[kg * 512:kg * 512 + 512, :]
                            return [(d[:, :, 256 * v:256 * v + 256],
                                     rr[:, 2816 * v + 256 * s:2816 * v + 256 * s + 256].rearrange("(k p) n -> p k n", p=128)) for v in range(2)]
                        k, buf, tok = wload(parts)
                        bl.append((k, r3(buf, 512), tok, 4))
                    held = {}

                    def ev(i, o_, tok, s=s, held=held):
                        v, j = i // 2, i % 2
                        ti = 22 * v + 2 * s + j
                        pk, pad, pf = pads.take()
                        c1 = copy(AC, pad[:, 2:514], o_, tok, pf, tz)
                        ak, ac_, af = accs.take()
                        w3 = lambda q_: vcw2[:, layer * 132 + q_ * 44 + ti:layer * 132 + q_ * 44 + ti + 1]
                        t = ts(PL, ac_, pad[:, 0:512], w3(0), ALU.mult, c1, af)
                        t = stt(ac_, pad[:, 1:513], w3(1), ac_, ALU.mult, ALU.add, t)
                        t = stt(ac_, pad[:, 2:514], w3(2), ac_, ALU.mult, ALU.add, t)
                        pads.release(pk, t)
                        bb = vcb[:, 24 + layer * 44 + ti:24 + layer * 44 + ti + 1]
                        if v == 0:
                            t = act(ac_, ac_, ACT.Silu, t, bias=bb)
                            held[j] = (ak, ac_, t)
                        else:
                            gk, ga, gt = held[j]
                            t = stt(actT[:, 2 * s + j, :], ac_, bb, ga, ALU.add, ALU.mult, t, gt, tb)
                            accs.release(ak, t)
                            accs.release(gk, t)
                            tact.append(t)
                        return c1
                    gemm(bl, (0, 1, 2, 3), lambda i, kt, w: w[:, i * 128:(i + 1) * 128], lambda i, kt, w: HT2[:, kt, :], ev, tH)
                tX = []
                for half in range(2):
                    blocks = wcols(A["w_down_2"][layer], 2816, 512 * half, 512)

                    def ev(i, o_, tok, half=half):
                        d = X[:, i, half * 512:half * 512 + 512]
                        t = tt(DVE, d, o_, d, ALU.add, tok)
                        tX.append(t)
                        return t
                    chunked(blocks, range(4), lambda i, kt, w: actT[:, kt, i * 128:(i + 1) * 128], lambda i, kt, w: w, ev, 1, tact)
                if layer == 0:
                    dump("X4", X)
            tb = latest()
            gf = sb(PG, 1024)
            ob = r3(sb(PG + 1024, 4096), 1024)
            tgf = dma(AC, gf, A["g_final"].partition_broadcast(128), tb)
            ssq = small[:, 128:132]
            tq = [act(ob[:, i, :], X[:, i, :], ACT.Square, tX, tb, acc=ssq[:, i:i + 1]) for i in range(4)]
            t = rstd(ssq, 4, tq)
            osem = [sem("s_out"), 0]
            for i in range(4):
                t1 = stt(ob[:, i, :], X[:, i, :], ssq[:, i:i + 1], gf, ALU.mult, ALU.mult, t, tgf)
                tend = dma(SP, out[0, i * 128:(i + 1) * 128, :], ob[:, i, :], t1, s=osem)
            SP.need([tend])
        else:
            SP.need([latest(), tyD])

        SP.need(tdump)
        block = ctx.enter_context(nc.Block())
        block.sync(SP.run)
        block.tensor(PE.run)
        block.vector(DVE.run)
        block.scalar(AC.run)
        block.gpsimd(PL.run)


_INS = ['x', 'c', 'ctx', 'c_ctx', 'w_ada', 'b_ada', 'norm_pre_mix', 'norm_post_mix', 'norm_pre_ffn', 'norm_post_ffn',
        'w_in', 'na_rpb', 'ssd_conv_w', 'ssd_conv_b', 'ssd_a_log_fwd', 'ssd_a_log_bwd', 'ssd_dt_bias_fwd',
        'ssd_dt_bias_bwd', 'ssd_d_skip', 'ssd_norm', 'w_branch_na', 'w_branch_ssd', 'w_out', 'w_router',
        'w_exp_gate', 'w_exp_up', 'w_exp_down', 'positions_2', 'g_mix_2', 'w_in_2', 'w_out_2', 'lambda_q1_2',
        'lambda_k1_2', 'lambda_q2_2', 'lambda_k2_2', 'g_diff_2', 'g_ffn_2', 'w_up_2', 'conv_w_2', 'conv_b_2',
        'w_down_2', 'g_final_2']
_DROP = ['w_ada', 'w_in', 'w_branch_na', 'w_branch_ssd', 'w_out', 'w_router', 'w_exp_gate', 'w_exp_up', 'w_exp_down']
_NAMES = {'positions_2': 'positions', 'lambda_q1_2': 'lambda_q1', 'lambda_k1_2': 'lambda_k1',
          'lambda_q2_2': 'lambda_q2', 'lambda_k2_2': 'lambda_k2', 'g_diff_2': 'g_diff', 'g_final_2': 'g_final'}


def kernel(**inputs):
    import concourse.bacc as _bacc
    from concourse.bass_utils import run_bass_kernel_spmd as _run

    nc = _bacc.Bacc("TRN2", target_bir_lowering=False, num_devices=1)
    arrays, A = {}, {}
    consts, at = shape_constants()
    for name in _INS + ["consts"]:
        a = np.ascontiguousarray(consts if name == "consts" else inputs[name])
        if name in _DROP:
            a = a[0]
        arrays[f"in_{name}_dram"] = a
        A[_NAMES.get(name, name)] = nc.dram_tensor(f"in_{name}_dram", a.shape, mybir.dt.from_np(a.dtype), kind="ExternalInput").ap()
    A["at"] = at
    out = nc.dram_tensor("out_0_dram", (1, 512, 1024), F32, kind="ExternalOutput").ap()
    build(nc, A, out)
    r = _run(nc, [arrays], core_ids=[0])
    return r.results[0]["out_0_dram"]
```

```python
import math

import numpy as np
import concourse.bass as bass
from concourse import mybir
from contextlib import ExitStack

F32 = mybir.dt.float32
I32 = mybir.dt.int32
ALU = mybir.AluOpType
ACT = mybir.ActivationFunctionType
AX = mybir.AxisListType

EPS = 1e-6
NEG = -1e30
MAGIC = 12582912.0
WSLOT = 2048

CQ, CK, CV, CZ, CX, CB, CC, CDT, CGN, CGS = 0, 1024, 2048, 3072, 5120, 7168, 7680, 8192, 8256, 9280


def shape_constants():
    parts, at, n = [], {}, 0

    def put(name, a):
        nonlocal n
        a = np.asarray(a, np.float32)
        at[name] = (n, n + a.shape[1])
        parts.append(a)
        n += a.shape[1]

    def mark(group):
        at[group] = (sum(b - a for g, (a, b) in at.items() if len(g) == 1), n)

    p = np.arange(128)
    put("ident", np.eye(128))
    put("ule", p[:, None] <= p[None, :])
    put("uge", p[:, None] >= p[None, :])
    put("ones", np.ones((128, 128)))
    dist = 384 + p[:, None] - np.arange(512)[None, :]
    mark("a")
    put("causal", np.where(dist >= 0, 0.0, NEG))
    count = (dist >= 0) * ((dist <= 128) * 1.0 + (dist % 4 == 0) + (dist % 16 == 0))
    put("dilated", np.where(count > 0, np.log(np.maximum(count, 1.0)), NEG))
    rna = np.zeros((128, 128))
    rb = np.zeros((128, 128))
    rd = np.zeros((128, 128))
    for f in range(128):
        if f % 32 < 16:
            rna[f, f + 16] = -1
        else:
            rna[f, f - 16] = 1
        if f % 64 < 8:
            rb[f, f + 8] = -1
        elif f % 64 < 16:
            rb[f, f - 8] = 1
        if f % 32 < 4:
            rd[f, f + 4] = -1
        elif f % 32 < 8:
            rd[f, f - 4] = 1
    put("rb", rb.T)
    put("rd", rd.T)
    t = np.arange(512)
    inv = (np.float32(10000.0) ** (-np.arange(16, dtype=np.float32) / np.float32(16))).astype(np.float32)
    pos = np.where(((p % 64) < 32)[:, None], (t // 64)[None, :], (t % 64)[None, :]).astype(np.float32)
    ang = (pos * inv[p % 16][:, None]).astype(np.float32).astype(np.float64)
    ib = np.power(np.float32(500000.0), -np.arange(8, dtype=np.float32) * np.float32(2.0) / np.float32(16))
    idf = np.power(np.float32(500000.0), -np.arange(4, dtype=np.float32) * np.float32(2.0) / np.float32(8))
    put("invb", np.where(p % 64 < 16, ib[p % 8], 0.0)[:, None])
    put("invd", np.where(p % 32 < 8, idf[p % 4], 0.0)[:, None])
    col = np.arange(64)
    mark("g")
    put("rna", rna.T)
    put("nacos", np.cos(ang))
    put("nasin", np.sin(ang))
    cs = np.clip(col - 8, 0, 48)
    ok = (col[None, :] >= cs[:, None]) & (col[None, :] < cs[:, None] + 16)
    put("colmask", np.where(ok[p % 64], 0.0, NEG))
    mark("d")
    put("iota", np.tile(col[None, :], (128, 1)))
    mark("f")
    return np.concatenate(parts, axis=1), at


class Engine:

    def __init__(self, sem):
        self.sem, self.count, self.todo, self.seen = sem, 0, [], {}

    def need(self, waits):
        for t in waits:
            if t is None:
                continue
            if isinstance(t, list):
                self.need(t)
                continue
            sem, v = t
            if self.seen.get(id(sem), 0) < v:
                self.seen[id(sem)] = v
                self.todo.append(lambda e, s=sem, v=v: e.wait_ge(s, v))

    def op(self, make, *waits, signal=True):
        self.need(waits)
        if not signal:
            self.todo.append(make)
            return None
        self.count += 1
        self.todo.append(lambda e: make(e).then_inc(self.sem, 1))
        return (self.sem, self.count)

    def run(self, e):
        for f in self.todo:
            f(e)


class Ring:

    def __init__(self, bufs, keys=None, state=None):
        self.bufs = bufs
        self.keys = keys or list(range(len(bufs)))
        self.state = state if state is not None else [[i - len(bufs), False, []] for i in range(len(bufs))]

    def take(self):
        k = min((k for k in self.keys if not self.state[k][1]), key=lambda k: self.state[k][0])
        waits = self.state[k][2]
        self.state[k][1:] = [True, []]
        return k, self.bufs[k], waits

    def release(self, k, *toks):
        s = self.state[k]
        s[0], s[1], s[2] = max(x[0] for x in self.state) + 1, False, s[2] + list(toks)


def weave(main, filler, per):
    owed = 0.0
    for _ in main:
        owed += per
        while owed >= 1.0:
            owed -= 1.0
            next(filler, None)
    for _ in filler:
        pass


def run(steps):
    for _ in steps:
        pass


def build(nc, A, out, dumps=None, stop=None):
    dumps = dumps or {}
    ctx = ExitStack()
    with ctx:
        arena = ctx.enter_context(nc.sbuf_tensor("arena", [128, 53200], F32))
        psum = ctx.enter_context(nc.psum_tensor("psum", [128, 4096], F32))
        nsem = [0]

        def sem(name=None):
            nsem[0] += 1
            return ctx.enter_context(nc.semaphore(name or f"s{nsem[0]}"))

        PE, DVE, AC, PL, SP = (Engine(sem("s_" + n)) for n in ("pe", "dve", "act", "pool", "sp"))
        ENG = [PE, DVE, AC, PL]

        def sb(a, n):
            return arena[:, a:a + n]

        def r3(ap, n):
            return ap.rearrange("p (a b) -> p a b", b=n)

        top = [0]

        def place(n):
            a = top[0]
            top[0] += n
            assert top[0] <= 53200, top[0]
            return sb(a, n)

        at = A["at"]
        cplace = {}

        def con_load(group, ap):
            a, b = at[group]
            for name, (x0, x1) in at.items():
                if len(name) > 1 and a <= x0 and x1 <= b:
                    cplace[name] = ap[:, x0 - a:x1 - a]
            return A["consts"][:, a:b]

        def con(name):
            return cplace[name]

        NA_ = at["a"][1]
        consts = place(NA_)
        csrc = con_load("a", consts)
        ident, ones = con("ident"), con("ones")
        NW = 5
        WR = place(NW * WSLOT)
        cvT = place(16)
        vecs = place(128 + 120 + 112 + 3 * 88)
        vmain, vcw, vcb = vecs[:, 0:128], vecs[:, 128:248], vecs[:, 248:360]
        vcw2 = vecs[:, 360:624]
        modc = place(64)
        small = place(256)
        BASE = top[0]

        banks = [psum[:, 512 * i:512 * i + 512] for i in range(8)]
        PALL = Ring(banks)
        PA = Ring(banks, [3, 4, 5, 6, 7], PALL.state)
        PG_ = Ring(banks, [0, 1, 2], PALL.state)
        cur = [PALL]

        class PS:
            take = staticmethod(lambda: cur[0].take())
            release = staticmethod(lambda k, *t: cur[0].release(k, *t))

        def using(ring, steps):
            it = iter(steps)
            while True:
                old, cur[0] = cur[0], ring
                try:
                    next(it)
                except StopIteration:
                    return
                finally:
                    cur[0] = old
                yield

        wslots = [WR[:, i * WSLOT:(i + 1) * WSLOT] for i in range(NW)]
        wsems = [sem(f"s_w{i}") for i in range(8)]
        wcount = [0] * 8
        W = Ring(wslots)

        def mm(o, l, r, start, stop_, *waits, signal=False):
            return PE.op(lambda e: e.matmul(o, l, r, start=start, stop=stop_), *waits, signal=signal)

        def tr(o, i, *waits, signal=False):
            k = i.shape[0]
            return PE.op(lambda e: e.transpose(o, i, ident[0:k, 0:k]), *waits, signal=signal)

        def dma(eng, o, i, *waits, s=None):
            if s is None:
                s = [sem(), 0]
            s[1] += 16
            eng.need(waits)
            eng.todo.append(lambda e: e.dma_start(o, i).then_inc(s[0], 16))
            return (s[0], s[1])

        def tt(E, o, a, b, op, *waits):
            return E.op(lambda e: e.tensor_tensor(o, a, b, op), *waits)

        def ts(E, o, a, s1, op0, *waits, s2=None, op1=None):
            if op1 is None:
                return E.op(lambda e: e.tensor_scalar(o, a, s1, None, op0), *waits)
            return E.op(lambda e: e.tensor_scalar(o, a, s1, s2, op0, op1), *waits)

        def stt(o, a, s, b, op0, op1, *waits):
            return DVE.op(lambda e: e.scalar_tensor_tensor(out=o, in0=a, scalar=s, in1=b, op0=op0, op1=op1), *waits)

        def act(o, i, f, *waits, bias=0.0, scale=1.0, acc=None):
            if acc is not None:
                return AC.op(lambda e: e.activation(o, i, f, bias=bias, scale=scale, accum_out=acc), *waits)
            return AC.op(lambda e: e.activation(o, i, f, bias=bias, scale=scale), *waits)

        def copy(E, o, i, *waits):
            if E is AC:
                return act(o, i, ACT.Copy, *waits)
            return E.op(lambda e: e.tensor_copy(o, i), *waits)

        def zero(E, o, *waits):
            return E.op(lambda e: e.memset(o, 0.0), *waits)

        def recip(o, i, *waits):
            return DVE.op(lambda e: e.reciprocal(o, i), *waits)

        def reduce_(o, i, op, *waits, negate=None):
            return DVE.op(lambda e: e.tensor_reduce(o, i, AX.X, op, negate=negate), *waits)

        def latest():
            return [(E.sem, E.count) for E in ENG]

        def bc(ap, n):
            return ap.unsqueeze(2).to_broadcast([ap.shape[0], ap.shape[1], n])

        def rep(ap, n):
            return ap.unsqueeze(1).to_broadcast([ap.shape[0], n, ap.shape[1]])

        def wload(parts, *waits):
            k, buf, w = W.take()
            SP.need([w, list(waits)])
            for dst, src in parts(buf):
                wcount[k] += 16
                SP.todo.append(lambda e, d=dst, s=src, k=k: e.dma_start(d, s).then_inc(wsems[k], 16))
            return k, buf, (wsems[k], wcount[k])

        def wblock(src, r0, nk, c0, n):
            def parts(buf):
                d = r3(buf[:, 0:nk * n], n)
                return [(d, src[r0:r0 + 128 * nk, c0:c0 + n].rearrange("(k p) n -> p k n", p=128))]
            k, buf, tok = wload(parts)
            return k, r3(buf[:, 0:nk * n], n), tok, nk

        def wcols(src, rows, c0, n):
            nk = rows // 128
            return [wblock(src, r0 * 128, min(4, nk - r0), c0, n) for r0 in range(0, nk, 4)]

        def wcols_later(src, rows, c0, n):
            nk = rows // 128
            return [(src, r0 * 128, min(4, nk - r0), c0, n) for r0 in range(0, nk, 4)]

        def gemm_steps(blocks, outs, stat, mov, evac, *waits):
            nkt = sum(x[3] for x in blocks)
            for n, i in enumerate(outs):
                b, bank, free = PS.take()
                kt = 0
                for k, w, tok, nk in blocks:
                    for j in range(nk):
                        o, l, r = shape_mm(bank, stat(i, kt, w[:, j, :]), mov(i, kt, w[:, j, :]))
                        last = mm(o, l, r, kt == 0, kt == nkt - 1, free, tok, list(waits),
                                  signal=(kt == nkt - 1 or (n == len(outs) - 1 and j == nk - 1)))
                        kt += 1
                    if n == len(outs) - 1:
                        W.release(k, last)
                PS.release(b, evac(i, o, last))
                yield

        def gemm(*a):
            run(gemm_steps(*a))

        def shape_mm(bank, l, r):
            m = l.shape[1]
            n = 1
            for d in r.shape[1:]:
                n *= d
            return bank[0:m, 0:n], l, r

        def chunked(blocks, outs, stat, mov, evac, per, *waits):
            opened = {}
            nkt = sum(x[2] for x in blocks)
            kt0 = 0
            for g in range(0, len(blocks), per):
                part = [wblock(*x) for x in blocks[g:g + per]]
                nk_part = sum(x[3] for x in part)
                for n, i in enumerate(outs):
                    if i not in opened:
                        opened[i] = PS.take()
                    b, bank, free = opened[i]
                    kt = kt0
                    for k, w, tok, nk in part:
                        for j in range(nk):
                            o, l, r = shape_mm(bank, stat(i, kt, w[:, j, :]), mov(i, kt, w[:, j, :]))
                            fin = kt == nkt - 1
                            last = mm(o, l, r, kt == 0, fin, free, tok, list(waits),
                                      signal=fin or (n == len(outs) - 1 and j == nk - 1))
                            kt += 1
                        if n == len(outs) - 1:
                            W.release(k, last)
                    if kt == nkt:
                        PS.release(b, evac(i, o, last))
                kt0 += nk_part

        def evac2(n):
            return AC if n % 2 else DVE

        tmods = []

        def rstd(v, n, *waits, mean=1024.0):
            s = small[:, 0:n]
            s2 = small[:, 64:64 + n]
            t = ts(DVE, v, v, 1.0 / mean, ALU.mult, list(waits), s2=EPS, op1=ALU.add)
            t = act(s, v, ACT.Ln, t)
            t = act(s, s, ACT.Exp, t, scale=-0.5)
            t = tt(DVE, s2, s, v, ALU.mult, t)
            t = tt(DVE, s2, s2, s, ALU.mult, t)
            t = ts(DVE, s2, s2, -0.5, ALU.mult, t, s2=1.5, op1=ALU.add)
            return tt(DVE, v, s, s2, ALU.mult, t)

        def normed_rows(src, nt, junk, xn, ssq, *waits):
            tq = list(waits)
            for i in range(nt):
                tq = [act(junk[:, 0:1024], src[:, i, :], ACT.Square, tq, acc=ssq[:, i:i + 1])]
            t = rstd(ssq[:, 0:nt], nt, tq)
            return [ts(DVE if i % 2 else PL, xn[:, i, :], src[:, i, :], ssq[:, i:i + 1], ALU.mult, t) for i in range(nt)]

        def turned(nt, HTd, xn, tx, scale_of, shift_of):
            done = []
            for j in range(8):
                b, bank, free = PS.take()
                for i in range(nt):
                    last = tr(bank[:, i * 128:(i + 1) * 128], xn[:, i, j * 128:(j + 1) * 128], free, tx[i],
                              signal=(i == nt - 1))
                s1, s2 = scale_of(j), shift_of(j)
                if j % 2:
                    if s2 is None:
                        t = act(HTd[:, j, :], bank[:, 0:nt * 128], ACT.Copy, last, tmods, scale=s1)
                    else:
                        t = act(HTd[:, j, :], bank[:, 0:nt * 128], ACT.Identity, last, tmods, scale=s1, bias=s2)
                elif s2 is None:
                    t = ts(DVE, HTd[:, j, :], bank[:, 0:nt * 128], s1, ALU.mult, last)
                else:
                    t = ts(DVE, HTd[:, j, :], bank[:, 0:nt * 128], s1, ALU.mult, last, tmods, s2=s2, op1=ALU.add)
                PS.release(b, t)
                done.append(t)
            return done

        def normed_T(src, nt, HTd, junk, xn, ssq, scale_of, shift_of, *waits):
            return turned(nt, HTd, xn, normed_rows(src, nt, junk, xn, ssq, *waits), scale_of, shift_of)

        xT = A["x"].rearrange("a (t p) d -> p (a t) d", p=128)
        HT = r3(sb(BASE, 6144), 768)
        PB = BASE + 6144
        cvb = sb(PB, 1024)
        S0 = PB + 1024
        xin = r3(sb(S0, 4096), 1024)
        cin = r3(sb(S0 + 4096, 2048), 1024)
        xn = r3(sb(S0 + 6144, 6144), 1024)
        junk = sb(S0 + 12288, 1024)
        stage = sb(S0 + 13312, 6 * 128)
        setup = [dma(SP, consts, csrc)]
        z0 = zero(PL, stage)
        tx = dma(AC, xin, xT)
        tc_ = dma(AC, cin, A["ctx"].rearrange("a (t p) d -> p (a t) d", p=128))
        dsem = [sem("s_vec"), 0]
        rows = 0

        def vec(col, r, ap, n):
            return dma(AC, stage[r:r + n, col * 128:(col + 1) * 128], ap, z0, s=dsem)

        one = lambda ap: ap.rearrange("a (n p) -> (a n) p", p=128)
        vl = [
            (0, 0, one(A["b_ada"]), 48), (0, 48, one(A["norm_pre_mix"]), 8), (0, 56, one(A["norm_pre_ffn"]), 8),
            (0, 64, one(A["ssd_norm"]), 16), (0, 80, one(A["g_mix_2"]), 16), (0, 96, one(A["g_ffn_2"]), 16),
            (0, 112, one(A["c"]), 8), (0, 120, A["c_ctx"].rearrange("(n p) -> n p", p=128), 8),
            (1, 0, A["ssd_conv_w"].rearrange("a j (n p) -> (a j n) p", p=128), 120),
            (2, 0, one(A["ssd_conv_b"]), 24), (2, 24, one(A["conv_b_2"]), 88),
        ]
        cw2 = A["conv_w_2"].rearrange("a j (n p) -> (a j n) p", p=128)
        for i in range(3):
            vl.append((3 + i, 0, cw2[88 * i:88 * i + 88, :], 88))
        for col, r, ap, n in vl:
            tv = vec(col, r, ap, n)
        dst = [(vmain, 128), (vcw, 120), (vcb, 112)] + [(vcw2[:, 88 * i:88 * i + 88], 88) for i in range(3)]
        tvec = []
        for i, (d, n) in enumerate(dst):
            b, bank, free = PS.take()
            t = tr(bank[:, 0:128], stage[:, i * 128:(i + 1) * 128], free, tv, setup, signal=True)
            t = copy(DVE, d, bank[:, 0:n], t)
            PS.release(b, t)
            tvec.append(t)
        bada = vmain[:, 0:48]
        gpm, gpf, gssd = vmain[:, 48:56], vmain[:, 56:64], vmain[:, 64:80]
        gmix2, gffn2 = vmain[:, 80:96], vmain[:, 96:112]
        cv3 = r3(cvT, 2)
        t1 = act(cv3[:, :, 0], vmain[:, 112:120], ACT.Silu, tvec[0])
        t2 = act(cv3[:, :, 1], vmain[:, 120:128], ACT.Silu, tvec[0])
        tcb = copy(DVE, r3(cvb, 128), bc(cv3[:, :, 0], 128), t1)

        ssq = small[:, 128:144]
        txn = normed_rows(xin, 4, junk, xn, ssq[:, 0:4], tx)
        tcn = normed_rows(cin, 2, junk, xn[:, 4:6, :], ssq[:, 4:6], tc_, txn)

        def ada_cols(ci, chunk):
            for half in range(2):
                blocks = wcols(A["w_ada"], 1024, chunk * 1024 + half * 512, 512)

                def ev(i, o, tok, half=half):
                    j = half * 4 + i
                    d = modc[:, ci * 16 + j * 2:ci * 16 + j * 2 + 2]
                    return ts(DVE, d, o, bada[:, chunk * 8 + j:chunk * 8 + j + 1], ALU.add, tok)
                gemm(blocks, range(4), lambda i, kt, w: w[:, i * 128:(i + 1) * 128], lambda i, kt, w: cv3[:, kt, :], ev, t2)
                yield

        gamD = nc.dram_tensor("gam_scratch", [2, 1024], F32, kind="Internal").ap()
        bc1 = lambda ap: ap.rearrange("a n -> (a n)").partition_broadcast(128)
        cvb3 = r3(cvb, 128)
        tgam = []

        def ada_rows(ring):
            gs = [sem("s_grow"), 0]
            for gi, (chunk, nrm) in enumerate(((2, A["norm_post_mix"]), (5, A["norm_post_ffn"]))):
                for half in range(2):
                    c0 = chunk * 1024 + half * 512
                    blocks = wcols(A["w_ada"], 1024, c0, 512)
                    k1, r1, f1 = ring.take()
                    k2, r2, f2 = ring.take()
                    dma(AC, r1, bc1(A["b_ada"][:, c0:c0 + 512]), f1, s=gs)
                    tl = dma(AC, r2, bc1(nrm[:, half * 512:half * 512 + 512]), f2, s=gs)

                    def ev(i, o, tok, r1=r1, r2=r2, gi=gi, half=half):
                        t = tt(DVE, r1, o, r1, ALU.add, tok, tl)
                        t = tt(DVE, r1, r1, r2, ALU.mult, t)
                        tgam.append(dma(AC, gamD[gi:gi + 1, half * 512:half * 512 + 512], r1[0:1, :], t))
                        return t
                    gemm(blocks, [0], lambda i, kt, w: cvb3[:, kt, :], lambda i, kt, w: w, ev, tcb)
                    ring.release(k1, tgam[-1])
                    ring.release(k2, tgam[-1])
                    yield

        mc = modc.rearrange("p (c j w) -> p c j w", c=4, w=2)

        def ada_scale(ci, g):
            t0 = (DVE.sem, DVE.count)
            return [stt(mc[:, ci, :, w_], mc[:, ci, :, w_], 1.0, g, ALU.add, ALU.mult, t0) for w_ in range(2)]

        run(ada_cols(0, 0))
        run(ada_cols(1, 1))
        tmods += ada_scale(1, gpm)

        def ada_rest(ring):
            yield from ada_cols(2, 3)
            yield from ada_cols(3, 4)
            ada_scale(3, gpf)
            yield from ada_rows(ring)

        tH = turned(4, HT[:, :, 0:512], xn, txn, lambda j: mc[:, 1, j, 0:1], lambda j: mc[:, 0, j, 0:1])
        tH += turned(2, HT[:, :, 512:768], xn[:, 4:6, :], tcn, lambda j: mc[:, 1, j, 1:2], lambda j: mc[:, 0, j, 1:2])
        tdump = []
        tyD = []

        def dump(name, ap, *waits):
            if name in dumps:
                tdump.append(dma(SP, dumps[name], ap, latest(), list(waits)))
                for E in ENG:
                    E.need([tdump[-1]])

        dump("HT", HT)

        def dram(name, shape):
            return nc.dram_tensor(name, shape, F32, kind="Internal").ap()

        if stop != "B":
            yD = dram("yT_scratch", [128, 16, 512])
            acsD = dram("acs_scratch", [64, 512])
            tb = latest()
            o = S0

            def bufs(n, w):
                nonlocal o
                r = [sb(o + w * i, w) for i in range(n)]
                o += n * w
                return r

            BF = r3(bufs(1, 3072)[0], 768)
            CF = r3(bufs(1, 2048)[0], 512)
            BT2 = [r3(x_, 128) for x_ in bufs(2, 768)]
            pads = Ring(bufs(2, 776))
            accs = Ring(bufs(1, 772))
            xsF = Ring(bufs(1, 768) + [cvb[:, 0:768]])
            xs2 = [r3(x_, 512) for x_ in bufs(2, 3072)]
            hf, hb = (r3(x_, 512) for x_ in bufs(2, 2048))
            zs2 = [r3(x_, 512) for x_ in bufs(2, 2048)]
            yTr = Ring(bufs(1, 512))
            RBr = Ring(bufs(2, 512))
            Er = Ring(bufs(4, 512))
            XD = Ring(bufs(4, 512))
            TY = Ring(bufs(3, 512))
            cbr = Ring(bufs(2, 256))
            dt, acs, eac, wst, cdec = bufs(5, 384)
            rows64 = bufs(1, 160)[0]
            assert o <= 53200, o
            d1, atot = XD.bufs[0][:, 0:384], XD.bufs[1][:, 0:384]
            tz = []
            for p_ in pads.bufs:
                for a, b in ((0, 2), (514, 518), (774, 776)):
                    tz.append(zero(DVE, p_[:, a:b], tb))
            dtb, nA, dsk = rows64[:, 0:64], rows64[:, 64:128], rows64[:, 128:160]
            rs = [sem("s_rows"), 0]
            for d, ap in ((dtb[:, 0:32], A["ssd_dt_bias_fwd"]), (dtb[:, 32:64], A["ssd_dt_bias_bwd"]),
                          (nA[:, 0:32], A["ssd_a_log_fwd"]), (nA[:, 32:64], A["ssd_a_log_bwd"]), (dsk, A["ssd_d_skip"])):
                tr_ = dma(AC, d, bc1(ap), tb, s=rs)
            ac3 = r3(acs, 64)
            T = {}

            def steps_dt():
                t = act(nA, nA, ACT.Exp, tr_)
                tnA = ts(DVE, nA, nA, -1.0, ALU.mult, t)
                blk = wblock(A["w_in"], 0, 8, CDT, 64)
                b, bank, free = PS.take()
                for i in range(6):
                    for kt in range(8):
                        last = mm(bank[:, i * 64:(i + 1) * 64], HT[:, kt, i * 128:(i + 1) * 128], blk[1][:, kt, :],
                                  kt == 0, kt == 7, free, blk[2], tH, signal=(i == 5 and kt == 7))
                W.release(blk[0], last)
                raw = dt
                t = tt(DVE, r3(raw, 64), r3(bank[:, 0:384], 64), rep(dtb, 6), ALU.add, last, tr_, tb)
                PS.release(b, t)
                yield
                t = stt(d1, raw, -1.0, raw, ALU.mult, ALU.max, t)
                t = act(acs, d1, ACT.Exp, t, scale=-1.0)
                t = ts(DVE, d1, acs, 1.0, ALU.add, t)
                tl = act(eac, d1, ACT.Ln, t)
                t = ts(DVE, atot, d1, -1.0, ALU.add, t)
                t = tt(DVE, acs, acs, atot, ALU.subtract, t)
                t = recip(d1, d1, t, tl)
                t = tt(DVE, acs, acs, d1, ALU.mult, t)
                t = tt(DVE, acs, acs, eac, ALU.add, t, tl)
                T["dt"] = stt(dt, raw, 0.0, acs, ALU.max, ALU.add, t)
                a_ = d1
                ta_ = tt(DVE, r3(a_, 64), r3(dt, 64), rep(nA, 6), ALU.mult, T["dt"], tnA)
                a3 = r3(a_, 64)
                yield
                b, bank, free = PS.take()
                mm(bank[:, 0:192], con("ule"), a3[:, :, 0:32], True, True, free, ta_)
                last = mm(bank[:, 192:384], con("uge"), a3[:, :, 32:64], True, True, signal=True)
                t = copy(DVE, ac3[:, :, 0:32], r3(bank[:, 0:192], 32), last)
                tac = T["ac"] = copy(DVE, ac3[:, :, 32:64], r3(bank[:, 192:384], 32), last)
                PS.release(b, tac)
                b, bank, free = PS.take()
                last = mm(bank[:, 0:384], ones, a_, True, True, free, signal=True)
                tat = copy(DVE, atot, bank[:, 0:384], last)
                PS.release(b, tat)
                T["cd"] = act(cdec, atot, ACT.Exp, tat)
                XD.release(1, T["cd"])
                T["ea"] = act(eac, acs, ACT.Exp, tac)
                t = tt(DVE, wst, atot, acs, ALU.subtract, tat, tac)
                t = act(wst, wst, ACT.Exp, t)
                T["ws"] = tt(DVE, wst, wst, dt, ALU.mult, t)
                yield
                acT = TY.bufs[0][0:64, :]
                b, bank, free = PS.take()
                for i in range(4):
                    last = tr(bank[0:64, i * 128:(i + 1) * 128], ac3[:, i, :], free, tac, signal=(i == 3))
                t = copy(DVE, acT, bank[0:64, 0:512], last)
                PS.release(b, t)
                T["acD"] = dma(AC, acsD, acT, t)
                TY.release(0, T["acD"])

            def conv_tile(blocks, i, ti, dx, dc, *dwaits):
                b1, k1, f1 = PS.take()
                for kt in range(8):
                    blk = blocks[kt // 4]
                    last1 = mm(k1[:, 0:512], blk[1][:, kt % 4, i * 128:(i + 1) * 128], HT[:, kt, 0:512],
                               kt == 0, kt == 7, f1, blk[2], tH, signal=(kt == 7))
                b2, k2, f2 = PS.take()
                for kt in range(8):
                    blk = blocks[kt // 4]
                    last2 = mm(k2[:, 0:256], blk[1][:, kt % 4, i * 128:(i + 1) * 128], HT[:, kt, 512:768],
                               kt == 0, kt == 7, f2, signal=(kt == 7))
                pk, pad, pf = pads.take()
                c1 = copy(AC, pad[:, 2:514], k1[:, 0:512], last1, pf, tz)
                c2 = copy(AC, pad[:, 518:774], k2[:, 0:256], last2)
                PS.release(b1, c1)
                PS.release(b2, c2)
                ak, ac_, af = accs.take()
                w5 = lambda j: vcw[:, j * 24 + ti:j * 24 + ti + 1]
                t = ts(DVE, ac_, pad[:, 0:772], w5(0), ALU.mult, c1, c2, af)
                for j in range(1, 5):
                    t = stt(ac_, pad[:, j:j + 772], w5(j), ac_, ALU.mult, ALU.add, t)
                pads.release(pk, t)
                bias = vcb[:, ti:ti + 1]
                s1 = act(dx, ac_[:, 0:512], ACT.Silu, t, list(dwaits), bias=bias)
                s2 = s1
                if dc is not None:
                    s2 = act(dc, ac_[:, 516:772], ACT.Silu, bias=bias)
                accs.release(ak, s2)
                return s2, last2

            def steps_bc():
                for name, c0, t0_ in (("BF", CB, 16), ("CF", CC, 20)):
                    blocks = wcols(A["w_in"], 1024, c0, 512)
                    T[name] = []
                    for g in range(4):
                        F_ = BF if name == "BF" else CF
                        t, last = conv_tile(blocks, g, t0_ + g, F_[:, g, 0:512], BF[:, g, 512:768] if name == "BF" else None, tb)
                        T[name].append(t)
                        if g < 3:
                            yield
                    for x_ in blocks:
                        W.release(x_[0], last)
                    yield

            done = {}
            gone = {}

            def steps_proj(g):
                xsT, zs, BT = xs2[g % 2], zs2[g % 2], BT2[g % 2]
                before = gone.get(g - 2, tb)
                blocks = wcols(A["w_in"], 1024, CX + 512 * g, 512)
                txs = T["xs", g] = []

                def turn_x(i, k, xf, t):
                    for part, n in ((0, 4), (4, 2)):
                        b, bank, free = PS.take()
                        for c in range(n):
                            lt = tr(bank[:, c * 128:(c + 1) * 128], xf[:, (part + c) * 128:(part + c + 1) * 128], free, t,
                                    signal=(c == n - 1))
                        e = copy(AC if part else DVE, xsT[:, part:part + n, i * 128:(i + 1) * 128], r3(bank[:, 0:n * 128], 128), lt, before)
                        PS.release(b, e)
                        txs.append(e)
                    xsF.release(k, lt)

                late = None
                for i in range(4):
                    k, xf, f = xsF.take()
                    t, last = conv_tile(blocks, i, 4 * g + i, xf[:, 0:512], xf[:, 512:768], f)
                    if i == 3:
                        for x_ in blocks:
                            W.release(x_[0], last)
                    if late:
                        turn_x(*late)
                    late = (i, k, xf, t)
                    yield
                tbt = T["bt", g] = []
                for part, n in ((0, 4), (4, 2)):
                    b, bank, free = PS.take()
                    for c in range(n):
                        lt = tr(bank[:, c * 128:(c + 1) * 128], BF[:, g, (part + c) * 128:(part + c + 1) * 128], free,
                                T["BF"][g], signal=(c == n - 1))
                    e = copy(DVE, BT[:, part:part + n, :], r3(bank[:, 0:n * 128], 128), lt, before)
                    PS.release(b, e)
                    tbt.append(e)
                blocks = wcols(A["w_in"], 1024, CZ + 512 * g, 512)
                tzs = T["zs", g] = []

                def ev(i, o_, tok):
                    t = act(zs[:, i, :], o_, ACT.Silu, tok, before, done.get(g - 2))
                    tzs.append(t)
                    if i == 1:
                        turn_x(*late)
                    return t
                yield from gemm_steps(blocks, range(4), lambda i, kt, w: HT[:, kt, i * 128:(i + 1) * 128], lambda i, kt, w: w, ev, tH)

            rbs = [[sem(f"s_rb{i}"), 0] for i in range(2)]
            ysem = [[sem(f"s_yD{i}"), 0] for i in range(1)]

            def steps_chunks(g):
                xsT, zs, BT = xs2[g % 2], zs2[g % 2], BT2[g % 2]
                txs, tbt, tzs = T["xs", g], T["bt", g], T["zs", g]
                before = gone.get(g - 1, tb)
                items = [(c, hq, d) for c in range(4) for hq in range(2) for d in range(2)]
                loaded = []

                def load_rows():
                    n = len(loaded)
                    if n < len(items):
                        c, hq, d = items[n]
                        h0 = 8 * g + 4 * hq
                        rk, rb, rf = RBr.take()
                        srcr = acsD[32 * d + h0:32 * d + h0 + 4, c * 128:(c + 1) * 128]
                        td = dma(AC, r3(rb, 128), srcr.partition_broadcast(128), rf, T["acD"], s=rbs[rk])
                        loaded.append((rk, rb, td))
                for _ in range(2):
                    load_rows()

                sweep = [(d, n, ((4, 5, 0, 1, 2), (5, 4, 3, 2, 1))[d][n]) for n in range(5) for d in range(2)]
                ahead = []

                def weigh():
                    m_ = len(ahead)
                    if m_ < len(sweep):
                        d, n, c = sweep[m_]
                        k, xd, f = XD.take()
                        wv = r3(wst, 64)[:, c, 32 * d + 8 * g:32 * d + 8 * g + 8]
                        ahead.append((k, xd, tt(PL if m_ % 2 else DVE, r3(xd, 64), r3(xsT[:, c, :], 64), bc(wv, 64), ALU.mult,
                                                f, txs, T["ws"])))
                for _ in range(3):
                    weigh()
                tst = [None, None]
                for m_, (d, n, c) in enumerate(sweep):
                    weigh()
                    H_ = (hf, hb)[d]
                    slots = ((0, 0, 1, 2, 3), (3, 3, 2, 1, 0))[d]
                    k, xd, tx_ = ahead[m_]
                    b, bank, free = PS.take()
                    lt = mm(bank, BT[:, c, :], xd, True, True, free, tbt, tx_, signal=True)
                    XD.release(k, lt)
                    dstn = H_[:, slots[n], :]
                    if n == 0:
                        t = copy(DVE, dstn, bank, lt, before)
                    else:
                        srcn = H_[:, slots[n - 1], :]
                        cd = bc(r3(cdec, 64)[:, c, 32 * d + 8 * g:32 * d + 8 * g + 8], 64)
                        t = tt(DVE, r3(dstn, 64), r3(srcn, 64), cd, ALU.mult, tst[d], T["cd"])
                        t = tt(DVE, dstn, dstn, bank, ALU.add, t, lt)
                    tst[d] = t
                    PS.release(b, t)
                    if d:
                        if n == 0 and g:
                            scale_z(g - 1)
                        if n == 2 and g:
                            finish(g - 1)
                        yield
                th_ = tst

                st = {}
                ssy = small[:, 160:164]
                tus = []

                def first(n):
                    c, hq, _ = items[2 * n]
                    cs_ = slice(c * 128, (c + 1) * 128)
                    if hq == 0:
                        b, bank, free = PS.take()
                        lt = mm(bank[:, 0:128], BF[:, g, cs_], CF[:, g, cs_], True, True, free, T["BF"][g], T["CF"][g], signal=True)
                        ck, cb, cf = cbr.take()
                        t1_ = tt(DVE, cb[:, 0:128], bank[:, 0:128], con("ule"), ALU.mult, lt, cf)
                        t2_ = tt(DVE, cb[:, 128:256], bank[:, 0:128], con("uge"), ALU.mult, lt)
                        PS.release(b, t2_)
                        xd2 = []
                        for d in range(2):
                            k, xd, f = XD.take()
                            dv = r3(dt, 64)[:, c, 32 * d + 8 * g:32 * d + 8 * g + 8]
                            t = tt(PL, r3(xd, 64), r3(xsT[:, c, :], 64), bc(dv, 64), ALU.mult, f, txs, T["dt"])
                            xd2.append((k, xd, t))
                        st[c] = dict(cb=(ck, cb, [t1_, t2_]), xd=xd2)
                    M = []
                    for d in range(2):
                        h0 = 8 * g + 4 * hq
                        rk, rb, td = loaded[2 * n + d]
                        for h in range(4):
                            colv = ac3[:, c, 32 * d + h0 + h:32 * d + h0 + h + 1]
                            r_ = rb[:, h * 128:(h + 1) * 128]
                            t = ts(DVE, r_, r_, colv, ALU.subtract, td, T["ac"], s2=0.0, op1=ALU.min)
                        ek, eb, ef = Er.take()
                        t = act(eb, rb, ACT.Exp, t, ef)
                        RBr.release(rk, t)
                        load_rows()
                        cbd = st[c]["cb"][1][:, 128 * d:128 * d + 128]
                        tm = tt(PL, r3(eb, 128), r3(eb, 128), rep(cbd, 4), ALU.mult, t, st[c]["cb"][2])
                        M.append((ek, r3(eb, 128), tm))
                    if hq == 1:
                        cbr.release(st[c]["cb"][0], tm)
                    st[c, hq] = M

                def second(n):
                    c, hq, _ = items[2 * n]
                    cs_ = slice(c * 128, (c + 1) * 128)
                    M, xd2 = st[c, hq], st[c]["xd"]
                    if hq == 0:
                        st[c]["y"] = PS.take()
                    yb, ybank, yfree = st[c]["y"]
                    for h in range(4):
                        hh = 4 * hq + h
                        for d in range(2):
                            ek, eb, tm = M[d]
                            lt = mm(ybank[:, hh * 64:hh * 64 + 64], eb[:, h, :], xd2[d][1][:, hh * 64:hh * 64 + 64],
                                    d == 0, d == 1, yfree, tm, xd2[d][2], signal=(h == 3 and d == 1))
                    for d in range(2):
                        Er.release(M[d][0], lt)
                    if hq == 0:
                        return
                    for k, _, _ in xd2:
                        XD.release(k, lt)
                    tyd = lt
                    ty = []
                    for d, H_ in ((0, hf), (1, hb)):
                        b, bank, free = PS.take()
                        lt = mm(bank, CF[:, g, cs_], H_[:, c, :], True, True, free, T["CF"][g], th_[d], signal=True)
                        k, tb1, f = TY.take()
                        ev_ = bc(r3(eac, 64)[:, c, 32 * d + 8 * g:32 * d + 8 * g + 8], 64)
                        t = tt(DVE, r3(tb1, 64), r3(bank, 64), ev_, ALU.mult, lt, T["ea"], f)
                        PS.release(b, t)
                        ty.append((k, tb1, t))
                    k, tb2, f = TY.take()
                    t2_ = tt(PL, r3(tb2, 64), r3(xsT[:, c, :], 64), bc(dsk[:, 8 * g:8 * g + 8], 64), ALU.mult, f, txs, tr_)
                    t = tt(PL, ty[0][1], ty[0][1], ty[1][1], ALU.add, ty[0][2], ty[1][2])
                    t3 = tt(PL, ty[0][1], ty[0][1], tb2, ALU.add, t, t2_)
                    t4 = tt(DVE, ty[0][1], ybank, ty[0][1], ALU.add, t3, tyd)
                    PS.release(yb, t4)
                    if g == 0:
                        dump(f"y{c}", ty[0][1], t4)
                    t5 = tt(DVE, zs[:, c, :], zs[:, c, :], ty[0][1], ALU.mult, t4, tzs)
                    TY.release(ty[0][0], t5)
                    TY.release(ty[1][0], t)
                    t6 = act(tb2, zs[:, c, :], ACT.Square, t5, t3, acc=ssy[:, c:c + 1])
                    TY.release(k, t6)
                    tus.append(t6)

                for n in range(10):
                    if n >= 2:
                        second(n - 2)
                    if n < 8:
                        first(n)
                    yield
                T["us", g] = tus
                gone[g] = latest()
                if g == 3:
                    scale_z(g)
                    finish(g)

            def scale_z(g):
                zs = zs2[g % 2]
                t = rstd(small[:, 160:164], 4, T["us", g], mean=512.0)
                ssy = small[:, 160:164]
                T["n", g] = [ts(PL if c % 2 else DVE, zs[:, c, :], zs[:, c, :], ssy[:, c:c + 1], ALU.mult, t) for c in range(4)]

            def finish(g):
                zs, tn = zs2[g % 2], T["n", g]
                for i in range(4):
                    b, bank, free = PS.take()
                    for c in range(4):
                        lt = tr(bank[:, c * 128:(c + 1) * 128], zs[:, c, i * 128:(i + 1) * 128], free, tn, signal=(c == 3))
                    k, yt, f = yTr.take()
                    t = act(yt, bank, ACT.Copy, lt, f, scale=gssd[:, 4 * g + i:4 * g + i + 1])
                    PS.release(b, t)
                    td = dma(AC, yD[:, 4 * g + i, :], yt, t, s=ysem[k])
                    yTr.release(k, td)
                    tyD[:] = [td]
                done[g] = latest()

            rest = ada_rest(Er)
            weave(using(PALL, steps_bc()), rest, 1)
            xsF.release(1, (PE.sem, PE.count))
            weave(using(PALL, steps_proj(0)), steps_dt(), 0.5)
            for g in range(4):
                weave(using(PA, steps_chunks(g)), using(PG_, steps_proj(g + 1) if g < 3 else iter(())), 0.48)

        def attention(units, Sr, PTr):
            small_ring = Ring([small[:, 176 + 4 * i:180 + 4 * i] for i in range(8)])

            def scores(u):
                u["P"] = []
                for m in u["maps"]:
                    sk, S, sf = Sr.take()
                    vk, sv, vf = small_ring.take()
                    n = 0
                    td = []
                    for kp, kn, bias in m["keys"]:
                        b, bank, free = PS.take()
                        lt = mm(bank[:, 0:kn], m["q"], kp, True, True, free, u["qk"], signal=True)
                        if bias is None:
                            t = act(S[:, n:n + kn], bank[:, 0:kn], ACT.Copy, lt, sf, scale=u["scale"])
                        else:
                            bap, btok = bias()
                            t = stt(S[:, n:n + kn], bank[:, 0:kn], u["scale"], bap, ALU.mult, ALU.add, lt, sf, btok)
                            tbias = t
                        PS.release(b, t)
                        td.append(t)
                        n += kn
                    t = reduce_(sv[:, 0:1], S[:, 0:n], ALU.max, td, vf, negate=True)
                    t = act(S[:, 0:n], S[:, 0:n], ACT.Exp, t, bias=sv[:, 0:1], acc=sv[:, 1:2])
                    t = recip(sv[:, 1:2], sv[:, 1:2], t)
                    u["P"].append((sk, S, vk, sv, t, n))
                if "post" in u:
                    u["post"](tbias)
                if len(u["P"]) == 2:
                    (sk0, S0, vk0, sv0, t0, n), (sk1, S1, vk1, sv1, t1, _) = u["P"]
                    t = tt(DVE, sv1[:, 2:3], sv1[:, 1:2], u["nlam"], ALU.mult, t1)
                    t = ts(PL, S1[:, 0:n], S1[:, 0:n], sv1[:, 2:3], ALU.mult, t)
                    t = stt(S0[:, 0:n], S0[:, 0:n], sv0[:, 1:2], S1[:, 0:n], ALU.mult, ALU.add, t, t0)
                    Sr.release(sk1, t)
                    small_ring.release(vk1, t)
                    u["P"] = [(sk0, S0, vk0, sv0, t, n)]

            def turn(u, par):
                sk, S, vk, sv, t, n = u["P"][0]
                pk, PT, pf = PTr.take()
                te = []
                for a in range(0, n, 512):
                    m_ = min(512, n - a)
                    b, bank, free = PS.take()
                    for j in range(m_ // 128):
                        lt = tr(bank[:, j * 128:(j + 1) * 128], S[:, a + j * 128:a + (j + 1) * 128], free, t,
                                signal=(j == m_ // 128 - 1))
                    e = copy(AC if (a or par) else DVE, PT[:, a:a + m_], bank[:, 0:m_], lt, pf)
                    PS.release(b, e)
                    te.append(e)
                Sr.release(sk, lt)
                u["PT"] = (pk, PT, te)

            def values(u):
                sk, S, vk, sv, t, n = u["P"][0]
                pk, PT, te = u["PT"]
                b, bank, free = PS.take()
                nk = n // 128
                for j in range(nk):
                    lt = mm(bank[:, 0:64], PT[:, j * 128:(j + 1) * 128], u["v"](j), j == 0, j == nk - 1, free, te, u["vt"],
                            signal=(j == nk - 1))
                PTr.release(pk, lt)
                t2 = u["out"](bank[:, 0:64], lt, sv)
                PS.release(b, t2)
                small_ring.release(vk, t2)

            N = len(units)
            for i in range(N + 3):
                for u in units[0:5] if i == 0 else units[i + 4:i + 5]:
                    if "pre" in u:
                        u["pre"]()
                if i < N:
                    scores(units[i])
                if 0 <= i - 2 < N:
                    turn(units[i - 2], i % 2)
                if 0 <= i - 3 < N:
                    values(units[i - 3])
                yield

        def rope(blocks, i, par, cos, sin, rot, dests, tmp, waits, ttab):
            b1, k1, f1 = PS.take()
            for kt in range(8):
                blk = blocks[kt // 4]
                l1 = mm(k1[:, 0:512], blk[1][:, kt % 4, i * 128:(i + 1) * 128], HT[:, kt, 0:512], kt == 0, kt == 7,
                        f1, blk[2], waits, signal=(kt == 7))
            rk, (raw, tc1, tc2), rf = tmp.take()
            t = copy(AC, raw, k1[:, 0:512], l1, rf)
            PS.release(b1, t)
            b2, k2, f2 = PS.take()
            l2 = mm(k2[:, 0:512], rot, raw, True, True, f2, t, ttab, signal=True)
            ta1 = tt(PL, tc1, raw, cos, ALU.mult, t, ttab)
            tb1 = tt(DVE, tc2, k2[:, 0:512], sin, ALU.mult, l2, ttab)
            PS.release(b2, tb1)
            tds = []
            for n, (a, z, d) in enumerate(dests):
                E_ = PL if z - a == 128 else DVE
                tds.append(tt(E_, d[a:z, :], tc1[a:z, :], tc2[a:z, :], ALU.add, ta1, tb1, waits))
            tmp.release(rk, tds, l2)
            return tds, l1

        def more_slots(*at_):
            for i, a in enumerate(at_):
                W.bufs[NW + i:NW + i + 1] = [sb(a, WSLOT)]
                W.state[NW + i:NW + i + 1] = [[W.state[0][0], False, latest()]]
            W.keys = list(range(NW + len(at_)))

        def fewer_slots():
            w = [W.state[k][2] for k in W.keys[NW:]]
            assert not any(W.state[k][1] for k in W.keys[NW:])
            W.keys = W.keys[:NW]
            return w

        if stop not in ("B", "C"):
            sets = []
            for o in (PB, PB + 5120):
                sets.append((r3(sb(o, 1536), 768), r3(sb(o + 1536, 2048), 512), r3(sb(o + 3584, 1536), 256)))
            o = PB + 10240
            tmp = Ring([tuple(sb(o + 1536 * i + 512 * j, 512) for j in range(3)) for i in range(2)]); o += 3072
            yT = r3(sb(PB + 5120, 8192), 512)
            uT = r3(sb(o, 4096), 512); o += 4096
            G = [r3(sb(o, 2048), 512)] ; o += 2048
            O = r3(sb(o, 4096), 1024); o += 4096
            biasr = Ring([sb(o + 896 * i, 896) for i in range(2)]); o += 1792
            Sr = Ring([sb(o + 768 * i, 768) for i in range(4)]); o += 3072
            PTr = Ring([sb(o + 768 * i, 768) for i in range(2)]); o += 1536
            dcon = sb(o, at["d"][1] - at["d"][0]); o += at["d"][1] - at["d"][0]
            tmpE = Ring([sb(o, 512), sb(o + 512, 512)]); o += 1024
            more_slots(o)
            o += WSLOT
            assert o <= 53200, o
            oT = r3(sb(PB, 4096), 512)
            mix = r3(sb(PB + 5120, 4096), 1024)
            tb = latest() + tyD
            tcon = dma(AC, dcon, con_load("d", dcon), tb)
            rp = dram("rpb_copies", [16, 64, 465])
            rpb = A["na_rpb"]
            trp = dma(AC, rp, bass.AP(rpb.tensor, 0, [[465, 16], [0, 64], [1, 465]]), tb)
            tzq = [zero(PL if k_ else DVE, sets[k_][1].rearrange("p a b -> p (a b)"), tb) for k_ in (1, 0)]
            bsem = [[sem(f"s_bias{i}"), 0] for i in range(2)]
            over = {}
            tq, tk, tv_ = {}, {}, {}

            def na_proj(n):
                kF, qP, V = sets[(n + 1) % 2]
                prev = [tb, tzq, over.get(n - 2)]
                tq[n], tk[n], tv_[n] = [], [], []
                blocks = wcols(A["w_in"], 1024, CQ + 256 * n, 256)
                for i in range(2):
                    tds, last = rope(blocks, i, 0, con("nacos"), con("nasin"), con("rna"),
                                     [(0, 64, qP[:, 2 * i, :]), (64, 128, qP[:, 2 * i + 1, :])], tmp, [tH, prev], tcon)
                    tq[n].append(tds)
                    if i == 1:
                        for x_ in blocks:
                            W.release(x_[0], last)
                    yield
                blocks = wcols(A["w_in"], 1024, CK + 256 * n, 256)
                for i in range(2):
                    tds, last = rope(blocks, i, 0, con("nacos"), con("nasin"), con("rna"), [(0, 128, kF[:, i, 0:512])], tmp, [tH, prev], tcon)
                    b2, k2, f2 = PS.take()
                    for kt in range(8):
                        blk = blocks[kt // 4]
                        last = mm(k2[:, 0:256], blk[1][:, kt % 4, i * 128:(i + 1) * 128], HT[:, kt, 512:768], kt == 0, kt == 7,
                                  f2, signal=(kt == 7))
                    t = copy(AC, kF[:, i, 512:768], k2[:, 0:256], last, prev)
                    PS.release(b2, t)
                    tk[n].append([tds, t])
                    if i == 1:
                        for x_ in blocks:
                            W.release(x_[0], last)
                    yield
                blocks = wcols(A["w_in"], 1024, CV + 256 * n, 256)

                def ev(i, o_, tok):
                    t = copy(evac2(i), V[:, i, :], o_, tok, prev)
                    tv_[n].append(t)
                    return t
                yield from gemm_steps(blocks, range(6), lambda i, kt, w: HT[:, kt, i * 128:(i + 1) * 128], lambda i, kt, w: w, ev, tH)

            def na_attention(n):
                kF, qP, V = sets[(n + 1) % 2]
                units = []
                for hl in range(4):
                    h = 4 * n + hl
                    st = {}

                    def pre(h=h, st=st):
                        k, bb, f = biasr.take()
                        for a in range(2):
                            base = h * 29760 + (1 - a) * 31 + 15
                            src = bass.AP(rp.tensor, base, [[464, 64], [31, 14], [1, 64]])
                            td = dma(AC, r3(bb[64 * a:64 * a + 64, :], 64), src, f, trp, s=bsem[k])
                        st["k"], st["b"] = k, bb
                        st["t"] = tt(PL, r3(bb, 64), r3(bb, 64), rep(con("colmask"), 14), ALU.add, td, tcon)

                    for qt in range(4):
                        def outf(ps, lt, sv, qt=qt, h=h):
                            return ts(DVE, O[:, qt, h * 64:(h + 1) * 64], ps, sv[:, 1:2], ALU.mult, lt)
                        q = qP[:, hl, qt * 128:(qt + 1) * 128]
                        kk = kF[:, hl // 2, :]

                        def bias(st=st, qt=qt):
                            return st["b"][:, (6 - 2 * qt) * 64:(6 - 2 * qt) * 64 + 512], st["t"]
                        u = dict(maps=[dict(q=q, keys=[(kk[:, 0:512], 512, bias), (kk[:, 512:768], 256, None)])],
                                 scale=0.125, out=outf, v=lambda j, hl=hl: V[:, j, hl * 64:(hl + 1) * 64],
                                 qk=[tq[n], tk[n][hl // 2]], vt=tv_[n])
                        if qt == 0:
                            u["pre"] = pre
                        if qt == 3:
                            u["post"] = lambda t, st=st: biasr.release(st["k"], t)
                        units.append(u)
                yield from attention(units, Sr, PTr)
                over[n] = [(PE.sem, PE.count)]

            tu, tG, tmx = {}, {}, []

            def gates(c0, half):
                blocks = wcols(A["w_in"], 1024, c0 + 512 * half, 512)

                def ev(i, o_, tok):
                    t = act(G[0][:, i, :], o_, ACT.Sigmoid, tok, tb, tG.get(("r", i)))
                    tG[i] = t
                    return t
                yield from gemm_steps(blocks, range(4), lambda i, kt, w: w[:, i * 128:(i + 1) * 128],
                                      lambda i, kt, w: HT[:, kt, 0:512], ev, tH)

            def branch_ssd():
                ty_ = dma(AC, yT, yD, tyD, over[2], (DVE.sem, DVE.count), (PL.sem, PL.count), (AC.sem, AC.count))
                for half in range(2):
                    yield from gates(CGS, half)
                    blocks = wcols(A["w_branch_ssd"], 2048, 512 * half, 512)

                    def ev(i, o_, tok, half=half):
                        j = half * 4 + i
                        tG["r", i] = tu[j] = tt(DVE, uT[:, j, :], o_, G[0][:, i, :], ALU.mult, tok, tG[i], tb)
                        return tu[j]
                    yield from gemm_steps(blocks, range(4), lambda i, kt, w: w[:, i * 128:(i + 1) * 128],
                                          lambda i, kt, w: yT[:, kt, :], ev, ty_)
                yield from gates(CGN, 0)

            def branch_na(toT):
                for half in range(2):
                    if half:
                        yield from gates(CGN, half)
                    blocks = wcols(A["w_branch_na"], 1024, 512 * half, 512)

                    def ev(i, o_, tok, half=half):
                        j = half * 4 + i
                        k, tm_, f = tmpE.take()
                        t = tt(DVE, tm_, o_, G[0][:, i, :], ALU.mult, tok, tG[i], f)
                        tG["r", i] = t
                        tu[j] = tt(PL, uT[:, j, :], uT[:, j, :], tm_, ALU.add, t, tu[j])
                        tmpE.release(k, tu[j])
                        return t
                    yield from gemm_steps(blocks, range(4), lambda i, kt, w: w[:, i * 128:(i + 1) * 128],
                                          lambda i, kt, w: oT[:, kt, :], ev, toT)

            run(na_proj(0))
            for n in range(3):
                weave(using(PA, na_attention(n)), using(PG_, na_proj(n + 1)), 0.55)
            weave(using(PA, na_attention(3)), using(PG_, branch_ssd()), 0.4)
            dump("O", O)
            toT, tO = [], (DVE.sem, DVE.count)
            for j in range(8):
                b, bank, free = PS.take()
                for i in range(4):
                    lt = tr(bank[:, i * 128:(i + 1) * 128], O[:, i, j * 128:(j + 1) * 128], free, tO, signal=(i == 3))
                t = copy(evac2(j), oT[:, j, :], bank, lt, over[3])
                PS.release(b, t)
                toT.append(t)
            run(branch_na(toT))
            tu_ = [tu[j] for j in range(8)]
            tyd_ = [(PE.sem, PE.count)]
            for half in range(2):
                blocks = wcols(A["w_out"], 1024, 512 * half, 512)

                def ev(i, o_, tok, half=half):
                    t = copy(evac2(i), mix[:, i, half * 512:half * 512 + 512], o_, tok, tyd_)
                    tmx.append(t)
                    return t
                gemm(blocks, range(4), lambda i, kt, w: uT[:, kt, i * 128:(i + 1) * 128], lambda i, kt, w: w, ev, tu_)
            wfree = fewer_slots()
            dump("mix", mix)

        X = r3(sb(BASE, 4096), 1024)
        HT2 = r3(sb(BASE + 4096, 4096), 512)
        PF = BASE + 8192

        def residual(m, gam, ssq_, junk_, tm_, txload):
            tq = tm_
            for i in range(4):
                tq = [act(junk_, m[:, i, :], ACT.Square, tq, acc=ssq_[:, i:i + 1])]
            t = rstd(ssq_, 4, tq)
            done = []
            for i in range(4):
                t1 = stt(m[:, i, :], m[:, i, :], ssq_[:, i:i + 1], gam, ALU.mult, ALU.mult, t, txload)
                done.append(tt(PL if i % 2 else DVE, X[:, i, :], X[:, i, :], m[:, i, :], ALU.add, t1, txload))
            return done

        t2nd = []

        def second_tables():
            tcg = dma(AC, gcon, con_load("g", gcon), tb)
            posf = scratch[:, 0:512]
            angb = [scratch[:, 512 * (i + 1):512 * (i + 2)] for i in range(3)]
            posi = scratch[:, 2048:2560].bitcast(I32)
            t = dma(AC, posi, A["positions"].rearrange("a n -> (a n)").partition_broadcast(128), tb)
            t = copy(DVE, posf, posi, t)
            C1 = 6.28125
            rest = 2 * math.pi - C1
            C2 = float(np.float32(round(rest * 2 ** 21) / 2 ** 21))
            C3 = float(np.float32(rest - C2))
            ttab = []
            for n, (inv_, which) in enumerate((("invb", 0), ("invb", 1), ("invd", 0), ("invd", 1))):
                ang, kk_, r_ = angb
                t = ts(DVE, ang, posf, con(inv_), ALU.mult, t, tcg)
                t = ts(DVE, kk_, ang, 1.0 / (2 * math.pi), ALU.mult, t, s2=0.25 if which == 0 else 0.0, op1=ALU.add)
                t = ts(DVE, kk_, kk_, MAGIC, ALU.add, t)
                t = ts(DVE, kk_, kk_, MAGIC, ALU.subtract, t)
                t = stt(r_, kk_, -C1, ang, ALU.mult, ALU.add, t)
                t = stt(r_, kk_, -C2, r_, ALU.mult, ALU.add, t)
                t = stt(r_, kk_, -C3, r_, ALU.mult, ALU.add, t)
                if which == 0:
                    t = ts(DVE, r_, r_, math.pi / 2, ALU.add, t)
                t = ts(DVE, r_, r_, 3.1415925, ALU.min, t, s2=-3.1415925, op1=ALU.max)
                t = act(tabs[n], r_, ACT.Sin, t)
                ttab.append(t)
            lam4 = scratch[:, 2560:2816]
            ls = [sem("s_lam"), 0]
            for i, nme in enumerate(("lambda_q1", "lambda_k1", "lambda_q2", "lambda_k2")):
                tl_ = dma(AC, lam4[:, i * 64:(i + 1) * 64], A[nme].rearrange("a n -> (a n)").partition_broadcast(128), tb, s=ls)
            tgd = dma(AC, gd, A["g_diff"].rearrange("a n -> (a n)").partition_broadcast(128), tb)
            prod = lam4
            t = tt(DVE, prod[:, 0:64], lam4[:, 0:64], lam4[:, 64:128], ALU.mult, tl_)
            t = tt(DVE, prod[:, 64:128], lam4[:, 128:192], lam4[:, 192:256], ALU.mult, t)
            t = reduce_(lamv[:, 0:4], r3(prod[:, 0:128], 32), ALU.add, t)
            t = act(lamv[:, 4:8], lamv[:, 0:4], ACT.Exp, t)
            inits = [0.8 - 0.6 * math.exp(-0.3 * l) for l in range(2)]
            t = tt(DVE, lamv[:, 8:10], lamv[:, 6:8], lamv[:, 4:6], ALU.subtract, t)
            tlam = [ts(DVE, lamv[:, 8 + l:9 + l], lamv[:, 8 + l:9 + l], -inits[l], ALU.add, t) for l in range(2)]
            tgs = [ts(DVE, gd[:, 64 * l:64 * l + 64], gd[:, 64 * l:64 * l + 64], 1.0 - inits[l], ALU.mult, tgd) for l in range(2)]
            t2nd.extend(ttab + tlam + tgs + [tcg])

        if stop not in ("B", "C", "D", "E0"):
            txr = dma(AC, X, xT, (PE.sem, PE.count))
            tb = latest()
            junk = sb(PB + 9216, 1024)
            gam1 = sb(PB + 10240, 1024)
            tg1 = dma(AC, gam1, gamD[0:1, :].rearrange("a n -> (a n)").partition_broadcast(128), tb, tgam)
            tX = residual(mix, gam1, small[:, 128:132], junk, tmx, [txr, tg1])
            dump("X1", X)
            tb = latest() + tX + wfree
            o = PF
            tabs = [sb(o + 512 * i, 512) for i in range(4)]; o += 2048
            lamv = sb(o, 16); o += 16
            gd = sb(o, 128); o += 128
            ng = at["g"][1] - at["g"][0]
            gcon = sb(o, ng); o += ng
            PG = o
            h2 = r3(sb(o, 4096), 1024); o += 4096
            moe = r3(sb(o, 4096), 1024); o += 4096
            xgr = Ring([r3(sb(o + 1024 * i, 1024), 128) for i in range(2)]); o += 2048
            yor = Ring([sb(o + 1024 * i, 1024) for i in range(2)]); o += 2048
            Pr = Ring([r3(sb(o + 512 * i, 512), 128) for i in range(2)]); o += 1024
            PTr = Ring([sb(o + 512 * i, 512) for i in range(2)]); o += 1024
            Pg = r3(sb(o, 512), 128); o += 512
            hidr = Ring([sb(o + 512 * i, 512) for i in range(2)]); o += 1024
            hidTr = Ring([r3(sb(o + 2048 * i, 2048), 128) for i in range(2)]); o += 4096
            wr_ = sb(o, 128); o += 128
            aff = sb(o, 64); o += 64
            slot = sb(o, 64); o += 64
            iota = sb(o, 64); o += 64
            m8 = sb(o, 8); o += 8
            more_slots(*[o + WSLOT * i for i in range(3)]); o += 3 * WSLOT
            assert o <= 53200, (o)
            ytmp = moe.rearrange("p a b -> p (a b)")
            wrk, slotT = ytmp[:, 0:512], ytmp[:, 512:1024]
            tio = dma(AC, iota, con_load("f", iota), tb)
            twr = dma(AC, r3(wr_, 16), A["w_router"].rearrange("(k p) e -> p k e", p=128), tb)
            th2 = normed_T(X, 4, HT2, xgr.bufs[0].rearrange("p a b -> p (a b)"), h2, small[:, 128:132],
                           lambda j: mc[:, 3, j, 0:1], lambda j: mc[:, 2, j, 0:1], tb)
            tall = latest()
            b, bank, free = PS.take()
            for i in range(4):
                for kt in range(8):
                    lt = mm(bank[:, i * 16:(i + 1) * 16], HT2[:, kt, i * 128:(i + 1) * 128], r3(wr_, 16)[:, kt, :], kt == 0, kt == 7,
                            free, twr, th2, signal=(i == 3 and kt == 7))
            sv = small[:, 144:160]
            t = reduce_(sv[:, 0:4], r3(bank[:, 0:64], 16), ALU.max, lt)
            t = tt(DVE, r3(aff, 16), r3(bank[:, 0:64], 16), bc(sv[:, 0:4], 16), ALU.subtract, t, tb)
            PS.release(b, t)
            t = act(aff, aff, ACT.Exp, t)
            t = reduce_(sv[:, 4:8], r3(aff, 16), ALU.add, t)
            t = recip(sv[:, 4:8], sv[:, 4:8], t)
            taff = tt(DVE, r3(aff, 16), r3(aff, 16), bc(sv[:, 4:8], 16), ALU.mult, t)
            b, bank, free = PS.take()
            for i in range(4):
                lt = tr(bank[0:16, i * 128:(i + 1) * 128], aff[:, i * 16:(i + 1) * 16], free, taff, signal=(i == 3))
            t = copy(DVE, wrk[0:16, :], bank[0:16, :], lt, tb)
            PS.release(b, t)
            th3 = []
            for i in range(4):
                for hf_ in range(2):
                    b, bank, free = PS.take()
                    for j in range(4):
                        lt = tr(bank[:, j * 128:(j + 1) * 128], HT2[:, hf_ * 4 + j, i * 128:(i + 1) * 128], free, th2, signal=(j == 3))
                    te = copy(AC, h2[:, i, hf_ * 512:hf_ * 512 + 512], bank, lt, tall)
                    PS.release(b, te)
                    th3.append(te)
            for n in range(8):
                t = DVE.op(lambda e: e.max(m8[0:16, :], wrk[0:16, :]), t)
                t = DVE.op(lambda e: e.match_replace(wrk[0:16, :], m8[0:16, :], wrk[0:16, :], -1.0), t)
            t = ts(DVE, wrk[0:16, :], wrk[0:16, :], 0.0, ALU.is_lt, t)
            t = DVE.op(lambda e: e.tensor_tensor_scan(slotT[0:16, :], wrk[0:16, :], wrk[0:16, :], 0.0, ALU.add, ALU.max), t)
            t = tt(DVE, slotT[0:16, :], slotT[0:16, :], wrk[0:16, :], ALU.mult, t)
            t = ts(DVE, slotT[0:16, :], slotT[0:16, :], -1.0, ALU.add, t)
            b, bank, free = PS.take()
            for i in range(4):
                lt = tr(bank[:, i * 16:(i + 1) * 16], slotT[0:16, i * 128:(i + 1) * 128], free, t, signal=(i == 3))
            tsl = copy(DVE, slot, bank[:, 0:64], lt)
            PS.release(b, tsl)
            dump("slot", slot)
            dump("aff", aff)
            tPg = [None]

            def gather(m):
                pk, P, pf = Pr.take()
                tP = []
                for i in range(4):
                    tP.append(tt(DVE, r3(P[:, i, :], 64), bc(slot[:, i * 16 + 2 * m:i * 16 + 2 * m + 2], 64), rep(iota, 2),
                                 ALU.is_equal, tsl, tio, pf, tb))
                t = [tt(PL, r3(Pg[:, i, :], 64), r3(P[:, i, :], 64), bc(aff[:, i * 16 + 2 * m:i * 16 + 2 * m + 2], 64), ALU.mult,
                        tP[i], tPg[0]) for i in range(4)]
                xk, xg, xf = xgr.take()
                txg = []
                for q_ in range(2):
                    b, bank, free = PS.take()
                    for kt in range(4):
                        for i in range(4):
                            c0 = (4 * q_ + kt) * 128
                            lt = mm(bank[:, kt * 128:(kt + 1) * 128], h2[:, i, c0:c0 + 128], P[:, i, :], i == 0, i == 3, free,
                                    tP, th3, signal=(kt == 3 and i == 3))
                    e = copy(evac2(q_), xg[:, 4 * q_:4 * q_ + 4, :], r3(bank, 128), lt, xf, tb)
                    PS.release(b, e)
                    txg.append(e)
                Pr.release(pk, lt, t)
                b, bank, free = PS.take()
                for i in range(4):
                    lt = tr(bank[:, i * 128:(i + 1) * 128], Pg[:, i, :], free, t, signal=(i == 3))
                tPg[0] = lt
                k, PT, f = PTr.take()
                e = copy(AC, PT, bank, lt, f)
                PS.release(b, e)
                return dict(xk=xk, xg=xg, txg=txg, PT=(k, PT, e))

            def scatter(u):
                k, PT, tpt = u["PT"]
                yk, yo, tyo = u["yo"]
                for i in range(4):
                    for n in range(2):
                        b, bank, free = PS.take()
                        lt = mm(bank, PT[:, i * 128:(i + 1) * 128], yo[:, n * 512:n * 512 + 512], True, True, free, tpt, tyo,
                                signal=True)
                        d = moe[:, i, n * 512:n * 512 + 512]
                        if u["m"]:
                            t = tt(DVE, d, bank, d, ALU.add, lt, tms.get((i, n)))
                        else:
                            t = copy(DVE, d, bank, lt, tsl)
                        tms[i, n] = t
                        PS.release(b, t)
                PTr.release(k, lt)
                yor.release(yk, lt)

            tms = {}
            u, last_u = gather(0), None
            tb = tb + [(PE.sem, PE.count)]
            scratch = HT2.rearrange("p a b -> p (a b)")
            second_tables()
            for m in range(8):
                xg, txg = u["xg"], u["txg"]
                eg = [A["w_exp_gate"][2 * m + j] for j in range(2)]
                eu = [A["w_exp_up"][2 * m + j] for j in range(2)]
                ed = [A["w_exp_down"][2 * m + j] for j in range(2)]
                thT = []
                hk, hidT, hf_ = hidTr.take()
                for s in range(4):
                    res = []
                    for w2 in (eg, eu):
                        b, bank, free = PS.take()
                        for kg in range(2):
                            bl = [wblock(w2[j], kg * 512, 4, s * 512, 512) for j in range(2)]
                            for kk in range(4):
                                kt = kg * 4 + kk
                                for j in range(2):
                                    lt = mm(bank[64 * j:64 * j + 64, :], xg[:, kt, 64 * j:64 * j + 64],
                                            bl[j][1][:, kk, :], kt == 0, kt == 7, free, bl[j][2], txg,
                                            signal=(kk == 3))
                                    if kk == 3:
                                        W.release(bl[j][0], lt)
                        res.append((b, bank, lt))
                    k, hid, f = hidr.take()
                    t = act(hid, res[0][1], ACT.Silu, res[0][2], f, tb)
                    PS.release(res[0][0], t)
                    t = tt(DVE, hid, hid, res[1][1], ALU.mult, t, res[1][2])
                    PS.release(res[1][0], t)
                    b, bank, free = PS.take()
                    for j in range(4):
                        lt = tr(bank[:, j * 128:(j + 1) * 128], hid[:, j * 128:(j + 1) * 128], free, t, signal=(j == 3))
                    hidr.release(k, lt)
                    e = copy(DVE, hidT[:, s * 4:s * 4 + 4, :], r3(bank, 128), lt, hf_, tb)
                    PS.release(b, e)
                    thT.append(e)
                    if s == 0 and last_u:
                        scatter(last_u)
                xgr.release(u["xk"], lt)
                yk, yo, yf = yor.take()
                tyo = []
                nxt = None
                for n in range(2):
                    b, bank, free = PS.take()
                    for kg in range(4):
                        bl = [wblock(ed[j], kg * 512, 4, n * 512, 512) for j in range(2)]
                        for kk in range(4):
                            kt = kg * 4 + kk
                            for j in range(2):
                                lt = mm(bank[64 * j:64 * j + 64, :], hidT[:, kt, 64 * j:64 * j + 64], bl[j][1][:, kk, :],
                                        kt == 0, kt == 15, free, bl[j][2], thT, signal=(kk == 3))
                                if kk == 3:
                                    W.release(bl[j][0], lt)
                    e = copy(AC, yo[:, n * 512:n * 512 + 512], bank, lt, yf, tb)
                    PS.release(b, e)
                    tyo.append(e)
                    if n == 0 and m < 7:
                        nxt = gather(m + 1)
                hidTr.release(hk, lt)
                u.update(yo=(yk, yo, tyo), m=m)
                last_u, u = u, nxt
            gam2 = h2.rearrange("p a b -> p (a b)")[:, 0:1024]
            tg2 = dma(AC, gam2, gamD[1:2, :].rearrange("a n -> (a n)").partition_broadcast(128), (PE.sem, PE.count))
            scatter(last_u)
            wfree = fewer_slots()
            tX = residual(moe, gam2, small[:, 128:132], h2[:, 1, :], list(tms.values()), tg2)
            dump("X2", X)

        if stop not in ("B", "C", "D", "E0", "E", "F"):
            cosb, sinb, cosd, sind = tabs
            ttab = []
            for layer in range(2):
                tb = latest() + t2nd + tX
                o = PG
                qP = r3(sb(o, 6144), 512); o += 6144
                kF = r3(sb(o, 2048), 512); o += 2048
                V = r3(sb(o, 2048), 512); o += 2048
                O = r3(sb(o, 4096), 1024); o += 4096
                Sr = Ring([sb(o + 512 * i, 512) for i in range(6)]); o += 3072
                PTr = Ring([sb(o + 512 * i, 512) for i in range(3)]); o += 1536
                tmp = Ring([tuple(sb(o + 1536 * i + 512 * j, 512) for j in range(3)) for i in range(2)]); o += 3072
                hn = sb(o, 64 * 4); o += 256
                assert o <= 53200, o
                xnb = r3(sb(PG, 4096), 1024)
                HT = HT2
                tH = normed_T(X, 4, HT2, sb(PG + 4096, 1024), xnb, small[:, 128:132],
                              lambda j: gmix2[:, layer * 8 + j:layer * 8 + j + 1], lambda j: None, tb)
                tb = latest()
                tz2 = [zero(DVE, qP.rearrange("p a b -> p (a b)"), tb)]
                tOall = []
                Wi = A["w_in_2"][layer]
                hnr = Ring([hn[:, 64 * i:64 * i + 64] for i in range(4)])

                def vcols(c0, n, d0, dst_wait, blocks, w0, tv_):
                    def ev(i, o_, tok):
                        t = copy(evac2(i), V[:, i, d0:d0 + n], o_, tok, dst_wait)
                        tv_.append(t)
                        return t
                    gemm(blocks, range(4), lambda i, kt, w: HT2[:, kt, i * 128:(i + 1) * 128], lambda i, kt, w: w[:, w0:w0 + n], ev, tH)

                def proj(c0, kind, dest, waits_, toks):
                    blocks = wcols(Wi, 1024, c0, 256)
                    cs2 = (cosd, sind, con("rd")) if kind == "d" else (cosb, sinb, con("rb"))
                    for i in range(2):
                        tds, last = rope(blocks, i, 0, *cs2, dest(i), tmp, [tH, waits_], ttab)
                        toks.append(tds)
                    for x_ in blocks:
                        W.release(x_[0], last)

                def outn(O_, qt, col):
                    def f(ps, lt, sv):
                        t = ts(DVE, O_[:, qt, col:col + 64], ps, sv[:, 1:2], ALU.mult, lt)
                        tOall.append(t)
                        return t
                    return f

                def outd(O_, qt, col):
                    def f(ps, lt, sv):
                        k, hb_, f_ = hnr.take()
                        t0 = copy(DVE, hb_, ps, lt, f_)
                        d = O_[:, qt, col:col + 64]
                        t = act(d, hb_, ACT.Square, t0, acc=sv[:, 0:1])
                        t = ts(DVE, sv[:, 0:1], sv[:, 0:1], 1.0 / 64, ALU.mult, t, s2=EPS, op1=ALU.add)
                        t = act(sv[:, 1:2], sv[:, 0:1], ACT.Ln, t)
                        t = act(sv[:, 1:2], sv[:, 1:2], ACT.Exp, t, scale=-0.5)
                        t = stt(sv[:, 2:3], sv[:, 1:2], sv[:, 0:1], sv[:, 1:2], ALU.mult, ALU.mult, t)
                        t = ts(DVE, sv[:, 2:3], sv[:, 2:3], -0.5, ALU.mult, t, s2=1.5, op1=ALU.add)
                        t = tt(DVE, sv[:, 1:2], sv[:, 1:2], sv[:, 2:3], ALU.mult, t)
                        t = stt(d, hb_, sv[:, 1:2], gd[:, 64 * layer:64 * layer + 64], ALU.mult, ALU.mult, t)
                        hnr.release(k, t)
                        tOall.append(t)
                        return t
                    return f

                tq, tk, tv_ = [], [], []
                proj(0, "d", lambda i: [(32 * c, 32 * c + 32, qP[:, 4 * i + c, :]) for c in range(4)], tz2, tq)
                proj(256, "d", lambda i: [(0, 128, kF[:, i, :])], tb, tk)
                blocks = wcols(Wi, 1024, 512, 256)
                vcols(512, 256, 0, tb, blocks, 0, tv_)
                proj(768, "b", lambda i: [(64 * c, 64 * c + 64, qP[:, 8 + 2 * i + c, :]) for c in range(2)], tz2, tq)
                proj(1024, "b", lambda i: [(0, 128, kF[:, 2 + i, :])], tb, tk)
                blocks = wcols(Wi, 1024, 1280, 256)
                vcols(1280, 256, 256, tb, blocks, 0, tv_)
                units = []
                for h in range(8):
                    for qt in range(4):
                        n = 128 * (qt + 1)
                        bias = lambda qt=qt: (con("causal")[:, 384 - 128 * qt:512], None)
                        qs = slice(qt * 128, qt * 128 + 128)
                        if h < 4:
                            maps = [dict(q=qP[:, 4 * (h // 2) + 2 * (h % 2) + c, qs], keys=[(kF[:, h // 2, 0:n], n, bias)]) for c in range(2)]
                            units.append(dict(maps=maps, scale=32 ** -0.5, out=outd(O, qt, 64 * h), nlam=lamv[:, 8 + layer:9 + layer],
                                              v=lambda j, h=h: V[:, j, 64 * h:64 * h + 64]))
                        else:
                            hb2 = h - 4
                            maps = [dict(q=qP[:, 8 + hb2, qs], keys=[(kF[:, 2 + hb2 // 2, 0:n], n, bias)])]
                            units.append(dict(maps=maps, scale=0.125, out=outn(O, qt, 64 * h),
                                              v=lambda j, h=h: V[:, j, 64 * h:64 * h + 64]))
                [u.update(qk=[tq, tk], vt=tv_) for u in units]; run(attention(units, Sr, PTr))
                if layer == 0:
                    dump("kF", kF); dump("V", V); dump("qP", qP); dump("HT2", HT2)
                tb2 = latest()
                tz2 = [zero(DVE, qP[:, 0:8, :].rearrange("p a b -> p (a b)"), tb2)]
                tq, tk, tv_ = [], [], []
                for s in range(2):
                    proj(1536 + 256 * s, "b", lambda i: [(64 * c, 64 * c + 64, qP[:, 4 * s + 2 * i + c, :]) for c in range(2)], tz2, tq)
                for s in range(2):
                    proj(2048 + 256 * s, "b", lambda i: [(0, 128, kF[:, 2 * s + i, :])], tb2, tk)
                blocks = wcols(Wi, 1024, 2560, 512)
                vcols(2560, 512, 0, tb2, blocks, 0, tv_)
                units = []
                for h in range(8):
                    for qt in range(4):
                        n = 128 * (qt + 1)
                        qs = slice(qt * 128, qt * 128 + 128)
                        bias = lambda qt=qt: (con("dilated")[:, 384 - 128 * qt:512], None)
                        maps = [dict(q=qP[:, h, qs], keys=[(kF[:, h // 2, 0:n], n, bias)])]
                        units.append(dict(maps=maps, scale=0.125, out=outn(O, qt, 512 + 64 * h),
                                          v=lambda j, h=h: V[:, j, 64 * h:64 * h + 64]))
                [u.update(qk=[tq, tk], vt=tv_) for u in units]; run(attention(units, Sr, PTr))
                tO = latest()
                if layer == 0:
                    dump("O2", O)
                oT = HT2
                toT = []
                for j in range(8):
                    b, bank, free = PS.take()
                    for i in range(4):
                        lt = tr(bank[:, i * 128:(i + 1) * 128], O[:, i, j * 128:(j + 1) * 128], free, tO, signal=(i == 3))
                    t = copy(evac2(j), oT[:, j, :], bank, lt)
                    PS.release(b, t)
                    toT.append(t)
                tX = []
                for half in range(2):
                    blocks = wcols(A["w_out_2"][layer], 1024, 512 * half, 512)

                    def ev(i, o_, tok, half=half):
                        d = X[:, i, half * 512:half * 512 + 512]
                        t = tt(DVE, d, o_, d, ALU.add, tok)
                        tX.append(t)
                        return t
                    gemm(blocks, range(4), lambda i, kt, w: oT[:, kt, i * 128:(i + 1) * 128], lambda i, kt, w: w, ev, toT)
                if layer == 0:
                    dump("X3", X)
                tb = latest() + tX
                o = PG
                actT = r3(sb(o, 11264), 512); o += 11264
                pads = Ring([sb(o + 516 * i, 514) for i in range(4)]); o += 2064
                accs = Ring([sb(o + 512 * i, 512) for i in range(4)]); o += 2048
                xnb = r3(sb(o, 4096), 1024)
                junk = sb(o + 4096, 1024)
                tH = normed_T(X, 4, HT2, junk, xnb, small[:, 128:132],
                              lambda j: gffn2[:, layer * 8 + j:layer * 8 + j + 1], lambda j: None, tb)
                tz = [zero(DVE, p_[:, 0:2], tb) for p_ in pads.bufs]
                Wu = A["w_up_2"][layer]
                tact = []
                for s in range(11):
                    bl = []
                    for kg in range(2):
                        def parts(buf, kg=kg, s=s):
                            d = r3(buf, 512)
                            rr = Wu[kg * 512:kg * 512 + 512, :]
                            return [(d[:, :, 256 * v:256 * v + 256],
                                     rr[:, 2816 * v + 256 * s:2816 * v + 256 * s + 256].rearrange("(k p) n -> p k n", p=128)) for v in range(2)]
                        k, buf, tok = wload(parts)
                        bl.append((k, r3(buf, 512), tok, 4))
                    held = {}

                    def ev(i, o_, tok, s=s, held=held):
                        v, j = i // 2, i % 2
                        ti = 22 * v + 2 * s + j
                        pk, pad, pf = pads.take()
                        c1 = copy(AC, pad[:, 2:514], o_, tok, pf, tz)
                        ak, ac_, af = accs.take()
                        w3 = lambda q_: vcw2[:, layer * 132 + q_ * 44 + ti:layer * 132 + q_ * 44 + ti + 1]
                        t = ts(PL, ac_, pad[:, 0:512], w3(0), ALU.mult, c1, af)
                        t = stt(ac_, pad[:, 1:513], w3(1), ac_, ALU.mult, ALU.add, t)
                        t = stt(ac_, pad[:, 2:514], w3(2), ac_, ALU.mult, ALU.add, t)
                        pads.release(pk, t)
                        bb = vcb[:, 24 + layer * 44 + ti:24 + layer * 44 + ti + 1]
                        if v == 0:
                            t = act(ac_, ac_, ACT.Silu, t, bias=bb)
                            held[j] = (ak, ac_, t)
                        else:
                            gk, ga, gt = held[j]
                            t = stt(actT[:, 2 * s + j, :], ac_, bb, ga, ALU.add, ALU.mult, t, gt, tb)
                            accs.release(ak, t)
                            accs.release(gk, t)
                            tact.append(t)
                        return c1
                    gemm(bl, (0, 1, 2, 3), lambda i, kt, w: w[:, i * 128:(i + 1) * 128], lambda i, kt, w: HT2[:, kt, :], ev, tH)
                tX = []
                for half in range(2):
                    blocks = wcols_later(A["w_down_2"][layer], 2816, 512 * half, 512)

                    def ev(i, o_, tok, half=half):
                        d = X[:, i, half * 512:half * 512 + 512]
                        t = tt(DVE, d, o_, d, ALU.add, tok)
                        tX.append(t)
                        return t
                    chunked(blocks, range(4), lambda i, kt, w: actT[:, kt, i * 128:(i + 1) * 128], lambda i, kt, w: w, ev, 1, tact)
                if layer == 0:
                    dump("X4", X)
            tb = latest()
            gf = sb(PG, 1024)
            ob = r3(sb(PG + 1024, 4096), 1024)
            tgf = dma(AC, gf, A["g_final"].partition_broadcast(128), tb)
            ssq = small[:, 128:132]
            tq = [act(ob[:, i, :], X[:, i, :], ACT.Square, tX, tb, acc=ssq[:, i:i + 1]) for i in range(4)]
            t = rstd(ssq, 4, tq)
            osem = [sem("s_out"), 0]
            for i in range(4):
                t1 = stt(ob[:, i, :], X[:, i, :], ssq[:, i:i + 1], gf, ALU.mult, ALU.mult, t, tgf)
                tend = dma(SP, out[0, i * 128:(i + 1) * 128, :], ob[:, i, :], t1, s=osem)
            SP.need([tend])
        else:
            SP.need([latest(), tyD])

        SP.need(tdump)
        block = ctx.enter_context(nc.Block())
        block.sync(SP.run)
        block.tensor(PE.run)
        block.vector(DVE.run)
        block.scalar(AC.run)
        block.gpsimd(PL.run)


_INS = ['x', 'c', 'ctx', 'c_ctx', 'w_ada', 'b_ada', 'norm_pre_mix', 'norm_post_mix', 'norm_pre_ffn', 'norm_post_ffn',
        'w_in', 'na_rpb', 'ssd_conv_w', 'ssd_conv_b', 'ssd_a_log_fwd', 'ssd_a_log_bwd', 'ssd_dt_bias_fwd',
        'ssd_dt_bias_bwd', 'ssd_d_skip', 'ssd_norm', 'w_branch_na', 'w_branch_ssd', 'w_out', 'w_router',
        'w_exp_gate', 'w_exp_up', 'w_exp_down', 'positions_2', 'g_mix_2', 'w_in_2', 'w_out_2', 'lambda_q1_2',
        'lambda_k1_2', 'lambda_q2_2', 'lambda_k2_2', 'g_diff_2', 'g_ffn_2', 'w_up_2', 'conv_w_2', 'conv_b_2',
        'w_down_2', 'g_final_2']
_DROP = ['w_ada', 'w_in', 'w_branch_na', 'w_branch_ssd', 'w_out', 'w_router', 'w_exp_gate', 'w_exp_up', 'w_exp_down']
_NAMES = {'positions_2': 'positions', 'lambda_q1_2': 'lambda_q1', 'lambda_k1_2': 'lambda_k1',
          'lambda_q2_2': 'lambda_q2', 'lambda_k2_2': 'lambda_k2', 'g_diff_2': 'g_diff', 'g_final_2': 'g_final'}


def kernel(**inputs):
    import concourse.bacc as _bacc
    from concourse.bass_utils import run_bass_kernel_spmd as _run

    nc = _bacc.Bacc("TRN2", target_bir_lowering=False, num_devices=1)
    arrays, A = {}, {}
    consts, at = shape_constants()
    for name in _INS + ["consts"]:
        a = np.ascontiguousarray(consts if name == "consts" else inputs[name])
        if name in _DROP:
            a = a[0]
        arrays[f"in_{name}_dram"] = a
        A[_NAMES.get(name, name)] = nc.dram_tensor(f"in_{name}_dram", a.shape, mybir.dt.from_np(a.dtype), kind="ExternalInput").ap()
    A["at"] = at
    out = nc.dram_tensor("out_0_dram", (1, 512, 1024), F32, kind="ExternalOutput").ap()
    build(nc, A, out)
    r = _run(nc, [arrays], core_ids=[0])
    return r.results[0]["out_0_dram"]
```

```python
import math

import numpy as np
import concourse.bass as bass
from concourse import mybir
from contextlib import ExitStack

F32 = mybir.dt.float32
I32 = mybir.dt.int32
ALU = mybir.AluOpType
ACT = mybir.ActivationFunctionType
AX = mybir.AxisListType

EPS = 1e-6
NEG = -1e30
MAGIC = 12582912.0
WSLOT = 2048

CQ, CK, CV, CZ, CX, CB, CC, CDT, CGN, CGS = 0, 1024, 2048, 3072, 5120, 7168, 7680, 8192, 8256, 9280


def shape_constants():
    parts, at, n = [], {}, 0

    def put(name, a):
        nonlocal n
        a = np.asarray(a, np.float32)
        at[name] = (n, n + a.shape[1])
        parts.append(a)
        n += a.shape[1]

    def mark(group):
        at[group] = (sum(b - a for g, (a, b) in at.items() if len(g) == 1), n)

    p = np.arange(128)
    put("ident", np.eye(128))
    put("ule", p[:, None] <= p[None, :])
    put("uge", p[:, None] >= p[None, :])
    put("ones", np.ones((128, 128)))
    put("sel", (p[:, None] % 32 == np.arange(2)) * (p[:, None] < 96))
    dist = 384 + p[:, None] - np.arange(512)[None, :]
    mark("a")
    put("causal", np.where(dist >= 0, 0.0, NEG))
    count = (dist >= 0) * ((dist <= 128) * 1.0 + (dist % 4 == 0) + (dist % 16 == 0))
    put("dilated", np.where(count > 0, np.log(np.maximum(count, 1.0)), NEG))
    rna = np.zeros((128, 128))
    rb = np.zeros((128, 128))
    rd = np.zeros((128, 128))
    for f in range(128):
        if f % 32 < 16:
            rna[f, f + 16] = -1
        else:
            rna[f, f - 16] = 1
        if f % 64 < 8:
            rb[f, f + 8] = -1
        elif f % 64 < 16:
            rb[f, f - 8] = 1
        if f % 32 < 4:
            rd[f, f + 4] = -1
        elif f % 32 < 8:
            rd[f, f - 4] = 1
    put("rb", rb.T)
    put("rd", rd.T)
    t = np.arange(512)
    inv = (np.float32(10000.0) ** (-np.arange(16, dtype=np.float32) / np.float32(16))).astype(np.float32)
    pos = np.where(((p % 64) < 32)[:, None], (t // 64)[None, :], (t % 64)[None, :]).astype(np.float32)
    ang = (pos * inv[p % 16][:, None]).astype(np.float32).astype(np.float64)
    ib = np.power(np.float32(500000.0), -np.arange(8, dtype=np.float32) * np.float32(2.0) / np.float32(16))
    idf = np.power(np.float32(500000.0), -np.arange(4, dtype=np.float32) * np.float32(2.0) / np.float32(8))
    put("invb", np.where(p % 64 < 16, ib[p % 8], 0.0)[:, None])
    put("invd", np.where(p % 32 < 8, idf[p % 4], 0.0)[:, None])
    col = np.arange(64)
    mark("g")
    put("rna", rna.T)
    put("nacos", np.cos(ang))
    put("nasin", np.sin(ang))
    cs = np.clip(col - 8, 0, 48)
    ok = (col[None, :] >= cs[:, None]) & (col[None, :] < cs[:, None] + 16)
    put("colmask", np.where(ok[p % 64], 0.0, NEG))
    mark("d")
    put("iota", np.tile(col[None, :], (128, 1)))
    mark("f")
    return np.concatenate(parts, axis=1), at


class Engine:

    def __init__(self, sem):
        self.sem, self.count, self.todo, self.seen = sem, 0, [], {}

    def need(self, waits):
        for t in waits:
            if t is None:
                continue
            if isinstance(t, list):
                self.need(t)
                continue
            sem, v = t
            if self.seen.get(id(sem), 0) < v:
                self.seen[id(sem)] = v
                self.todo.append(lambda e, s=sem, v=v: e.wait_ge(s, v))

    def op(self, make, *waits, signal=True):
        self.need(waits)
        if not signal:
            self.todo.append(make)
            return None
        self.count += 1
        self.todo.append(lambda e: make(e).then_inc(self.sem, 1))
        return (self.sem, self.count)

    def run(self, e):
        for f in self.todo:
            f(e)


class Ring:

    def __init__(self, bufs, keys=None, state=None):
        self.bufs = bufs
        self.keys = keys or list(range(len(bufs)))
        self.state = state if state is not None else [[i - len(bufs), False, []] for i in range(len(bufs))]

    def take(self):
        k = min((k for k in self.keys if not self.state[k][1]), key=lambda k: self.state[k][0])
        waits = self.state[k][2]
        self.state[k][1:] = [True, []]
        return k, self.bufs[k], waits

    def release(self, k, *toks):
        s = self.state[k]
        s[0], s[1], s[2] = max(x[0] for x in self.state) + 1, False, s[2] + list(toks)


def weave(main, filler, per, owed=0.0):
    while True:
        while owed >= 1.0:
            owed -= 1.0
            next(filler, None)
        if next(main, main) is main:
            break
        owed += per
    for _ in filler:
        pass


def run(steps):
    for _ in steps:
        pass


def build(nc, A, out, dumps=None, stop=None):
    dumps = dumps or {}
    ctx = ExitStack()
    with ctx:
        arena = ctx.enter_context(nc.sbuf_tensor("arena", [128, 53200], F32))
        psum = ctx.enter_context(nc.psum_tensor("psum", [128, 4096], F32))
        nsem = [0]

        def sem(name=None):
            nsem[0] += 1
            return ctx.enter_context(nc.semaphore(name or f"s{nsem[0]}"))

        PE, DVE, AC, PL, SP = (Engine(sem("s_" + n)) for n in ("pe", "dve", "act", "pool", "sp"))
        ENG = [PE, DVE, AC, PL]

        def sb(a, n):
            return arena[:, a:a + n]

        def r3(ap, n):
            return ap.rearrange("p (a b) -> p a b", b=n)

        top = [0]

        def place(n):
            a = top[0]
            top[0] += n
            assert top[0] <= 53200, top[0]
            return sb(a, n)

        at = A["at"]
        cplace = {}

        def con_load(group, ap):
            a, b = at[group]
            for name, (x0, x1) in at.items():
                if len(name) > 1 and a <= x0 and x1 <= b:
                    cplace[name] = ap[:, x0 - a:x1 - a]
            return A["consts"][:, a:b]

        def con(name):
            return cplace[name]

        NA_ = at["a"][1]
        consts = place(NA_)
        csrc = con_load("a", consts)
        ident, ones = con("ident"), con("ones")
        NW = 5
        WR = place(NW * WSLOT)
        cvT = place(256)
        vecs = place(128 + 120 + 112 + 3 * 88)
        vmain, vcw, vcb = vecs[:, 0:128], vecs[:, 128:248], vecs[:, 248:360]
        vcw2 = vecs[:, 360:624]
        modc = place(64)
        small = place(256)
        BASE = top[0]

        banks = [psum[:, 512 * i:512 * i + 512] for i in range(8)]
        PALL = Ring(banks)
        PA = Ring(banks, [3, 4, 5, 6, 7], PALL.state)
        PG_ = Ring(banks, [0, 1, 2], PALL.state)
        cur = [PALL]

        class PS:
            take = staticmethod(lambda: cur[0].take())
            release = staticmethod(lambda k, *t: cur[0].release(k, *t))

        def using(ring, steps):
            it = iter(steps)
            while True:
                old, cur[0] = cur[0], ring
                try:
                    next(it)
                except StopIteration:
                    return
                finally:
                    cur[0] = old
                yield

        wslots = [WR[:, i * WSLOT:(i + 1) * WSLOT] for i in range(NW)]
        wsems = [sem(f"s_w{i}") for i in range(8)]
        wcount = [0] * 8
        W = Ring(wslots)

        def mm(o, l, r, start, stop_, *waits, signal=False):
            return PE.op(lambda e: e.matmul(o, l, r, start=start, stop=stop_), *waits, signal=signal)

        def tr(o, i, *waits, signal=False):
            k = i.shape[0]
            return PE.op(lambda e: e.transpose(o, i, ident[0:k, 0:k]), *waits, signal=signal)

        def dma(eng, o, i, *waits, s=None):
            if s is None:
                s = [sem(), 0]
            s[1] += 16
            eng.need(waits)
            eng.todo.append(lambda e: e.dma_start(o, i).then_inc(s[0], 16))
            return (s[0], s[1])

        def tt(E, o, a, b, op, *waits):
            return E.op(lambda e: e.tensor_tensor(o, a, b, op), *waits)

        def ts(E, o, a, s1, op0, *waits, s2=None, op1=None):
            if op1 is None:
                return E.op(lambda e: e.tensor_scalar(o, a, s1, None, op0), *waits)
            return E.op(lambda e: e.tensor_scalar(o, a, s1, s2, op0, op1), *waits)

        def stt(o, a, s, b, op0, op1, *waits):
            return DVE.op(lambda e: e.scalar_tensor_tensor(out=o, in0=a, scalar=s, in1=b, op0=op0, op1=op1), *waits)

        def act(o, i, f, *waits, bias=0.0, scale=1.0, acc=None):
            if acc is not None:
                return AC.op(lambda e: e.activation(o, i, f, bias=bias, scale=scale, accum_out=acc), *waits)
            return AC.op(lambda e: e.activation(o, i, f, bias=bias, scale=scale), *waits)

        def copy(E, o, i, *waits):
            if E is AC:
                return act(o, i, ACT.Copy, *waits)
            return E.op(lambda e: e.tensor_copy(o, i), *waits)

        def zero(E, o, *waits):
            return E.op(lambda e: e.memset(o, 0.0), *waits)

        def recip(o, i, *waits):
            return DVE.op(lambda e: e.reciprocal(o, i), *waits)

        def reduce_(o, i, op, *waits, negate=None):
            return DVE.op(lambda e: e.tensor_reduce(o, i, AX.X, op, negate=negate), *waits)

        def latest():
            return [(E.sem, E.count) for E in ENG]

        def bc(ap, n):
            return ap.unsqueeze(2).to_broadcast([ap.shape[0], ap.shape[1], n])

        def rep(ap, n):
            return ap.unsqueeze(1).to_broadcast([ap.shape[0], n, ap.shape[1]])

        def wload(parts, *waits):
            k, buf, w = W.take()
            SP.need([w, list(waits)])
            for dst, src in parts(buf):
                wcount[k] += 16
                SP.todo.append(lambda e, d=dst, s=src, k=k: e.dma_start(d, s).then_inc(wsems[k], 16))
            return k, buf, (wsems[k], wcount[k])

        def wblock(src, r0, nk, c0, n):
            def parts(buf):
                d = r3(buf[:, 0:nk * n], n)
                return [(d, src[r0:r0 + 128 * nk, c0:c0 + n].rearrange("(k p) n -> p k n", p=128))]
            k, buf, tok = wload(parts)
            return k, r3(buf[:, 0:nk * n], n), tok, nk

        def wcols(src, rows, c0, n):
            nk = rows // 128
            return [wblock(src, r0 * 128, min(4, nk - r0), c0, n) for r0 in range(0, nk, 4)]

        def wcols_later(src, rows, c0, n):
            nk = rows // 128
            return [(src, r0 * 128, min(4, nk - r0), c0, n) for r0 in range(0, nk, 4)]

        def gemm_steps(blocks, outs, stat, mov, evac, *waits):
            nkt = sum(x[3] for x in blocks)
            for n, i in enumerate(outs):
                b, bank, free = PS.take()
                kt = 0
                for k, w, tok, nk in blocks:
                    for j in range(nk):
                        o, l, r = shape_mm(bank, stat(i, kt, w[:, j, :]), mov(i, kt, w[:, j, :]))
                        last = mm(o, l, r, kt == 0, kt == nkt - 1, free, tok, list(waits),
                                  signal=(kt == nkt - 1 or (n == len(outs) - 1 and j == nk - 1)))
                        kt += 1
                    if n == len(outs) - 1:
                        W.release(k, last)
                PS.release(b, evac(i, o, last))
                yield

        def gemm(*a):
            run(gemm_steps(*a))

        def shape_mm(bank, l, r):
            m = l.shape[1]
            n = 1
            for d in r.shape[1:]:
                n *= d
            return bank[0:m, 0:n], l, r

        def chunked(blocks, outs, stat, mov, evac, per, *waits):
            opened = {}
            nkt = sum(x[2] for x in blocks)
            kt0 = 0
            for g in range(0, len(blocks), per):
                part = [wblock(*x) for x in blocks[g:g + per]]
                nk_part = sum(x[3] for x in part)
                for n, i in enumerate(outs):
                    if i not in opened:
                        opened[i] = PS.take()
                    b, bank, free = opened[i]
                    kt = kt0
                    for k, w, tok, nk in part:
                        for j in range(nk):
                            o, l, r = shape_mm(bank, stat(i, kt, w[:, j, :]), mov(i, kt, w[:, j, :]))
                            fin = kt == nkt - 1
                            last = mm(o, l, r, kt == 0, fin, free, tok, list(waits),
                                      signal=fin or (n == len(outs) - 1 and j == nk - 1))
                            kt += 1
                        if n == len(outs) - 1:
                            W.release(k, last)
                    if kt == nkt:
                        PS.release(b, evac(i, o, last))
                kt0 += nk_part

        def evac2(n):
            return AC if n % 2 else DVE

        tmods = []

        def rstd(v, n, *waits, mean=1024.0):
            s = small[:, 0:n]
            s2 = small[:, 64:64 + n]
            t = ts(DVE, v, v, 1.0 / mean, ALU.mult, list(waits), s2=EPS, op1=ALU.add)
            t = act(s, v, ACT.Ln, t)
            t = act(s, s, ACT.Exp, t, scale=-0.5)
            t = tt(DVE, s2, s, v, ALU.mult, t)
            t = tt(DVE, s2, s2, s, ALU.mult, t)
            t = ts(DVE, s2, s2, -0.5, ALU.mult, t, s2=1.5, op1=ALU.add)
            return tt(DVE, v, s, s2, ALU.mult, t)

        def normed_rows(src, nt, junk, xn, ssq, *waits):
            tq = list(waits)
            for i in range(nt):
                tq = [act(junk[:, 0:1024], src[:, i, :], ACT.Square, tq, acc=ssq[:, i:i + 1])]
            t = rstd(ssq[:, 0:nt], nt, tq)
            return [ts(DVE if i % 2 else PL, xn[:, i, :], src[:, i, :], ssq[:, i:i + 1], ALU.mult, t) for i in range(nt)]

        def turned(nt, HTd, xn, tx, scale_of, shift_of):
            done = []
            for j in range(8):
                b, bank, free = PS.take()
                for i in range(nt):
                    last = tr(bank[:, i * 128:(i + 1) * 128], xn[:, i, j * 128:(j + 1) * 128], free, tx[i],
                              signal=(i == nt - 1))
                s1, s2 = scale_of(j), shift_of(j)
                if j % 2:
                    if s2 is None:
                        t = act(HTd[:, j, :], bank[:, 0:nt * 128], ACT.Copy, last, tmods, scale=s1)
                    else:
                        t = act(HTd[:, j, :], bank[:, 0:nt * 128], ACT.Identity, last, tmods, scale=s1, bias=s2)
                elif s2 is None:
                    t = ts(DVE, HTd[:, j, :], bank[:, 0:nt * 128], s1, ALU.mult, last)
                else:
                    t = ts(DVE, HTd[:, j, :], bank[:, 0:nt * 128], s1, ALU.mult, last, tmods, s2=s2, op1=ALU.add)
                PS.release(b, t)
                done.append(t)
            return done

        xT = A["x"].rearrange("a (t p) d -> p (a t) d", p=128)
        HT = r3(sb(BASE, 6144), 768)
        PB = BASE + 6144
        spare = sb(PB, 1024)
        S0 = PB + 1024
        xin = r3(sb(S0, 4096), 1024)
        cin = r3(sb(S0 + 4096, 2048), 1024)
        xn = r3(sb(S0 + 6144, 6144), 1024)
        junk = sb(S0 + 12288, 1024)
        stage = sb(S0 + 13312, 6 * 128)
        setup = [dma(SP, consts, csrc)]
        z0 = zero(PL, stage)
        zc = zero(PL, cvT)
        dsem = [sem("s_vec"), 0]

        def vec(col, r, ap, n):
            return dma(AC, stage[r:r + n, col * 128:(col + 1) * 128], ap, z0, s=dsem)

        one = lambda ap: ap.rearrange("a (n p) -> (a n) p", p=128)
        vl = [
            (0, 0, one(A["b_ada"]), 48), (0, 48, one(A["norm_pre_mix"]), 8), (0, 56, one(A["norm_pre_ffn"]), 8),
            (0, 64, one(A["ssd_norm"]), 16), (0, 80, one(A["g_mix_2"]), 16), (0, 96, one(A["g_ffn_2"]), 16),
            (0, 112, one(A["c"]), 8), (0, 120, A["c_ctx"].rearrange("(n p) -> n p", p=128), 8),
            (1, 0, A["ssd_conv_w"].rearrange("a j (n p) -> (a j n) p", p=128), 120),
            (2, 0, one(A["ssd_conv_b"]), 24), (2, 24, one(A["conv_b_2"]), 88),
        ]
        cw2 = A["conv_w_2"].rearrange("a j (n p) -> (a j n) p", p=128)
        for i in range(3):
            vl.append((3 + i, 0, cw2[88 * i:88 * i + 88, :], 88))
        for col, r, ap, n in vl:
            tv = vec(col, r, ap, n)
        tx = dma(AC, xin, xT)
        tc_ = dma(AC, cin, A["ctx"].rearrange("a (t p) d -> p (a t) d", p=128))
        dst = [(vmain, 128), (vcw, 120), (vcb, 112)] + [(vcw2[:, 88 * i:88 * i + 88], 88) for i in range(3)]
        tvec = []
        for i, (d, n) in enumerate(dst):
            b, bank, free = PS.take()
            t = tr(bank[:, 0:128], stage[:, i * 128:(i + 1) * 128], free, tv, setup, signal=True)
            t = copy(DVE, d, bank[:, 0:n], t)
            PS.release(b, t)
            tvec.append(t)
        bada = vmain[:, 0:48]
        gpm, gpf, gssd = vmain[:, 48:56], vmain[:, 56:64], vmain[:, 64:80]
        gmix2, gffn2 = vmain[:, 80:96], vmain[:, 96:112]
        cv3 = r3(cvT, 32)
        act(cv3[:, :, 0], vmain[:, 112:120], ACT.Silu, tvec[0], zc)
        t2 = act(cv3[:, :, 1], vmain[:, 120:128], ACT.Silu, tvec[0])

        bc1 = lambda ap: ap.rearrange("a n -> (a n)").partition_broadcast(128)
        sel = con("sel")

        def ada_product(c0, ring):
            blocks = wcols(A["w_ada"], 1024, c0, 512)
            b, bank, free = PS.take()
            for kt in range(8):
                blk = blocks[kt // 4]
                g = kt % 3
                lt = mm(bank[32 * g:32 * g + 32, :], cv3[:, kt, :], blk[1][:, kt % 4, :], kt < 3, kt > 4, free, blk[2], t2,
                        signal=(kt % 4 == 3))
                if kt % 4 == 3:
                    W.release(blk[0], lt)
            k, r, f = ring.take()
            t = copy(DVE, r[0:96, :], bank[0:96, :], lt, f)
            PS.release(b, t)
            return k, r, t

        def ada_cols(ci, chunk, ring):
            for half in range(2):
                k, r, t = ada_product(chunk * 1024 + half * 512, ring)
                b, bank, free = PS.take()
                for i in range(4):
                    lt = mm(bank[:, 2 * i:2 * i + 2], r[0:96, i * 128:(i + 1) * 128], sel[0:96, :], True, True, free, t, setup,
                            signal=(i == 3))
                ring.release(k, lt)
                j = chunk * 8 + half * 4
                t = tt(DVE, r3(modc[:, ci * 16 + half * 8:ci * 16 + half * 8 + 8], 2), r3(bank[:, 0:8], 2), bc(bada[:, j:j + 4], 2),
                       ALU.add, lt)
                PS.release(b, t)
                yield

        gamD = nc.dram_tensor("gam_scratch", [2, 1024], F32, kind="Internal").ap()
        tgam = []

        def ada_rows(ring):
            gs = [sem("s_grow"), 0]
            for gi, (chunk, nrm) in enumerate(((2, A["norm_post_mix"]), (5, A["norm_post_ffn"]))):
                for half in range(2):
                    c0 = chunk * 1024 + half * 512
                    k1, r1, f1 = ring.take()
                    k2, r2, f2 = ring.take()
                    dma(AC, r1[0:1, :], A["b_ada"][:, c0:c0 + 512], f1, s=gs)
                    tl = dma(AC, r2[0:1, :], nrm[:, half * 512:half * 512 + 512], f2, s=gs)
                    k, r, t = ada_product(c0, ring)
                    b, bank, free = PS.take()
                    lt = mm(bank[0:1, :], sel[0:96, 0:1], r[0:96, :], True, True, free, t, signal=True)
                    ring.release(k, lt)
                    t = tt(DVE, r1[0:1, :], bank[0:1, :], r1[0:1, :], ALU.add, lt, tl)
                    PS.release(b, t)
                    t = tt(DVE, r1[0:1, :], r1[0:1, :], r2[0:1, :], ALU.mult, t)
                    tgam.append(dma(AC, gamD[gi:gi + 1, half * 512:half * 512 + 512], r1[0:1, :], t))
                    ring.release(k1, tgam[-1])
                    ring.release(k2, t)
                    yield

        mc = modc.rearrange("p (c j w) -> p c j w", c=4, w=2)

        def ada_scale(ci, g):
            t0 = (DVE.sem, DVE.count)
            return [stt(mc[:, ci, :, w_], mc[:, ci, :, w_], 1.0, g, ALU.add, ALU.mult, t0) for w_ in range(2)]

        r0 = Ring([sb(S0 + 14080 + 512 * i, 512) for i in range(2)])
        run(ada_cols(0, 0, r0))
        ssq = small[:, 128:144]
        txn = normed_rows(xin, 4, junk, xn, ssq[:, 0:4], tx)
        tcn = normed_rows(cin, 2, junk, xn[:, 4:6, :], ssq[:, 4:6], tc_, txn)
        run(ada_cols(1, 1, r0))
        tmods += ada_scale(1, gpm)

        def ada_rest(ring):
            yield from ada_cols(2, 3, ring)
            yield from ada_cols(3, 4, ring)
            ada_scale(3, gpf)
            yield from ada_rows(ring)

        tH = turned(4, HT[:, :, 0:512], xn, txn, lambda j: mc[:, 1, j, 0:1], lambda j: mc[:, 0, j, 0:1])
        tH += turned(2, HT[:, :, 512:768], xn[:, 4:6, :], tcn, lambda j: mc[:, 1, j, 1:2], lambda j: mc[:, 0, j, 1:2])
        tdump = []
        tyD = []

        def dump(name, ap, *waits):
            if name in dumps:
                tdump.append(dma(SP, dumps[name], ap, latest(), list(waits)))
                for E in ENG:
                    E.need([tdump[-1]])

        dump("HT", HT)

        def dram(name, shape):
            return nc.dram_tensor(name, shape, F32, kind="Internal").ap()

        if stop != "B":
            yD = dram("yT_scratch", [128, 16, 512])
            acsD = dram("acs_scratch", [64, 512])
            tb = latest()
            o = S0

            def bufs(n, w):
                nonlocal o
                r = [sb(o + w * i, w) for i in range(n)]
                o += n * w
                return r

            xs0 = bufs(1, 3072)[0]
            pads = Ring(bufs(2, 776))
            accs = Ring(bufs(1, 772))
            xsF = Ring(bufs(1, 768) + [spare[:, 0:768]])
            bt0 = bufs(1, 768)[0]
            zs0 = bufs(1, 2048)[0]
            FREE = o
            BF = r3(bufs(1, 3072)[0], 768)
            CF = r3(bufs(1, 2048)[0], 512)
            BT2 = [r3(x_, 128) for x_ in [bt0] + bufs(1, 768)]
            xs2 = [r3(x_, 512) for x_ in [xs0] + bufs(1, 3072)]
            hf, hb = (r3(x_, 512) for x_ in bufs(2, 2048))
            zs2 = [r3(x_, 512) for x_ in [zs0] + bufs(1, 2048)]
            yTr = Ring(bufs(1, 512))
            RBr = Ring(bufs(2, 512))
            Er = Ring(bufs(4, 512))
            XD = Ring(bufs(4, 512))
            TY = Ring(bufs(3, 512))
            cbr = Ring(bufs(2, 256))
            dt, acs, eac, wst, cdec = bufs(5, 384)
            rows64 = bufs(1, 160)[0]
            assert o <= 53200, o
            d1, atot = XD.bufs[0][:, 0:384], XD.bufs[1][:, 0:384]
            tz = []
            for p_ in pads.bufs:
                for a, b in ((0, 2), (514, 518), (774, 776)):
                    tz.append(zero(DVE, p_[:, a:b], tb))
            dtb, nA, dsk = rows64[:, 0:64], rows64[:, 64:128], rows64[:, 128:160]
            rs = [sem("s_rows"), 0]
            for d, ap in ((dtb[:, 0:32], A["ssd_dt_bias_fwd"]), (dtb[:, 32:64], A["ssd_dt_bias_bwd"]),
                          (nA[:, 0:32], A["ssd_a_log_fwd"]), (nA[:, 32:64], A["ssd_a_log_bwd"]), (dsk, A["ssd_d_skip"])):
                tr_ = dma(AC, d, bc1(ap), tb, s=rs)
            ac3 = r3(acs, 64)
            T = {}
            rp = dram("rpb_copies", [16, 64, 465])
            rpb = A["na_rpb"]
            trp = dma(AC, rp, bass.AP(rpb.tensor, 0, [[465, 16], [0, 64], [1, 465]]))

            def steps_dt():
                t = act(nA, nA, ACT.Exp, tr_)
                tnA = ts(DVE, nA, nA, -1.0, ALU.mult, t)
                blk = wblock(A["w_in"], 0, 8, CDT, 64)
                b, bank, free = PS.take()
                for i in range(6):
                    for kt in range(8):
                        last = mm(bank[:, i * 64:(i + 1) * 64], HT[:, kt, i * 128:(i + 1) * 128], blk[1][:, kt, :],
                                  kt == 0, kt == 7, free, blk[2], tH, signal=(i == 5 and kt == 7))
                W.release(blk[0], last)
                raw = dt
                t = tt(DVE, r3(raw, 64), r3(bank[:, 0:384], 64), rep(dtb, 6), ALU.add, last, tr_, tb)
                PS.release(b, t)
                yield
                t = stt(d1, raw, -1.0, raw, ALU.mult, ALU.max, t)
                t = act(acs, d1, ACT.Exp, t, scale=-1.0)
                t = ts(DVE, d1, acs, 1.0, ALU.add, t)
                tl = act(eac, d1, ACT.Ln, t)
                t = ts(DVE, atot, d1, -1.0, ALU.add, t)
                t = tt(DVE, acs, acs, atot, ALU.subtract, t)
                t = recip(d1, d1, t, tl)
                t = tt(DVE, acs, acs, d1, ALU.mult, t)
                t = tt(DVE, acs, acs, eac, ALU.add, t, tl)
                T["dt"] = stt(dt, raw, 0.0, acs, ALU.max, ALU.add, t)
                a_ = d1
                ta_ = tt(DVE, r3(a_, 64), r3(dt, 64), rep(nA, 6), ALU.mult, T["dt"], tnA)
                a3 = r3(a_, 64)
                yield
                b, bank, free = PS.take()
                mm(bank[:, 0:192], con("ule"), a3[:, :, 0:32], True, True, free, ta_)
                last = mm(bank[:, 192:384], con("uge"), a3[:, :, 32:64], True, True, signal=True)
                t = copy(DVE, ac3[:, :, 0:32], r3(bank[:, 0:192], 32), last)
                tac = T["ac"] = copy(DVE, ac3[:, :, 32:64], r3(bank[:, 192:384], 32), last)
                PS.release(b, tac)
                b, bank, free = PS.take()
                last = mm(bank[:, 0:384], ones, a_, True, True, free, signal=True)
                tat = copy(DVE, atot, bank[:, 0:384], last)
                PS.release(b, tat)
                T["cd"] = act(cdec, atot, ACT.Exp, tat)
                XD.release(1, T["cd"])
                T["ea"] = act(eac, acs, ACT.Exp, tac)
                t = tt(DVE, wst, atot, acs, ALU.subtract, tat, tac)
                t = act(wst, wst, ACT.Exp, t)
                T["ws"] = tt(DVE, wst, wst, dt, ALU.mult, t)
                yield
                acT = TY.bufs[0][0:64, :]
                b, bank, free = PS.take()
                for i in range(4):
                    last = tr(bank[0:64, i * 128:(i + 1) * 128], ac3[:, i, :], free, tac, signal=(i == 3))
                t = copy(DVE, acT, bank[0:64, 0:512], last)
                PS.release(b, t)
                T["acD"] = dma(AC, acsD, acT, t)
                TY.release(0, T["acD"])

            def conv_tile(blocks, i, ti, dx, dc, *dwaits):
                b1, k1, f1 = PS.take()
                for kt in range(8):
                    blk = blocks[kt // 4]
                    last1 = mm(k1[:, 0:512], blk[1][:, kt % 4, i * 128:(i + 1) * 128], HT[:, kt, 0:512],
                               kt == 0, kt == 7, f1, blk[2], tH, signal=(kt == 7))
                b2, k2, f2 = PS.take()
                for kt in range(8):
                    blk = blocks[kt // 4]
                    last2 = mm(k2[:, 0:256], blk[1][:, kt % 4, i * 128:(i + 1) * 128], HT[:, kt, 512:768],
                               kt == 0, kt == 7, f2, signal=(kt == 7))
                pk, pad, pf = pads.take()
                c1 = copy(AC, pad[:, 2:514], k1[:, 0:512], last1, pf, tz)
                c2 = copy(AC, pad[:, 518:774], k2[:, 0:256], last2)
                PS.release(b1, c1)
                PS.release(b2, c2)
                ak, ac_, af = accs.take()
                w5 = lambda j: vcw[:, j * 24 + ti:j * 24 + ti + 1]
                t = ts(DVE, ac_, pad[:, 0:772], w5(0), ALU.mult, c1, c2, af)
                for j in range(1, 5):
                    t = stt(ac_, pad[:, j:j + 772], w5(j), ac_, ALU.mult, ALU.add, t)
                pads.release(pk, t)
                bias = vcb[:, ti:ti + 1]
                s1 = act(dx, ac_[:, 0:512], ACT.Silu, t, list(dwaits), bias=bias)
                s2 = s1
                if dc is not None:
                    s2 = act(dc, ac_[:, 516:772], ACT.Silu, bias=bias)
                accs.release(ak, s2)
                return s2, last2

            def steps_bc():
                for name, c0, t0_ in (("BF", CB, 16), ("CF", CC, 20)):
                    blocks = wcols(A["w_in"], 1024, c0, 512)
                    T[name] = []
                    for g in range(4):
                        F_ = BF if name == "BF" else CF
                        t, last = conv_tile(blocks, g, t0_ + g, F_[:, g, 0:512], BF[:, g, 512:768] if name == "BF" else None, tb)
                        T[name].append(t)
                        if g < 3:
                            yield
                    for x_ in blocks:
                        W.release(x_[0], last)
                    yield

            done = {}
            gone = {}

            def steps_proj(g):
                xsT, zs, BT = xs2[g % 2], zs2[g % 2], BT2[g % 2]
                before = gone.get(g - 2, tb)
                blocks = wcols(A["w_in"], 1024, CX + 512 * g, 512)
                txs = T["xs", g] = []

                def turn_x(i, k, xf, t):
                    for part, n in ((0, 4), (4, 2)):
                        b, bank, free = PS.take()
                        for c in range(n):
                            lt = tr(bank[:, c * 128:(c + 1) * 128], xf[:, (part + c) * 128:(part + c + 1) * 128], free, t,
                                    signal=(c == n - 1))
                        e = copy(AC if part else DVE, xsT[:, part:part + n, i * 128:(i + 1) * 128], r3(bank[:, 0:n * 128], 128), lt, before)
                        PS.release(b, e)
                        txs.append(e)
                    xsF.release(k, lt)

                late = None
                for i in range(4):
                    k, xf, f = xsF.take()
                    t, last = conv_tile(blocks, i, 4 * g + i, xf[:, 0:512], xf[:, 512:768], f)
                    if i == 3:
                        for x_ in blocks:
                            W.release(x_[0], last)
                    if late:
                        turn_x(*late)
                    late = (i, k, xf, t)
                    yield
                tbt = T["bt", g] = []
                for part, n in ((0, 4), (4, 2)):
                    b, bank, free = PS.take()
                    for c in range(n):
                        lt = tr(bank[:, c * 128:(c + 1) * 128], BF[:, g, (part + c) * 128:(part + c + 1) * 128], free,
                                T["BF"][g], signal=(c == n - 1))
                    e = copy(DVE, BT[:, part:part + n, :], r3(bank[:, 0:n * 128], 128), lt, before)
                    PS.release(b, e)
                    tbt.append(e)
                blocks = wcols(A["w_in"], 1024, CZ + 512 * g, 512)
                tzs = T["zs", g] = []

                def ev(i, o_, tok):
                    t = act(zs[:, i, :], o_, ACT.Silu, tok, before, done.get(g - 2))
                    tzs.append(t)
                    if i == 1:
                        turn_x(*late)
                    return t
                yield from gemm_steps(blocks, range(4), lambda i, kt, w: HT[:, kt, i * 128:(i + 1) * 128], lambda i, kt, w: w, ev, tH)

            rbs = [[sem(f"s_rb{i}"), 0] for i in range(2)]
            ysem = [[sem(f"s_yD{i}"), 0] for i in range(1)]

            def steps_chunks(g):
                xsT, zs, BT = xs2[g % 2], zs2[g % 2], BT2[g % 2]
                txs, tbt, tzs = T["xs", g], T["bt", g], T["zs", g]
                before = gone.get(g - 1, tb)
                items = [(c, hq, d) for c in range(4) for hq in range(2) for d in range(2)]
                loaded = []

                def load_rows():
                    n = len(loaded)
                    if n < len(items):
                        c, hq, d = items[n]
                        h0 = 8 * g + 4 * hq
                        rk, rb, rf = RBr.take()
                        srcr = acsD[32 * d + h0:32 * d + h0 + 4, c * 128:(c + 1) * 128]
                        td = dma(AC, r3(rb, 128), srcr.partition_broadcast(128), rf, T["acD"], s=rbs[rk])
                        loaded.append((rk, rb, td))
                for _ in range(2):
                    load_rows()

                sweep = [(d, n, ((4, 5, 0, 1, 2), (5, 4, 3, 2, 1))[d][n]) for n in range(5) for d in range(2)]
                ahead = []

                def weigh():
                    m_ = len(ahead)
                    if m_ < len(sweep):
                        d, n, c = sweep[m_]
                        k, xd, f = XD.take()
                        wv = r3(wst, 64)[:, c, 32 * d + 8 * g:32 * d + 8 * g + 8]
                        ahead.append((k, xd, tt(PL if m_ % 2 else DVE, r3(xd, 64), r3(xsT[:, c, :], 64), bc(wv, 64), ALU.mult,
                                                f, txs, T["ws"])))
                for _ in range(3):
                    weigh()
                tst = [None, None]
                for m_, (d, n, c) in enumerate(sweep):
                    weigh()
                    H_ = (hf, hb)[d]
                    slots = ((0, 0, 1, 2, 3), (3, 3, 2, 1, 0))[d]
                    k, xd, tx_ = ahead[m_]
                    b, bank, free = PS.take()
                    lt = mm(bank, BT[:, c, :], xd, True, True, free, tbt, tx_, signal=True)
                    XD.release(k, lt)
                    dstn = H_[:, slots[n], :]
                    if n == 0:
                        t = copy(DVE, dstn, bank, lt, before)
                    else:
                        srcn = H_[:, slots[n - 1], :]
                        cd = bc(r3(cdec, 64)[:, c, 32 * d + 8 * g:32 * d + 8 * g + 8], 64)
                        t = tt(DVE, r3(dstn, 64), r3(srcn, 64), cd, ALU.mult, tst[d], T["cd"])
                        t = tt(DVE, dstn, dstn, bank, ALU.add, t, lt)
                    tst[d] = t
                    PS.release(b, t)
                    if d:
                        if n == 0 and g:
                            scale_z(g - 1)
                        if n == 2 and g:
                            finish(g - 1)
                        yield
                th_ = tst

                st = {}
                ssy = small[:, 160:164]
                tus = []

                def first(n):
                    c, hq, _ = items[2 * n]
                    cs_ = slice(c * 128, (c + 1) * 128)
                    if hq == 0:
                        b, bank, free = PS.take()
                        lt = mm(bank[:, 0:128], BF[:, g, cs_], CF[:, g, cs_], True, True, free, T["BF"][g], T["CF"][g], signal=True)
                        ck, cb, cf = cbr.take()
                        t1_ = tt(DVE, cb[:, 0:128], bank[:, 0:128], con("ule"), ALU.mult, lt, cf)
                        t2_ = tt(DVE, cb[:, 128:256], bank[:, 0:128], con("uge"), ALU.mult, lt)
                        PS.release(b, t2_)
                        xd2 = []
                        for d in range(2):
                            k, xd, f = XD.take()
                            dv = r3(dt, 64)[:, c, 32 * d + 8 * g:32 * d + 8 * g + 8]
                            t = tt(PL, r3(xd, 64), r3(xsT[:, c, :], 64), bc(dv, 64), ALU.mult, f, txs, T["dt"])
                            xd2.append((k, xd, t))
                        st[c] = dict(cb=(ck, cb, [t1_, t2_]), xd=xd2)
                    M = []
                    for d in range(2):
                        h0 = 8 * g + 4 * hq
                        rk, rb, td = loaded[2 * n + d]
                        for h in range(4):
                            colv = ac3[:, c, 32 * d + h0 + h:32 * d + h0 + h + 1]
                            r_ = rb[:, h * 128:(h + 1) * 128]
                            t = ts(DVE, r_, r_, colv, ALU.subtract, td, T["ac"], s2=0.0, op1=ALU.min)
                        ek, eb, ef = Er.take()
                        t = act(eb, rb, ACT.Exp, t, ef)
                        RBr.release(rk, t)
                        load_rows()
                        cbd = st[c]["cb"][1][:, 128 * d:128 * d + 128]
                        tm = tt(DVE if d else PL, r3(eb, 128), r3(eb, 128), rep(cbd, 4), ALU.mult, t, st[c]["cb"][2])
                        M.append((ek, r3(eb, 128), tm))
                    if hq == 1:
                        cbr.release(st[c]["cb"][0], tm)
                    st[c, hq] = M

                def second(n):
                    c, hq, _ = items[2 * n]
                    cs_ = slice(c * 128, (c + 1) * 128)
                    M, xd2 = st[c, hq], st[c]["xd"]
                    if hq == 0:
                        st[c]["y"] = PS.take()
                    yb, ybank, yfree = st[c]["y"]
                    for h in range(4):
                        hh = 4 * hq + h
                        for d in range(2):
                            ek, eb, tm = M[d]
                            lt = mm(ybank[:, hh * 64:hh * 64 + 64], eb[:, h, :], xd2[d][1][:, hh * 64:hh * 64 + 64],
                                    d == 0, d == 1, yfree, tm, xd2[d][2], signal=(h == 3 and d == 1))
                    for d in range(2):
                        Er.release(M[d][0], lt)
                    if hq == 0:
                        return
                    for k, _, _ in xd2:
                        XD.release(k, lt)
                    tyd = lt
                    ty = []
                    for d, H_ in ((0, hf), (1, hb)):
                        b, bank, free = PS.take()
                        lt = mm(bank, CF[:, g, cs_], H_[:, c, :], True, True, free, T["CF"][g], th_[d], signal=True)
                        k, tb1, f = TY.take()
                        ev_ = bc(r3(eac, 64)[:, c, 32 * d + 8 * g:32 * d + 8 * g + 8], 64)
                        t = tt(DVE, r3(tb1, 64), r3(bank, 64), ev_, ALU.mult, lt, T["ea"], f)
                        PS.release(b, t)
                        ty.append((k, tb1, t))
                    k, tb2, f = TY.take()
                    t2_ = tt(PL, r3(tb2, 64), r3(xsT[:, c, :], 64), bc(dsk[:, 8 * g:8 * g + 8], 64), ALU.mult, f, txs, tr_)
                    t = tt(PL, ty[0][1], ty[0][1], ty[1][1], ALU.add, ty[0][2], ty[1][2])
                    t3 = tt(PL, ty[0][1], ty[0][1], tb2, ALU.add, t, t2_)
                    t4 = tt(DVE, ty[0][1], ybank, ty[0][1], ALU.add, t3, tyd)
                    PS.release(yb, t4)
                    if g == 0:
                        dump(f"y{c}", ty[0][1], t4)
                    t5 = tt(DVE, zs[:, c, :], zs[:, c, :], ty[0][1], ALU.mult, t4, tzs)
                    TY.release(ty[0][0], t5)
                    TY.release(ty[1][0], t)
                    t6 = act(tb2, zs[:, c, :], ACT.Square, t5, t3, acc=ssy[:, c:c + 1])
                    TY.release(k, t6)
                    tus.append(t6)

                for n in range(10):
                    if n >= 2:
                        second(n - 2)
                    if n < 8:
                        first(n)
                    yield
                T["us", g] = tus
                gone[g] = latest()
                if g == 3:
                    scale_z(g)
                    finish(g)

            def scale_z(g):
                zs = zs2[g % 2]
                t = rstd(small[:, 160:164], 4, T["us", g], mean=512.0)
                ssy = small[:, 160:164]
                T["n", g] = [ts(PL if c % 2 else DVE, zs[:, c, :], zs[:, c, :], ssy[:, c:c + 1], ALU.mult, t) for c in range(4)]

            def finish(g):
                zs, tn = zs2[g % 2], T["n", g]
                for i in range(4):
                    b, bank, free = PS.take()
                    for c in range(4):
                        lt = tr(bank[:, c * 128:(c + 1) * 128], zs[:, c, i * 128:(i + 1) * 128], free, tn, signal=(c == 3))
                    k, yt, f = yTr.take()
                    t = act(yt, bank, ACT.Copy, lt, f, scale=gssd[:, 4 * g + i:4 * g + i + 1])
                    PS.release(b, t)
                    td = dma(AC, yD[:, 4 * g + i, :], yt, t, s=ysem[k])
                    yTr.release(k, td)
                    tyD[:] = [td]
                done[g] = latest()

            rest = ada_rest(Er)
            weave(using(PALL, steps_bc()), rest, 1)
            xsF.release(1, (PE.sem, PE.count))
            weave(using(PALL, steps_proj(0)), steps_dt(), 0.5)
            for g in range(3):
                weave(using(PA, steps_chunks(g)), using(PG_, steps_proj(g + 1)), 0.56)

        def attention(units, Sr, PTr):
            small_ring = Ring([small[:, 176 + 4 * i:180 + 4 * i] for i in range(8)])

            def scores(u):
                u["P"] = []
                for m in u["maps"]:
                    sk, S, sf = Sr.take()
                    vk, sv, vf = small_ring.take()
                    n = 0
                    td = []
                    for kp, kn, bias in m["keys"]:
                        b, bank, free = PS.take()
                        lt = mm(bank[:, 0:kn], m["q"], kp, True, True, free, u["qk"], signal=True)
                        if bias is None:
                            t = act(S[:, n:n + kn], bank[:, 0:kn], ACT.Copy, lt, sf, scale=u["scale"])
                        else:
                            bap, btok = bias()
                            t = stt(S[:, n:n + kn], bank[:, 0:kn], u["scale"], bap, ALU.mult, ALU.add, lt, sf, btok)
                            tbias = t
                        PS.release(b, t)
                        td.append(t)
                        n += kn
                    t = reduce_(sv[:, 0:1], S[:, 0:n], ALU.max, td, vf, negate=True)
                    t = act(S[:, 0:n], S[:, 0:n], ACT.Exp, t, bias=sv[:, 0:1], acc=sv[:, 1:2])
                    t = recip(sv[:, 1:2], sv[:, 1:2], t)
                    u["P"].append((sk, S, vk, sv, t, n))
                if "post" in u:
                    u["post"](tbias)
                if len(u["P"]) == 2:
                    (sk0, S0, vk0, sv0, t0, n), (sk1, S1, vk1, sv1, t1, _) = u["P"]
                    t = tt(DVE, sv1[:, 2:3], sv1[:, 1:2], u["nlam"], ALU.mult, t1)
                    t = ts(PL, S1[:, 0:n], S1[:, 0:n], sv1[:, 2:3], ALU.mult, t)
                    t = stt(S0[:, 0:n], S0[:, 0:n], sv0[:, 1:2], S1[:, 0:n], ALU.mult, ALU.add, t, t0)
                    Sr.release(sk1, t)
                    small_ring.release(vk1, t)
                    u["P"] = [(sk0, S0, vk0, sv0, t, n)]

            def turn(u, par):
                sk, S, vk, sv, t, n = u["P"][0]
                pk, PT, pf = PTr.take()
                te = []
                for a in range(0, n, 512):
                    m_ = min(512, n - a)
                    b, bank, free = PS.take()
                    for j in range(m_ // 128):
                        lt = tr(bank[:, j * 128:(j + 1) * 128], S[:, a + j * 128:a + (j + 1) * 128], free, t,
                                signal=(j == m_ // 128 - 1))
                    e = copy(AC if (a or par) else DVE, PT[:, a:a + m_], bank[:, 0:m_], lt, pf)
                    PS.release(b, e)
                    te.append(e)
                Sr.release(sk, lt)
                u["PT"] = (pk, PT, te)

            def values(u):
                sk, S, vk, sv, t, n = u["P"][0]
                pk, PT, te = u["PT"]
                b, bank, free = PS.take()
                nk = n // 128
                for j in range(nk):
                    lt = mm(bank[:, 0:64], PT[:, j * 128:(j + 1) * 128], u["v"](j), j == 0, j == nk - 1, free, te, u["vt"],
                            signal=(j == nk - 1))
                PTr.release(pk, lt)
                t2 = u["out"](bank[:, 0:64], lt, sv)
                PS.release(b, t2)
                small_ring.release(vk, t2)

            N = len(units)
            for i in range(N + 3):
                for u in units[0:5] if i == 0 else units[i + 4:i + 5]:
                    if "pre" in u:
                        u["pre"]()
                if 0 <= i - 2 < N:
                    turn(units[i - 2], i % 2)
                if 0 <= i - 3 < N:
                    values(units[i - 3])
                if i < N:
                    scores(units[i])
                yield

        def rope(blocks, i, late, cos, sin, rot, dests, tmp, waits, ttab):
            b1, k1, f1 = PS.take()
            for kt in range(8):
                blk = blocks[kt // 4]
                l1 = mm(k1[:, 0:512], blk[1][:, kt % 4, i * 128:(i + 1) * 128], HT[:, kt, 0:512], kt == 0, kt == 7,
                        f1, blk[2], waits, signal=(kt == 7))
            rk, (raw, tc1, tc2), rf = tmp.take()
            t = copy(AC, raw, k1[:, 0:512], l1, rf)
            PS.release(b1, t)
            tds = []

            def finish():
                b2, k2, f2 = PS.take()
                l2 = mm(k2[:, 0:512], rot, raw, True, True, f2, t, ttab, signal=True)
                ta1 = tt(PL, tc1, raw, cos, ALU.mult, t, ttab)
                tb1 = tt(DVE, tc2, k2[:, 0:512], sin, ALU.mult, l2, ttab)
                PS.release(b2, tb1)
                for a, z, d in dests:
                    E_ = PL if z - a == 128 else DVE
                    tds.append(tt(E_, d[a:z, :], tc1[a:z, :], tc2[a:z, :], ALU.add, ta1, tb1, waits))
                tmp.release(rk, tds, l2)
            while late:
                late.pop()()
            late.append(finish)
            return tds, l1

        def then_late(late, steps):
            for n, _ in enumerate(steps):
                if n == 0:
                    while late:
                        late.pop()()
                yield

        def more_slots(*at_):
            for i, a in enumerate(at_):
                W.bufs[NW + i:NW + i + 1] = [sb(a, WSLOT)]
                W.state[NW + i:NW + i + 1] = [[max(x[0] for x in W.state) + 1, False, latest()]]
            W.keys = list(range(NW + len(at_)))

        def fewer_slots():
            w = [W.state[k][2] for k in W.keys[NW:]]
            assert not any(W.state[k][1] for k in W.keys[NW:])
            W.keys = W.keys[:NW]
            return w

        if stop not in ("B", "C"):
            SB = PB + 5120 + 3072 + at["d"][1] - at["d"][0]
            assert SB <= FREE
            sets = []
            for o in (PB, SB):
                sets.append((r3(sb(o, 1536), 768), r3(sb(o + 1536, 2048), 512), r3(sb(o + 3584, 1536), 256)))
            tmp = Ring([tuple(sb(PB + 5120 + 1536 * i + 512 * j, 512) for j in range(3)) for i in range(2)])
            dcon = sb(PB + 8192, at["d"][1] - at["d"][0])
            yT = r3(sb(PB, 8192), 512)
            mix = r3(sb(PB, 4096), 1024)
            oT = r3(sb(SB, 4096), 512)
            o = SB + 5120
            uT = r3(sb(o, 4096), 512); o += 4096
            G = r3(sb(o, 2048), 512); o += 2048
            O = r3(sb(o, 4096), 1024); o += 4096
            tmpE = Ring([sb(o, 512), sb(o + 512, 512)]); o += 1024
            DSLOT = o
            o += WSLOT
            TOP = 53200 - 3 * WSLOT
            assert o <= TOP
            o = TOP
            biasr = Ring([sb(o + 896 * i, 896) for i in range(2)]); o += 1792
            Sr = Ring([sb(o + 768 * i, 768) for i in range(3)]); o += 2304
            PTr = Ring([sb(o + 768 * i, 768) for i in range(2)]); o += 1536
            assert o <= 53200, o
            bsem = [[sem(f"s_bias{i}"), 0] for i in range(2)]
            tcon = []
            over = {}
            tq, tk, tv_ = {}, {}, {}

            def na_proj(n):
                kF, qP, V = sets[n % 2]
                if n < 2:
                    assert n or 2 in done
                    over[n - 2] = latest()
                    over[n - 2].append(zero(PL, qP.rearrange("p a b -> p (a b)"), over[n - 2]))
                    if n == 0:
                        tcon.append(dma(AC, dcon, con_load("d", dcon), over[-2]))
                prev = over[n - 2]
                tq[n], tk[n], tv_[n] = [], [], []
                late = []
                blocks = wcols(A["w_in"], 1024, CQ + 256 * n, 256)
                for i in range(2):
                    tds, last = rope(blocks, i, late, con("nacos"), con("nasin"), con("rna"),
                                     [(0, 64, qP[:, 2 * i, :]), (64, 128, qP[:, 2 * i + 1, :])], tmp, [tH, prev], tcon)
                    tq[n].append(tds)
                    if i == 1:
                        for x_ in blocks:
                            W.release(x_[0], last)
                    yield
                blocks = wcols(A["w_in"], 1024, CK + 256 * n, 256)
                for i in range(2):
                    tds, last = rope(blocks, i, late, con("nacos"), con("nasin"), con("rna"), [(0, 128, kF[:, i, 0:512])], tmp, [tH, prev], tcon)
                    b2, k2, f2 = PS.take()
                    for kt in range(8):
                        blk = blocks[kt // 4]
                        last = mm(k2[:, 0:256], blk[1][:, kt % 4, i * 128:(i + 1) * 128], HT[:, kt, 512:768], kt == 0, kt == 7,
                                  f2, signal=(kt == 7))
                    t = copy(AC, kF[:, i, 512:768], k2[:, 0:256], last, prev)
                    PS.release(b2, t)
                    tk[n].append([tds, t])
                    if i == 1:
                        for x_ in blocks:
                            W.release(x_[0], last)
                    yield
                blocks = wcols(A["w_in"], 1024, CV + 256 * n, 256)

                def ev(i, o_, tok):
                    t = copy(evac2(i), V[:, i, :], o_, tok, prev)
                    tv_[n].append(t)
                    return t
                yield from then_late(late, gemm_steps(blocks, range(6), lambda i, kt, w: HT[:, kt, i * 128:(i + 1) * 128],
                                                      lambda i, kt, w: w, ev, tH))

            def na_attention(n):
                kF, qP, V = sets[n % 2]
                units = []
                for hl in range(4):
                    h = 4 * n + hl
                    st = {}

                    def pre(h=h, st=st):
                        k, bb, f = biasr.take()
                        for a in range(2):
                            base = h * 29760 + (1 - a) * 31 + 15
                            src = bass.AP(rp.tensor, base, [[464, 64], [31, 14], [1, 64]])
                            td = dma(AC, r3(bb[64 * a:64 * a + 64, :], 64), src, f, trp, s=bsem[k])
                        st["k"], st["b"] = k, bb
                        st["t"] = tt(PL, r3(bb, 64), r3(bb, 64), rep(con("colmask"), 14), ALU.add, td, tcon)

                    for qt in range(4):
                        def outf(ps, lt, sv, qt=qt, h=h):
                            return ts(DVE, O[:, qt, h * 64:(h + 1) * 64], ps, sv[:, 1:2], ALU.mult, lt)
                        q = qP[:, hl, qt * 128:(qt + 1) * 128]
                        kk = kF[:, hl // 2, :]

                        def bias(st=st, qt=qt):
                            return st["b"][:, (6 - 2 * qt) * 64:(6 - 2 * qt) * 64 + 512], st["t"]
                        u = dict(maps=[dict(q=q, keys=[(kk[:, 0:512], 512, bias), (kk[:, 512:768], 256, None)])],
                                 scale=0.125, out=outf, v=lambda j, hl=hl: V[:, j, hl * 64:(hl + 1) * 64],
                                 qk=[tq[n], tk[n][hl // 2]], vt=tv_[n])
                        if qt == 0:
                            u["pre"] = pre
                        if qt == 3:
                            u["post"] = lambda t, st=st: biasr.release(st["k"], t)
                        units.append(u)
                yield from attention(units, Sr, PTr)
                over[n] = [(PE.sem, PE.count)]

            tu, tG, tmx = {}, {}, []

            def gates(c0, half):
                blocks = wcols(A["w_in"], 1024, c0 + 512 * half, 512)

                def ev(i, o_, tok):
                    t = act(G[:, i, :], o_, ACT.Sigmoid, tok, tb, tG.get(("r", i)))
                    tG[i] = t
                    return t
                yield from gemm_steps(blocks, range(4), lambda i, kt, w: w[:, i * 128:(i + 1) * 128],
                                      lambda i, kt, w: HT[:, kt, 0:512], ev, tH)

            def branch_ssd():
                ty_ = dma(AC, yT, yD, tyD, over[2], (DVE.sem, DVE.count), (PL.sem, PL.count), (AC.sem, AC.count))
                for half in range(2):
                    yield from gates(CGS, half)
                    blocks = wcols(A["w_branch_ssd"], 2048, 512 * half, 512)

                    def ev(i, o_, tok, half=half):
                        j = half * 4 + i
                        tG["r", i] = tu[j] = tt(DVE, uT[:, j, :], o_, G[:, i, :], ALU.mult, tok, tG[i], tb)
                        return tu[j]
                    yield from gemm_steps(blocks, range(4), lambda i, kt, w: w[:, i * 128:(i + 1) * 128],
                                          lambda i, kt, w: yT[:, kt, :], ev, ty_)
                yield from gates(CGN, 0)

            def branch_na(toT):
                for half in range(2):
                    if half:
                        yield from gates(CGN, half)
                    blocks = wcols(A["w_branch_na"], 1024, 512 * half, 512)

                    def ev(i, o_, tok, half=half):
                        j = half * 4 + i
                        k, tm_, f = tmpE.take()
                        t = tt(DVE, tm_, o_, G[:, i, :], ALU.mult, tok, tG[i], f)
                        tG["r", i] = t
                        tu[j] = tt(PL, uT[:, j, :], uT[:, j, :], tm_, ALU.add, t, tu[j])
                        tmpE.release(k, tu[j])
                        return t
                    yield from gemm_steps(blocks, range(4), lambda i, kt, w: w[:, i * 128:(i + 1) * 128],
                                          lambda i, kt, w: oT[:, kt, :], ev, toT)

            main = using(PA, steps_chunks(3))
            while 2 not in done:
                next(main)
            weave(main, using(PG_, na_proj(0)), 0.8)
            tb = latest() + tyD
            for ring in (biasr, Sr, PTr, tmpE):
                for k in ring.keys:
                    ring.release(k, tb)
            more_slots(DSLOT)
            for n in range(3):
                weave(using(PA, na_attention(n)), using(PG_, na_proj(n + 1)), 0.7, 0.0 if n else 3.0)
            weave(using(PA, na_attention(3)), using(PG_, branch_ssd()), 0.7)
            dump("O", O)
            wfree = fewer_slots()
            more_slots(*[TOP + WSLOT * i for i in range(3)])
            toT, tO = [], (DVE.sem, DVE.count)
            for j in range(8):
                b, bank, free = PS.take()
                for i in range(4):
                    lt = tr(bank[:, i * 128:(i + 1) * 128], O[:, i, j * 128:(j + 1) * 128], free, tO, signal=(i == 3))
                t = copy(evac2(j), oT[:, j, :], bank, lt, over[3])
                PS.release(b, t)
                toT.append(t)
            run(branch_na(toT))
            tu_ = [tu[j] for j in range(8)]
            tyd_ = [(PE.sem, PE.count)]
            X = r3(sb(BASE, 4096), 1024)
            txr = dma(AC, X, xT, tyd_)
            gam1, junk = sb(SB, 1024), sb(SB + 1024, 1024)
            tg1 = dma(AC, gam1, gamD[0:1, :].rearrange("a n -> (a n)").partition_broadcast(128), tyd_, tgam)
            tms = []
            for half in range(2):
                blocks = wcols(A["w_out"], 1024, 512 * half, 512)

                def ev(i, o_, tok, half=half):
                    t = copy(evac2(i), mix[:, i, half * 512:half * 512 + 512], o_, tok, tyd_)
                    tmx.append(t)
                    if half:
                        tms.append(act(junk, mix[:, i, :], ACT.Square, tmx[i], t, tyd_, tms[-1:], acc=small[:, 132 + i:133 + i]))
                    return t
                gemm(blocks, range(4), lambda i, kt, w: uT[:, kt, i * 128:(i + 1) * 128], lambda i, kt, w: w, ev, tu_)
            dump("mix", mix)

        HT2 = r3(sb(BASE + 4096, 4096), 512)
        PF = BASE + 8192

        ssq = small[:, 128:132]
        tsq = []

        def square(i, junk, *waits):
            tsq.append(act(junk, X[:, i, :], ACT.Square, tsq[-1:], list(waits), acc=ssq[:, i:i + 1]))

        def residual(m, gam, tm_, junk, *waits):
            sm = small[:, 132:136]
            t = rstd(sm, 4, tm_)
            done = []
            for i in range(4):
                t1 = stt(m[:, i, :], m[:, i, :], sm[:, i:i + 1], gam, ALU.mult, ALU.mult, t, list(waits))
                done.append(tt(PL if i % 2 else DVE, X[:, i, :], X[:, i, :], m[:, i, :], ALU.add, t1, list(waits)))
                square(i, junk, done[-1])
            return done

        def normed_2(xn, scale_of, shift_of, *waits):
            t = rstd(ssq, 4, tsq)
            tx_ = [act(xn[:, i, :], X[:, i, :], ACT.Copy, t, list(waits), scale=ssq[:, i:i + 1]) if i % 2 else
                   ts(DVE, xn[:, i, :], X[:, i, :], ssq[:, i:i + 1], ALU.mult, t, list(waits)) for i in range(4)]
            return turned(4, HT2, xn, tx_, scale_of, shift_of)

        t2nd = []

        def second_tables():
            tcg = dma(AC, gcon, con_load("g", gcon), tb)
            posf = scratch[:, 0:512]
            angb = [scratch[:, 512 * (i + 1):512 * (i + 2)] for i in range(3)]
            posi = scratch[:, 2048:2560].bitcast(I32)
            t = dma(AC, posi, A["positions"].rearrange("a n -> (a n)").partition_broadcast(128), tb)
            t = copy(DVE, posf, posi, t)
            C1 = 6.28125
            rest = 2 * math.pi - C1
            C2 = float(np.float32(round(rest * 2 ** 21) / 2 ** 21))
            C3 = float(np.float32(rest - C2))
            ttab = []
            for n, (inv_, which) in enumerate((("invb", 0), ("invb", 1), ("invd", 0), ("invd", 1))):
                ang, kk_, r_ = angb
                t = ts(DVE, ang, posf, con(inv_), ALU.mult, t, tcg)
                t = ts(DVE, kk_, ang, 1.0 / (2 * math.pi), ALU.mult, t, s2=0.25 if which == 0 else 0.0, op1=ALU.add)
                t = ts(DVE, kk_, kk_, MAGIC, ALU.add, t)
                t = ts(DVE, kk_, kk_, MAGIC, ALU.subtract, t)
                t = stt(r_, kk_, -C1, ang, ALU.mult, ALU.add, t)
                t = stt(r_, kk_, -C2, r_, ALU.mult, ALU.add, t)
                t = stt(r_, kk_, -C3, r_, ALU.mult, ALU.add, t)
                if which == 0:
                    t = ts(DVE, r_, r_, math.pi / 2, ALU.add, t)
                t = ts(DVE, r_, r_, 3.1415925, ALU.min, t, s2=-3.1415925, op1=ALU.max)
                t = act(tabs[n], r_, ACT.Sin, t)
                ttab.append(t)
            lam4 = scratch[:, 2560:2816]
            ls = [sem("s_lam"), 0]
            for i, nme in enumerate(("lambda_q1", "lambda_k1", "lambda_q2", "lambda_k2")):
                tl_ = dma(AC, lam4[:, i * 64:(i + 1) * 64], A[nme].rearrange("a n -> (a n)").partition_broadcast(128), tb, s=ls)
            tgd = dma(AC, gd, A["g_diff"].rearrange("a n -> (a n)").partition_broadcast(128), tb)
            prod = lam4
            t = tt(DVE, prod[:, 0:64], lam4[:, 0:64], lam4[:, 64:128], ALU.mult, tl_)
            t = tt(DVE, prod[:, 64:128], lam4[:, 128:192], lam4[:, 192:256], ALU.mult, t)
            t = reduce_(lamv[:, 0:4], r3(prod[:, 0:128], 32), ALU.add, t)
            t = act(lamv[:, 4:8], lamv[:, 0:4], ACT.Exp, t)
            inits = [0.8 - 0.6 * math.exp(-0.3 * l) for l in range(2)]
            t = tt(DVE, lamv[:, 8:10], lamv[:, 6:8], lamv[:, 4:6], ALU.subtract, t)
            tlam = [ts(DVE, lamv[:, 8 + l:9 + l], lamv[:, 8 + l:9 + l], -inits[l], ALU.add, t) for l in range(2)]
            tgs = [ts(DVE, gd[:, 64 * l:64 * l + 64], gd[:, 64 * l:64 * l + 64], 1.0 - inits[l], ALU.mult, tgd) for l in range(2)]
            t2nd.extend(ttab + tlam + tgs + [tcg])

        if stop not in ("B", "C", "D", "E0"):
            tX = residual(mix, gam1, tms, junk, txr, tg1)
            dump("X1", X)
            tb = latest() + tX + wfree
            o = PF
            tabs = [sb(o + 512 * i, 512) for i in range(4)]; o += 2048
            lamv = sb(o, 16); o += 16
            gd = sb(o, 128); o += 128
            ng = at["g"][1] - at["g"][0]
            gcon = sb(o, ng); o += ng
            PG = o
            h2 = r3(sb(o, 4096), 1024); o += 4096
            moe = r3(sb(o, 4096), 1024); o += 4096
            xgr = Ring([r3(sb(o + 1024 * i, 1024), 128) for i in range(2)]); o += 2048
            yor = Ring([sb(o + 1024 * i, 1024) for i in range(2)]); o += 2048
            Pr = Ring([r3(sb(o + 512 * i, 512), 128) for i in range(2)]); o += 1024
            PTr = Ring([sb(o + 512 * i, 512) for i in range(2)]); o += 1024
            Pg = r3(sb(o, 512), 128); o += 512
            hidr = Ring([sb(o + 512 * i, 512) for i in range(2)]); o += 1024
            hidTr = Ring([r3(sb(o + 2048 * i, 2048), 128) for i in range(2)]); o += 4096
            wr_ = sb(o, 128); o += 128
            aff = sb(o, 64); o += 64
            slot = sb(o, 64); o += 64
            iota = sb(o, 64); o += 64
            m8 = sb(o, 8); o += 8
            assert o <= TOP, o
            ytmp = moe.rearrange("p a b -> p (a b)")
            wrk, slotT = ytmp[:, 0:512], ytmp[:, 512:1024]
            tio = dma(AC, iota, con_load("f", iota), tb)
            twr = dma(AC, r3(wr_, 16), A["w_router"].rearrange("(k p) e -> p k e", p=128), tb)
            th2 = normed_2(h2, lambda j: mc[:, 3, j, 0:1], lambda j: mc[:, 2, j, 0:1], tb)
            tall = latest()
            b, bank, free = PS.take()
            for i in range(4):
                for kt in range(8):
                    lt = mm(bank[:, i * 16:(i + 1) * 16], HT2[:, kt, i * 128:(i + 1) * 128], r3(wr_, 16)[:, kt, :], kt == 0, kt == 7,
                            free, twr, th2, signal=(i == 3 and kt == 7))
            sv = small[:, 144:160]
            t = reduce_(sv[:, 0:4], r3(bank[:, 0:64], 16), ALU.max, lt)
            t = tt(DVE, r3(aff, 16), r3(bank[:, 0:64], 16), bc(sv[:, 0:4], 16), ALU.subtract, t, tb)
            PS.release(b, t)
            t = act(aff, aff, ACT.Exp, t)
            t = reduce_(sv[:, 4:8], r3(aff, 16), ALU.add, t)
            t = recip(sv[:, 4:8], sv[:, 4:8], t)
            taff = tt(DVE, r3(aff, 16), r3(aff, 16), bc(sv[:, 4:8], 16), ALU.mult, t)
            b, bank, free = PS.take()
            for i in range(4):
                lt = tr(bank[0:16, i * 128:(i + 1) * 128], aff[:, i * 16:(i + 1) * 16], free, taff, signal=(i == 3))
            t = copy(DVE, wrk[0:16, :], bank[0:16, :], lt, tb)
            PS.release(b, t)
            th3 = []
            for i in range(4):
                for hf_ in range(2):
                    b, bank, free = PS.take()
                    for j in range(4):
                        lt = tr(bank[:, j * 128:(j + 1) * 128], HT2[:, hf_ * 4 + j, i * 128:(i + 1) * 128], free, th2, signal=(j == 3))
                    te = copy(AC, h2[:, i, hf_ * 512:hf_ * 512 + 512], bank, lt, tall)
                    PS.release(b, te)
                    th3.append(te)
            for n in range(8):
                t = DVE.op(lambda e: e.max(m8[0:16, :], wrk[0:16, :]), t)
                t = DVE.op(lambda e: e.match_replace(wrk[0:16, :], m8[0:16, :], wrk[0:16, :], -1.0), t)
            t = ts(DVE, wrk[0:16, :], wrk[0:16, :], 0.0, ALU.is_lt, t)
            t = DVE.op(lambda e: e.tensor_tensor_scan(slotT[0:16, :], wrk[0:16, :], wrk[0:16, :], 0.0, ALU.add, ALU.max), t)
            t = tt(DVE, slotT[0:16, :], slotT[0:16, :], wrk[0:16, :], ALU.mult, t)
            t = ts(DVE, slotT[0:16, :], slotT[0:16, :], -1.0, ALU.add, t)
            b, bank, free = PS.take()
            for i in range(4):
                lt = tr(bank[:, i * 16:(i + 1) * 16], slotT[0:16, i * 128:(i + 1) * 128], free, t, signal=(i == 3))
            tsl = copy(DVE, slot, bank[:, 0:64], lt)
            PS.release(b, tsl)
            dump("slot", slot)
            dump("aff", aff)
            tPg = [None]

            def gather(m):
                pk, P, pf = Pr.take()
                tP = []
                for i in range(4):
                    tP.append(tt(DVE, r3(P[:, i, :], 64), bc(slot[:, i * 16 + 2 * m:i * 16 + 2 * m + 2], 64), rep(iota, 2),
                                 ALU.is_equal, tsl, tio, pf, tb))
                t = [tt(PL, r3(Pg[:, i, :], 64), r3(P[:, i, :], 64), bc(aff[:, i * 16 + 2 * m:i * 16 + 2 * m + 2], 64), ALU.mult,
                        tP[i], tPg[0]) for i in range(4)]
                xk, xg, xf = xgr.take()
                txg = []
                for q_ in range(2):
                    b, bank, free = PS.take()
                    for kt in range(4):
                        for i in range(4):
                            c0 = (4 * q_ + kt) * 128
                            lt = mm(bank[:, kt * 128:(kt + 1) * 128], h2[:, i, c0:c0 + 128], P[:, i, :], i == 0, i == 3, free,
                                    tP, th3, signal=(kt == 3 and i == 3))
                    e = copy(evac2(q_), xg[:, 4 * q_:4 * q_ + 4, :], r3(bank, 128), lt, xf, tb)
                    PS.release(b, e)
                    txg.append(e)
                Pr.release(pk, lt, t)
                b, bank, free = PS.take()
                for i in range(4):
                    lt = tr(bank[:, i * 128:(i + 1) * 128], Pg[:, i, :], free, t, signal=(i == 3))
                tPg[0] = lt
                k, PT, f = PTr.take()
                e = copy(AC, PT, bank, lt, f)
                PS.release(b, e)
                return dict(xk=xk, xg=xg, txg=txg, PT=(k, PT, e))

            def scatter(u):
                k, PT, tpt = u["PT"]
                yk, yo, tyo = u["yo"]
                for i in range(4):
                    for n in range(2):
                        b, bank, free = PS.take()
                        lt = mm(bank, PT[:, i * 128:(i + 1) * 128], yo[:, n * 512:n * 512 + 512], True, True, free, tpt, tyo,
                                signal=True)
                        d = moe[:, i, n * 512:n * 512 + 512]
                        if u["m"]:
                            t = tt(DVE, d, bank, d, ALU.add, lt, tms.get((i, n)))
                        else:
                            t = copy(DVE, d, bank, lt, tsl)
                        tms[i, n] = t
                        PS.release(b, t)
                    if u["m"] == 7:
                        tsm.append(act(h2[:, 1, :], moe[:, i, :], ACT.Square, tms[i, 0], tms[i, 1], lastPE, tsm[-1:],
                                       acc=small[:, 132 + i:133 + i]))
                PTr.release(k, lt)
                yor.release(yk, lt)

            tms, tsm, lastPE = {}, [], []
            u, last_u = gather(0), None
            tb = tb + [(PE.sem, PE.count)]
            scratch = HT2.rearrange("p a b -> p (a b)")
            second_tables()
            for m in range(8):
                xg, txg = u["xg"], u["txg"]
                eg = [A["w_exp_gate"][2 * m + j] for j in range(2)]
                eu = [A["w_exp_up"][2 * m + j] for j in range(2)]
                ed = [A["w_exp_down"][2 * m + j] for j in range(2)]
                thT = []
                hk, hidT, hf_ = hidTr.take()
                for s in range(4):
                    res = []
                    for w2 in (eg, eu):
                        b, bank, free = PS.take()
                        for kg in range(2):
                            bl = [wblock(w2[j], kg * 512, 4, s * 512, 512) for j in range(2)]
                            for kk in range(4):
                                kt = kg * 4 + kk
                                for j in range(2):
                                    lt = mm(bank[64 * j:64 * j + 64, :], xg[:, kt, 64 * j:64 * j + 64],
                                            bl[j][1][:, kk, :], kt == 0, kt == 7, free, bl[j][2], txg,
                                            signal=(kk == 3))
                                    if kk == 3:
                                        W.release(bl[j][0], lt)
                        res.append((b, bank, lt))
                    k, hid, f = hidr.take()
                    t = act(hid, res[0][1], ACT.Silu, res[0][2], f, tb)
                    PS.release(res[0][0], t)
                    t = tt(DVE, hid, hid, res[1][1], ALU.mult, t, res[1][2])
                    PS.release(res[1][0], t)
                    b, bank, free = PS.take()
                    for j in range(4):
                        lt = tr(bank[:, j * 128:(j + 1) * 128], hid[:, j * 128:(j + 1) * 128], free, t, signal=(j == 3))
                    hidr.release(k, lt)
                    e = copy(DVE, hidT[:, s * 4:s * 4 + 4, :], r3(bank, 128), lt, hf_, tb)
                    PS.release(b, e)
                    thT.append(e)
                    if s == 0 and last_u:
                        scatter(last_u)
                xgr.release(u["xk"], lt)
                yk, yo, yf = yor.take()
                tyo = []
                nxt = None
                for n in range(2):
                    b, bank, free = PS.take()
                    for kg in range(4):
                        bl = [wblock(ed[j], kg * 512, 4, n * 512, 512) for j in range(2)]
                        for kk in range(4):
                            kt = kg * 4 + kk
                            for j in range(2):
                                lt = mm(bank[64 * j:64 * j + 64, :], hidT[:, kt, 64 * j:64 * j + 64], bl[j][1][:, kk, :],
                                        kt == 0, kt == 15, free, bl[j][2], thT, signal=(kk == 3))
                                if kk == 3:
                                    W.release(bl[j][0], lt)
                    e = copy(AC, yo[:, n * 512:n * 512 + 512], bank, lt, yf, tb)
                    PS.release(b, e)
                    tyo.append(e)
                    if n == 0 and m < 7:
                        nxt = gather(m + 1)
                hidTr.release(hk, lt)
                u.update(yo=(yk, yo, tyo), m=m)
                last_u, u = u, nxt
            gam2 = h2.rearrange("p a b -> p (a b)")[:, 0:1024]
            tg2 = dma(AC, gam2, gamD[1:2, :].rearrange("a n -> (a n)").partition_broadcast(128), (PE.sem, PE.count))
            lastPE.append((PE.sem, PE.count))
            scatter(last_u)
            tX = residual(moe, gam2, tsm, h2[:, 1, :], tg2)
            dump("X2", X)

        if stop not in ("B", "C", "D", "E0", "E", "F"):
            cosb, sinb, cosd, sind = tabs
            ROT = {"d": (cosd, sind, con("rd")), "b": (cosb, sinb, con("rb"))}
            junk = sb(TOP - 1024, 1024)
            def add_X(i, o_, tok, half, last):
                d = X[:, i, half * 512:half * 512 + 512]
                t = tt(DVE, d, o_, d, ALU.add, tok)
                tX.append(t)
                if half and last:
                    square(i, junk, t)
                return t

            tb = latest() + t2nd + tX
            for layer in range(2):
                tb = latest() + t2nd + tX
                o = PG
                sets = []
                for nq in (8, 4):
                    sets.append((r3(sb(o, 512 * nq), 512), r3(sb(o + 512 * nq, 1024), 512), r3(sb(o + 512 * nq + 1024, 1024), 256)))
                    o += 512 * nq + 2048
                O = r3(sb(o, 4096), 1024); o += 4096
                Sr = Ring([sb(o + 512 * i, 512) for i in range(6)]); o += 3072
                PTr = Ring([sb(o + 512 * i, 512) for i in range(3)]); o += 1536
                tmp = Ring([tuple(sb(o + 1536 * i + 512 * j, 512) for j in range(3)) for i in range(2)]); o += 3072
                assert o <= TOP - 1024, o
                tz2 = [zero(PL, sets[k_][0].rearrange("p a b -> p (a b)"), tb) for k_ in range(2)]
                tH = normed_2(O, lambda j: gmix2[:, layer * 8 + j:layer * 8 + j + 1], lambda j: None, tb)
                tOn = (PE.sem, PE.count)
                HT = HT2
                Wi = A["w_in_2"][layer]
                groups = [(0, 256, 512, "d", 0, 0), (768, 1024, 1280, "b", 4, 1),
                          (1536, 2048, 2560, "b", 8, 0), (1792, 2304, 2816, "b", 12, 1)]
                tk_ = {}

                def proj_2(n):
                    cq, ck, cv, kind, h0, si = groups[n]
                    q_, k_, v_ = sets[si]
                    tq, tk, tv_ = tk_[n] = ([], [], [])
                    late = []
                    before = tz2 + over.get(n - 2, [])
                    per = 32 if kind == "d" else 64
                    for c0, toks, dest in ((cq, tq, lambda i: [(per * c, per * c + per, q_[:, (128 // per) * i + c, :])
                                                               for c in range(128 // per)]),
                                           (ck, tk, lambda i: [(0, 128, k_[:, i, :])])):
                        blocks = wcols(Wi, 1024, c0, 256)
                        for i in range(2):
                            tds, last = rope(blocks, i, late, *ROT[kind], dest(i), tmp, [tH, before], [])
                            toks.append(tds)
                            if i == 1:
                                for x_ in blocks:
                                    W.release(x_[0], last)
                            yield
                    blocks = wcols(Wi, 1024, cv, 256)

                    def ev(i, o_, tok):
                        t = copy(evac2(i), v_[:, i, :], o_, tok, before)
                        tv_.append(t)
                        return t
                    yield from then_late(late, gemm_steps(blocks, range(4), lambda i, kt, w: HT2[:, kt, i * 128:(i + 1) * 128],
                                                          lambda i, kt, w: w, ev, tH))

                def outn(O_, qt, col):
                    return lambda ps, lt, sv: ts(DVE, O_[:, qt, col:col + 64], ps, sv[:, 1:2], ALU.mult, lt, tOn)

                def outd(O_, qt, col):
                    return lambda ps, lt, sv: copy(DVE, O_[:, qt, col:col + 64], ps, lt, tOn)

                def norm_heads():
                    t0 = (DVE.sem, DVE.count)
                    sh = small[:, 32:48]
                    hsq = r3(junk, 256)
                    t = tt(DVE, hsq, O[:, :, 0:256], O[:, :, 0:256], ALU.mult, t0, tsq)
                    t = reduce_(sh, r3(junk, 64), ALU.add, t)
                    t = rstd(sh, 16, t, mean=64.0)
                    for qt in range(4):
                        d = r3(O[:, qt, 0:256], 64)
                        t1 = tt(DVE, d, d, bc(sh[:, 4 * qt:4 * qt + 4], 64), ALU.mult, t)
                        thn.append(tt(PL, d, d, rep(gd[:, 64 * layer:64 * layer + 64], 4), ALU.mult, t1))

                def attention_2(n):
                    cq, ck, cv, kind, h0, si = groups[n]
                    q_, k_, v_ = sets[si]
                    tq, tk, tv_ = tk_[n]
                    mask = con("dilated" if n > 1 else "causal")
                    units = []
                    for hl in range(4):
                        for qt in range(4):
                            nk_ = 128 * (qt + 1)
                            bias = lambda qt=qt: (mask[:, 384 - 128 * qt:512], None)
                            qs = slice(qt * 128, qt * 128 + 128)
                            comps = 2 if kind == "d" else 1
                            u = dict(maps=[dict(q=q_[:, comps * hl + c, qs], keys=[(k_[:, hl // 2, 0:nk_], nk_, bias)]) for c in range(comps)],
                                     scale=(64 // comps) ** -0.5, out=(outd if kind == "d" else outn)(O, qt, 64 * (h0 + hl)),
                                     v=lambda j, hl=hl: v_[:, j, 64 * hl:64 * hl + 64], qk=[tq[hl // 2], tk[hl // 2]], vt=tv_)
                            if kind == "d":
                                u["nlam"] = lamv[:, 8 + layer:9 + layer]
                            units.append(u)
                    yield from attention(units, Sr, PTr)
                    over[n] = [(PE.sem, PE.count)]
                    tOd[n] = [(DVE.sem, DVE.count)]

                oT = HT2
                toT = []
                tX = []

                def turn_O(cols, tO, *waits):
                    for j in cols:
                        b, bank, free = PS.take()
                        for i in range(4):
                            lt = tr(bank[:, i * 128:(i + 1) * 128], O[:, i, j * 128:(j + 1) * 128], free, tO, signal=(i == 3))
                        t = copy(evac2(j), oT[:, j, :], bank, lt, list(waits))
                        PS.release(b, t)
                        toT.append(t)

                def out_2(kt0, nk_, last):
                    for half in range(2):
                        src = A["w_out_2"][layer][128 * kt0:128 * (kt0 + nk_), :]
                        blocks = wcols(src, 128 * nk_, 512 * half, 512)
                        yield from gemm_steps(blocks, range(4), lambda i, kt, w: oT[:, kt0 + kt, i * 128:(i + 1) * 128], lambda i, kt, w: w,
                                              lambda i, o_, tok, half=half: add_X(i, o_, tok, half, last), toT)

                def early_out():
                    turn_O(range(6), tOd[2] + thn, (PE.sem, PE.count))
                    yield
                    yield from out_2(0, 6, False)

                over, tOd, thn = {}, {}, []
                run(proj_2(0))
                for n in range(3):
                    if n == 1:
                        tz2 = [zero(PL, sets[0][0][:, 0:4, :].rearrange("p a b -> p (a b)"), over[0])]
                        norm_heads()
                    weave(using(PA, attention_2(n)), using(PG_, proj_2(n + 1)), 0.5)
                weave(using(PA, attention_2(3)), using(PG_, early_out()), 0.55)
                if layer == 0:
                    dump("O2", O)
                turn_O((6, 7), tOd[3])
                run(out_2(6, 2, True))
                if layer == 0:
                    dump("X3", X)
                tb = latest() + tX
                o = PG
                actT = r3(sb(o, 11264), 512); o += 11264
                pads = Ring([sb(o + 516 * i, 514) for i in range(4)]); o += 2064
                accs = Ring([sb(o + 512 * i, 512) for i in range(4)]); o += 2048
                xnb = r3(sb(o, 4096), 1024); o += 4096
                assert o <= TOP - 1024, o
                tH = normed_2(xnb, lambda j: gffn2[:, layer * 8 + j:layer * 8 + j + 1], lambda j: None, tb)
                tz = [zero(DVE, p_[:, 0:2], tb) for p_ in pads.bufs]
                Wu = A["w_up_2"][layer]
                tact = []
                for s in range(11):
                    bl = []
                    for kg in range(2):
                        def parts(buf, kg=kg, s=s):
                            d = r3(buf, 512)
                            rr = Wu[kg * 512:kg * 512 + 512, :]
                            return [(d[:, :, 256 * v:256 * v + 256],
                                     rr[:, 2816 * v + 256 * s:2816 * v + 256 * s + 256].rearrange("(k p) n -> p k n", p=128)) for v in range(2)]
                        k, buf, tok = wload(parts)
                        bl.append((k, r3(buf, 512), tok, 4))
                    held = {}

                    def ev(i, o_, tok, s=s, held=held):
                        v, j = i // 2, i % 2
                        ti = 22 * v + 2 * s + j
                        pk, pad, pf = pads.take()
                        c1 = copy(AC, pad[:, 2:514], o_, tok, pf, tz)
                        ak, ac_, af = accs.take()
                        w3 = lambda q_: vcw2[:, layer * 132 + q_ * 44 + ti:layer * 132 + q_ * 44 + ti + 1]
                        t = ts(PL, ac_, pad[:, 0:512], w3(0), ALU.mult, c1, af)
                        t = stt(ac_, pad[:, 1:513], w3(1), ac_, ALU.mult, ALU.add, t)
                        t = stt(ac_, pad[:, 2:514], w3(2), ac_, ALU.mult, ALU.add, t)
                        pads.release(pk, t)
                        bb = vcb[:, 24 + layer * 44 + ti:24 + layer * 44 + ti + 1]
                        if v == 0:
                            t = act(ac_, ac_, ACT.Silu, t, bias=bb)
                            held[j] = (ak, ac_, t)
                        else:
                            gk, ga, gt = held[j]
                            t = stt(actT[:, 2 * s + j, :], ac_, bb, ga, ALU.add, ALU.mult, t, gt, tb)
                            accs.release(ak, t)
                            accs.release(gk, t)
                            tact.append(t)
                        return c1
                    gemm(bl, (0, 1, 2, 3), lambda i, kt, w: w[:, i * 128:(i + 1) * 128], lambda i, kt, w: HT2[:, kt, :], ev, tH)
                tX = []
                for half in range(2):
                    blocks = wcols_later(A["w_down_2"][layer], 2816, 512 * half, 512)

                    def ev(i, o_, tok, half=half):
                        return add_X(i, o_, tok, half, True)
                    chunked(blocks, range(4), lambda i, kt, w: actT[:, kt, i * 128:(i + 1) * 128], lambda i, kt, w: w, ev, 1, tact)
                if layer == 0:
                    dump("X4", X)
            tb = latest()
            gf = sb(PG, 1024)
            ob = r3(sb(PG + 1024, 4096), 1024)
            tgf = dma(AC, gf, A["g_final"].partition_broadcast(128), tb)
            t = rstd(ssq, 4, tsq)
            osem = [sem("s_out"), 0]
            for i in range(4):
                t1 = stt(ob[:, i, :], X[:, i, :], ssq[:, i:i + 1], gf, ALU.mult, ALU.mult, t, tgf, tb)
                tend = dma(SP, out[0, i * 128:(i + 1) * 128, :], ob[:, i, :], t1, s=osem)
            SP.need([tend])
        else:
            SP.need([latest(), tyD])

        SP.need(tdump)
        block = ctx.enter_context(nc.Block())
        block.sync(SP.run)
        block.tensor(PE.run)
        block.vector(DVE.run)
        block.scalar(AC.run)
        block.gpsimd(PL.run)


_INS = ['x', 'c', 'ctx', 'c_ctx', 'w_ada', 'b_ada', 'norm_pre_mix', 'norm_post_mix', 'norm_pre_ffn', 'norm_post_ffn',
        'w_in', 'na_rpb', 'ssd_conv_w', 'ssd_conv_b', 'ssd_a_log_fwd', 'ssd_a_log_bwd', 'ssd_dt_bias_fwd',
        'ssd_dt_bias_bwd', 'ssd_d_skip', 'ssd_norm', 'w_branch_na', 'w_branch_ssd', 'w_out', 'w_router',
        'w_exp_gate', 'w_exp_up', 'w_exp_down', 'positions_2', 'g_mix_2', 'w_in_2', 'w_out_2', 'lambda_q1_2',
        'lambda_k1_2', 'lambda_q2_2', 'lambda_k2_2', 'g_diff_2', 'g_ffn_2', 'w_up_2', 'conv_w_2', 'conv_b_2',
        'w_down_2', 'g_final_2']
_DROP = ['w_ada', 'w_in', 'w_branch_na', 'w_branch_ssd', 'w_out', 'w_router', 'w_exp_gate', 'w_exp_up', 'w_exp_down']
_NAMES = {'positions_2': 'positions', 'lambda_q1_2': 'lambda_q1', 'lambda_k1_2': 'lambda_k1',
          'lambda_q2_2': 'lambda_q2', 'lambda_k2_2': 'lambda_k2', 'g_diff_2': 'g_diff', 'g_final_2': 'g_final'}


def kernel(**inputs):
    import concourse.bacc as _bacc
    from concourse.bass_utils import run_bass_kernel_spmd as _run

    nc = _bacc.Bacc("TRN2", target_bir_lowering=False, num_devices=1)
    arrays, A = {}, {}
    consts, at = shape_constants()
    for name in _INS + ["consts"]:
        a = np.ascontiguousarray(consts if name == "consts" else inputs[name])
        if name in _DROP:
            a = a[0]
        arrays[f"in_{name}_dram"] = a
        A[_NAMES.get(name, name)] = nc.dram_tensor(f"in_{name}_dram", a.shape, mybir.dt.from_np(a.dtype), kind="ExternalInput").ap()
    A["at"] = at
    out = nc.dram_tensor("out_0_dram", (1, 512, 1024), F32, kind="ExternalOutput").ap()
    build(nc, A, out)
    r = _run(nc, [arrays], core_ids=[0])
    return r.results[0]["out_0_dram"]
```
